# Optimizing a Trainium2 kernel written in Bass

```python
import math
import jax, jax.numpy as jnp
from jax import lax
import numpy as np

D_MODEL = 1024
BATCH = 1
SEQ = 512
DEPTH = 1

CHUNK = 64
N_META = 16
SB_HEADS = 4
SB_HEAD_DIM = 64
SB_WIDTH = SB_HEADS * SB_HEAD_DIM
SSM_WIDTH = D_MODEL // 2
SSM_GROUP = 16
SSM_GROUPS = SSM_WIDTH // SSM_GROUP
SSM_STATE = 64
FFN_DIM = ((8 * D_MODEL // 3 + 127) // 128) * 128
CONV_WIDTH = 3
Q_BLOCK = 128
N_BRANCH = 2
IN_WIDTH = 3 * SB_WIDTH + SSM_WIDTH + N_BRANCH * D_MODEL
RMS_EPS = 1e-6
DT_MIN = 1e-3
DT_MAX = 1e-1
A_RE_MAX = -1e-4

kernel_name = "hybrid_stickbreak_s5_convffn"

def rmsnorm(x, g):
    xf = x.astype(jnp.float32)
    y = xf * lax.rsqrt(jnp.mean(xf * xf, axis=-1, keepdims=True) + RMS_EPS)
    return (y * g.astype(jnp.float32)).astype(x.dtype)

def stick_breaking_attention(q, k, v):
    b, l, h, dh = q.shape
    nb = l // Q_BLOCK
    q = q.transpose(0, 2, 1, 3)
    k = k.transpose(0, 2, 1, 3)
    v = v.transpose(0, 2, 1, 3)
    scale = dh ** -0.5
    ar = jnp.arange(Q_BLOCK)
    tri = (ar[:, None] >= ar[None, :]).astype(jnp.float32)

    def pair(p):
        def step(carry, s):
            acc, out, out_lo = carry
            second = s > p
            i = jnp.where(second, nb - 1 - p, p)
            j = jnp.where(second, nb - 1 - p - (s - p - 1), p - s)
            fresh = (s == 0) | (s == p + 1)
            acc = jnp.where(fresh, 0.0, acc)
            out = jnp.where(fresh, 0.0, out)
            qb = lax.dynamic_slice_in_dim(q, i * Q_BLOCK, Q_BLOCK, axis=2)
            kb = lax.dynamic_slice_in_dim(k, j * Q_BLOCK, Q_BLOCK, axis=2)
            vb = lax.dynamic_slice_in_dim(v, j * Q_BLOCK, Q_BLOCK, axis=2)
            z = jnp.einsum('bhqd,bhkd->bhqk', qb, kb) * scale
            mask = (j * Q_BLOCK + ar)[None, :] < (i * Q_BLOCK + ar)[:, None]
            log_keep = jnp.where(mask, jax.nn.log_sigmoid(-z), 0.0)
            rev = jnp.einsum('bhqk,kj->bhqj', log_keep, tri)
            attn = jnp.exp(jnp.where(mask, z + rev + acc[..., None], -jnp.inf))
            out = out + jnp.einsum('bhqk,bhkd->bhqd', attn, vb)
            acc = acc + jnp.sum(log_keep, axis=-1)
            out_lo = jnp.where(s == p, out, out_lo)
            return (acc, out, out_lo), None

        init = (jnp.zeros((b, h, Q_BLOCK), jnp.float32),
                jnp.zeros((b, h, Q_BLOCK, dh), jnp.float32),
                jnp.zeros((b, h, Q_BLOCK, dh), jnp.float32))
        (_, out_hi, out_lo), _ = lax.scan(step, init, jnp.arange(nb + 1))
        return out_lo, out_hi

    lo, hi = lax.map(pair, jnp.arange(nb // 2))
    blocks = jnp.concatenate([lo, hi[::-1]], axis=0)
    return blocks.transpose(1, 0, 3, 2, 4).reshape(b, l, h * dh)

def s5_ssm(u, a_re, a_im, log_step, b_re, b_im, c_re, c_im, d_skip):
    lam_re = jnp.minimum(a_re, A_RE_MAX)
    lam_im = a_im
    step = jnp.exp(log_step)[:, None]
    mag = jnp.exp(lam_re * step)
    abar_re = mag * jnp.cos(lam_im * step)
    abar_im = mag * jnp.sin(lam_im * step)
    den = lam_re * lam_re + lam_im * lam_im
    nr = abar_re - 1.0
    f_re = (nr * lam_re + abar_im * lam_im) / den
    f_im = (abar_im * lam_re - nr * lam_im) / den
    bbar_re = f_re[:, :, None] * b_re - f_im[:, :, None] * b_im
    bbar_im = f_re[:, :, None] * b_im + f_im[:, :, None] * b_re
    bu_re = jnp.einsum('blgh,gph->blgp', u, bbar_re)
    bu_im = jnp.einsum('blgh,gph->blgp', u, bbar_im)

    def combine(e1, e2):
        a1r, a1i, x1r, x1i = e1
        a2r, a2i, x2r, x2i = e2
        return (a2r * a1r - a2i * a1i,
                a2r * a1i + a2i * a1r,
                a2r * x1r - a2i * x1i + x2r,
                a2r * x1i + a2i * x1r + x2i)

    ar = jnp.broadcast_to(abar_re, bu_re.shape)
    ai = jnp.broadcast_to(abar_im, bu_re.shape)
    _, _, xr, xi = lax.associative_scan(combine, (ar, ai, bu_re, bu_im), axis=1)
    y = (jnp.einsum('blgp,ghp->blgh', xr, c_re)
         - jnp.einsum('blgp,ghp->blgh', xi, c_im)
         + d_skip * u)
    return y

def causal_dwconv(x, w, bias):
    l = x.shape[1]
    xp = jnp.pad(x, ((0, 0), (CONV_WIDTH - 1, 0), (0, 0)))
    return sum(xp[:, j:j + l] * w[j] for j in range(CONV_WIDTH)) + bias

def hybrid_layer(h, norm1_g, w_in, q_norm_g, k_norm_g, ssm_a_re, ssm_a_im, ssm_log_step,
                 ssm_b_re, ssm_b_im, ssm_c_re, ssm_c_im, ssm_d, w_glu, b_glu,
                 w_attn_proj, w_ssm_proj, w_o, norm2_g, w_up, conv_w, conv_b, w_down):
    b, l, _ = h.shape
    f32 = jnp.float32
    xn = rmsnorm(h, norm1_g)
    proj = xn @ w_in
    q, k, v, u, gates = jnp.split(
        proj, [SB_WIDTH, 2 * SB_WIDTH, 3 * SB_WIDTH, 3 * SB_WIDTH + SSM_WIDTH], axis=-1)
    q = rmsnorm(q.reshape(b, l, SB_HEADS, SB_HEAD_DIM), q_norm_g).astype(f32)
    k = rmsnorm(k.reshape(b, l, SB_HEADS, SB_HEAD_DIM), k_norm_g).astype(f32)
    v = v.reshape(b, l, SB_HEADS, SB_HEAD_DIM).astype(f32)
    attn = stick_breaking_attention(q, k, v).astype(h.dtype)

    uf = u.astype(f32).reshape(b, l, SSM_GROUPS, SSM_GROUP)
    y = s5_ssm(uf, ssm_a_re.astype(f32), ssm_a_im.astype(f32), ssm_log_step.astype(f32),
               ssm_b_re.astype(f32), ssm_b_im.astype(f32), ssm_c_re.astype(f32),
               ssm_c_im.astype(f32), ssm_d.astype(f32)).reshape(b, l, SSM_WIDTH)
    g = jax.nn.gelu(y)
    ssm = (g * jax.nn.sigmoid(g @ w_glu.astype(f32) + b_glu.astype(f32))).astype(h.dtype)

    gate_a, gate_s = jnp.split(gates, N_BRANCH, axis=-1)
    mixed = (jax.nn.sigmoid(gate_a) * (attn @ w_attn_proj)
             + jax.nn.sigmoid(gate_s) * (ssm @ w_ssm_proj))
    h = h + mixed @ w_o
    xn = rmsnorm(h, norm2_g)
    up = causal_dwconv(xn @ w_up, conv_w, conv_b)
    gate_f, val_f = jnp.split(up, 2, axis=-1)
    h = h + (jax.nn.silu(gate_f) * val_f) @ w_down
    return h

def setup_inputs(seed: int = 0) -> dict:
    key = jax.random.key(seed)
    ks = jax.random.split(key, 24)
    f32 = jnp.float32
    nrm = lambda k, shape, s: (jax.random.normal(k, shape, f32) * s).astype(f32)
    n_idx = jnp.arange(SSM_STATE, dtype=f32)
    log_step = jax.random.uniform(ks[8], (DEPTH, SSM_GROUPS), f32,
                                  math.log(DT_MIN), math.log(DT_MAX))
    return {
        "x": nrm(ks[0], (BATCH, SEQ, D_MODEL), 1.0),
        "meta_tokens": nrm(ks[1], (N_META, D_MODEL), 1.0),
        "norm1_g": 1.0 + nrm(ks[2], (DEPTH, D_MODEL), 0.01),
        "w_in": nrm(ks[3], (DEPTH, D_MODEL, IN_WIDTH), D_MODEL ** -0.5),
        "q_norm_g": 1.0 + nrm(ks[4], (DEPTH, SB_HEAD_DIM), 0.01),
        "k_norm_g": 1.0 + nrm(ks[5], (DEPTH, SB_HEAD_DIM), 0.01),
        "ssm_a_re": -0.5 * (1.0 + nrm(ks[6], (DEPTH, SSM_GROUPS, SSM_STATE), 0.01)),
        "ssm_a_im": math.pi * n_idx + nrm(ks[7], (DEPTH, SSM_GROUPS, SSM_STATE), 0.01),
        "ssm_log_step": log_step,
        "ssm_b_re": nrm(ks[9], (DEPTH, SSM_GROUPS, SSM_STATE, SSM_GROUP), (2 * SSM_GROUP) ** -0.5),
        "ssm_b_im": nrm(ks[10], (DEPTH, SSM_GROUPS, SSM_STATE, SSM_GROUP), (2 * SSM_GROUP) ** -0.5),
        "ssm_c_re": nrm(ks[11], (DEPTH, SSM_GROUPS, SSM_GROUP, SSM_STATE), (2 * SSM_STATE) ** -0.5),
        "ssm_c_im": nrm(ks[12], (DEPTH, SSM_GROUPS, SSM_GROUP, SSM_STATE), (2 * SSM_STATE) ** -0.5),
        "ssm_d": nrm(ks[13], (DEPTH, SSM_GROUPS, SSM_GROUP), 1.0),
        "w_glu": nrm(ks[14], (DEPTH, SSM_WIDTH, SSM_WIDTH), SSM_WIDTH ** -0.5),
        "b_glu": nrm(ks[15], (DEPTH, SSM_WIDTH), 0.01),
        "w_attn_proj": nrm(ks[16], (DEPTH, SB_WIDTH, D_MODEL), SB_WIDTH ** -0.5),
        "w_ssm_proj": nrm(ks[17], (DEPTH, SSM_WIDTH, D_MODEL), SSM_WIDTH ** -0.5),
        "w_o": nrm(ks[18], (DEPTH, D_MODEL, D_MODEL), D_MODEL ** -0.5),
        "norm2_g": 1.0 + nrm(ks[19], (DEPTH, D_MODEL), 0.01),
        "w_up": nrm(ks[20], (DEPTH, D_MODEL, 2 * FFN_DIM), D_MODEL ** -0.5),
        "conv_w": nrm(ks[21], (DEPTH, CONV_WIDTH, 2 * FFN_DIM), CONV_WIDTH ** -0.5),
        "conv_b": nrm(ks[22], (DEPTH, 2 * FFN_DIM), 0.01),
        "w_down": nrm(ks[23], (DEPTH, FFN_DIM, D_MODEL), FFN_DIM ** -0.5),
    }

def reference(x, meta_tokens, norm1_g, w_in, q_norm_g, k_norm_g, ssm_a_re, ssm_a_im, ssm_log_step,
              ssm_b_re, ssm_b_im, ssm_c_re, ssm_c_im, ssm_d, w_glu, b_glu,
              w_attn_proj, w_ssm_proj, w_o, norm2_g, w_up, conv_w, conv_b, w_down):
    b = x.shape[0]
    l_real = N_META + x.shape[1]
    l_pad = -(-l_real // (2 * Q_BLOCK)) * (2 * Q_BLOCK)
    meta = jnp.broadcast_to(meta_tokens[None].astype(x.dtype), (b, N_META, D_MODEL))
    h = jnp.concatenate([meta, x], axis=1)
    h = jnp.pad(h, ((0, 0), (0, l_pad - l_real), (0, 0)))
    for i in range(DEPTH):
        h = hybrid_layer(h, norm1_g[i], w_in[i], q_norm_g[i], k_norm_g[i],
                         ssm_a_re[i], ssm_a_im[i], ssm_log_step[i],
                         ssm_b_re[i], ssm_b_im[i], ssm_c_re[i], ssm_c_im[i], ssm_d[i],
                         w_glu[i], b_glu[i], w_attn_proj[i], w_ssm_proj[i], w_o[i],
                         norm2_g[i], w_up[i], conv_w[i], conv_b[i], w_down[i])
    return h[:, N_META:l_real]


_drawn_inputs = setup_inputs


def setup_inputs(seed=0):
    import zlib

    import numpy as np

    out = dict(_drawn_inputs(seed))
    spreads = {}
    factors = {'norm1_g': 8.0,
     'q_norm_g': 8.0,
     'k_norm_g': 8.0,
     'ssm_a_re': 64.0,
     'ssm_a_im': 40.408,
     'ssm_log_step': 40.328,
     'ssm_b_re': 57.776,
     'ssm_b_im': 57.92,
     'ssm_c_re': 57.32,
     'ssm_c_im': 57.576,
     'b_glu': 58.151,
     'norm2_g': 31.598,
     'conv_b': 32.596}
    for name, (base, spread) in spreads.items():
        noise = np.random.default_rng([zlib.crc32(name.encode()), seed]).standard_normal(out[name].shape)
        drawn = base * np.exp(spread * noise) if base else spread * noise
        out[name] = __import__('jax').numpy.asarray(drawn.astype(out[name].dtype))
    for name, factor in factors.items():
        out[name] = (out[name] * factor).astype(out[name].dtype)
    return out
```

```python
from contextlib import ExitStack

import concourse.bass as bass
from concourse import mybir

F32 = mybir.dt.float32
F32R = mybir.dt.float32r
BF16 = mybir.dt.bfloat16
ALU = mybir.AluOpType
ACT = mybir.ActivationFunctionType

P = 128
D = 1024
SEQ = 512
META = 16
L = META + SEQ
LATE0 = 12
LL = L - LATE0
HL, HLL = L // 2, LL // 2
KD = D // P
HEADS, DH = 4, 64
SBW = HEADS * DH
SW = 512
GROUPS, GH, ST = 32, 16, 64
KS = SW // P
PAIRS = GROUPS // 2
FFN = 2816
KF = FFN // P
EPS = 1e-6
TT_ROWS = 88
NTT = L // TT_ROWS
T8 = 8
NC = L // T8
RP = PAIRS // 4
ROUNDS = 4
UT = 11
NEG = -1e30
TWO_PI = 6.283185307179586
CW1 = 6.28125
CW2 = 0.0019350051879882812
CW3 = 3.019916050773725e-07
ROUND_MAGIC = 12582912.0
PI_BELOW = 3.1415925
A_RE_MAX = -1e-4
BC_DMAS = 6
Q_LAST = 512
GELU_A, GELU_B = 1.5957691216057308, 0.044715

(S_STEP, S_MAG, S_SIN, S_SINH, S_COS, S_TH, S_LST, S_LRE, S_N, S_FR, S_FI, S_D2, S_D4, S_DEN, S_NR,
 S_T1, S_T2) = range(17)

U_SSM, U_K, U_V, U_Q, U_GATE, U_GLU, U_GATE2, U_PROJ, U_WO, U_UP, U_DOWN, U_END = \
    0, 4, 6, 8, 10, 24, 26, 28, 36, 44, 88, 104

KEY0 = (0, 128, 256, 384, 400)
REGIONS = ((0, 0, 0, 12, 256), (0, 244, 1, 128, 256),
           (1, 0, 0, 256, 528), (2, 0, 1, 256, 528),
           (3, 0, 2, 256, 528), (3, 272, 3, 384, 528), (3, 416, 4, 512, 528))
BANK_COLS = (372, 272, 272, 432)
BANK_OFF = (0, 372, 644, 916)
ATT_COLS = 1348
Q_SPLIT = 256

STEPS = {4: [("norm", 0)], 5: [("prep", 0), ("norm", 1)], 7: [("state", 0)],
         8: [("readout", 0), ("norm", 2)], 9: [("prep", 1), ("norm", 3)],
         10: [("state", 1)], 11: [("readout", 1)], 12: [("prep", 2)],
         13: [("state", 2)], 14: [("readout", 2)], 15: [("prep", 3)],
         16: [("state", 3)], 17: [("readout", 3)],
         18: [("scores", 0)], 19: [("suffix", 0)], 20: [("values", 0), ("scores", 1)],
         21: [("suffix", 1)], 22: [("values", 1), ("scores", 2), ("gelu", 0)],
         23: [("suffix", 2), ("gelu", 1)], 24: [("values", 2), ("scores", 3)],
         25: [("suffix", 3)], 26: [("values", 3)]}
MOVES = {2: [("u_write", 0)], 3: [("u_write", 1)], 4: [("u_write", 2), ("u_read", 0)],
         5: [("u_write", 3), ("u_read", 1)], 7: [("toep", 0)], 9: [("u_read", 2)],
         10: [("y_write", 0)], 11: [("toep", 1)], 12: [("u_read", 3)], 13: [("y_write", 1)],
         14: [("toep", 2)], 16: [("y_write", 2)], 17: [("toep", 3)], 19: [("y_write", 3)],
         20: [("y_read", 0)]}

ROW_ARE, ROW_AIM, ROW_STEP, ROW_SKIP = 0, 32, 64, 96
COL_CW, COL_CB, COL_N1, COL_N2, COL_BG, COL_QG, COL_KG, NCOLS = 0, 132, 176, 184, 192, 196, 197, 198


def norm_of(i):
    return (True, i, U_K + i) if i < 2 else (False, i - 2, U_Q + i - 2)


def gate_of(unit):
    return unit - U_GATE if unit < U_GLU else unit - U_GATE2 + U_GLU - U_GATE


def is_gate(unit):
    return U_GATE <= unit < U_GLU or U_GATE2 <= unit < U_PROJ


def shared_queries(region, other):
    return max(region[3], other[3]), min(region[4], other[4])


def hybrid_trunk(nc, x, meta_tokens, norm1_g, w_in, q_norm_g, k_norm_g, ssm_a_re, ssm_a_im,
                 ssm_log_step, ssm_b_re, ssm_b_im, ssm_c_re, ssm_c_im, ssm_d, w_glu, b_glu,
                 w_attn_proj, w_ssm_proj, w_o, norm2_g, w_up, conv_w, conv_b, w_down, out):
    u_dram = nc.dram_tensor("u_dram", (SW, T8, NC), F32, kind="Internal").ap()
    y_dram = nc.dram_tensor("y_dram", (SW, T8, NC), F32, kind="Internal").ap()

    ctx = ExitStack()
    with ctx:
        def alloc(stack, name, shape, dt=F32):
            return stack.enter_context(nc.sbuf_tensor(name, shape, dt))

        def sb(name, shape, dt=F32):
            return alloc(ctx, name, shape, dt)

        def sem(name):
            return ctx.enter_context(nc.semaphore(name))

        ps = ctx.enter_context(nc.psum_tensor("ps", [P, 8, 512], F32))

        raw = [sb(f"raw{i}", [P, UT * P]) for i in range(2)]
        hi = [sb(f"hi{i}", [P, UT * P], F32R) for i in range(2)]
        lo = [sb(f"lo{i}", [P, UT * P], F32R) for i in range(2)]
        xh = sb("xh", [P, KD, L], F32R)
        xl = sb("xl", [P, KD, L], F32R)
        hT = sb("hT", [P, KD, L])
        ident = sb("ident", [P, P])
        ones = sb("ones", [P, P])
        cols = sb("cols", [P, NCOLS])
        rb = sb("rb", [P, L])

        start = ExitStack()
        xtok = alloc(start, "xtok", [P, NTT, D])
        stack = alloc(start, "stack", [P, 3, P])
        cdup = alloc(start, "cdup", [P, 2, 4, 2, ST])
        start.close()

        mix = ExitStack()
        gates = alloc(mix, "gates", [P, 16 * LL])
        sq = [gates[:, 5088 + i * L:5088 + (i + 1) * L] for i in range(4)]
        ta = gates[:, 16 * LL - 2 * L:16 * LL - L]
        tb = gates[:, 16 * LL - L:16 * LL]
        gate = [gates[:, i * LL:(i + 1) * LL] for i in range(16)]
        qk = ExitStack()
        qT = alloc(qk, "qT", [P, 2, L])
        kT = alloc(qk, "kT", [P, 2, L])
        qk.close()
        ma = [alloc(mix, f"ma{i}", [P, LL]) for i in range(2)]
        mb = [alloc(mix, f"mb{i}", [P, LL]) for i in range(2)]
        pad = alloc(mix, "pad", [P, 4 * (L - LL)])
        vt = alloc(mix, "vt", [P, 5, SBW])
        atth = alloc(mix, "atth", [P, 2, LL], F32R)
        attl = alloc(mix, "attl", [P, 2, LL], F32R)
        blocks = alloc(mix, "blocks", [P, P])
        negtri = alloc(mix, "negtri", [P, P])
        negones = alloc(mix, "negones", [P, P])
        ident_bf = alloc(mix, "ident_bf", [P, P], BF16)
        mask = alloc(mix, "mask", [P, P], BF16)
        mask_last = alloc(mix, "mask_last", [P, META], BF16)
        nbglu = alloc(mix, "nbglu", [P, KS])
        ssx = alloc(mix, "ssx", [P, 4, NTT])

        early = ExitStack()
        uy = alloc(early, "uy", [P, 2, T8, NC])
        uc = alloc(early, "uc", [P, 2, 2 * RP, NC])
        yg = alloc(early, "yg", [P, 2 * RP, NC])
        rot = alloc(early, "rot", [P, 2, PAIRS, NC])
        decay = alloc(early, "decay", [P, PAIRS, NC])
        g_in = alloc(early, "g_in", [P, 2, RP, T8, GH])
        win = alloc(early, "win", [P, 2, RP * P])
        hout = alloc(early, "hout", [P, 2, RP, T8 + 1, GH])
        kern = alloc(early, "kern", [GH, 2 * RP, P])
        toep = alloc(early, "toep", [P, 2 * RP, P])
        mod = alloc(early, "mod", [P, 4, RP, NC])
        xst = alloc(early, "xst", [P, 2, 2, RP, NC])
        skip_i = alloc(early, "skip_i", [GH, GROUPS, GH])
        colc = alloc(early, "colc", [P, P])
        sm = alloc(early, "sm", [P, 20, PAIRS])
        pw = alloc(early, "pw", [P, 2, T8 + 1, PAIRS])
        en = alloc(early, "en", [P, 4, 2, PAIRS])
        bb = alloc(early, "bb", [P, 2, PAIRS, GH])
        braw = alloc(early, "braw", [P, 2, PAIRS, GH])
        ct = alloc(early, "ct", [P, 2, PAIRS, GH])
        pt = alloc(early, "pt", [P, RP * (T8 + 1) * GH])
        lst = alloc(early, "lst", [P, 2])
        early.close()
        scr = ExitStack()
        under = ExitStack()
        yT = alloc(under, "yT", [P, KS, T8, NC])
        gh = alloc(under, "gh", [P, KS, L], F32R)
        gl = alloc(under, "gl", [P, KS, L], F32R)
        soft = alloc(under, "soft", [P, ATT_COLS])
        prob = alloc(under, "prob", [P, ATT_COLS])
        under.close()
        mh = alloc(scr, "mh", [P, KD, LL], F32R)
        ml = alloc(scr, "ml", [P, KD, LL], F32R)
        pad2 = alloc(scr, "pad2", [P, 3 * KS * L + 2 * ATT_COLS - 2 * KD * LL + 16])
        sh = alloc(scr, "sh", [P, KS, L], F32R)
        sl = alloc(scr, "sl", [P, KS, L], F32R)
        gt = [alloc(scr, f"gt{i}", [P, L]) for i in range(2)]
        qz = [alloc(scr, f"qz{i}", [P, LL]) for i in range(2)]
        scr.close()
        mix.close()

        late = ExitStack()
        sqh = [alloc(late, f"sqh{i}", [P, LL]) for i in range(2)]
        acc = alloc(late, "acc", [P, LL])
        nv = alloc(late, "nv", [P, LL])
        ut = [alloc(late, f"ut{i}", [P, 2, LL]) for i in range(2)]
        cv = [alloc(late, f"cv{i}", [P, 2, SEQ]) for i in range(2)]
        ah = alloc(late, "ah", [P, KF, SEQ], F32R)
        al = alloc(late, "al", [P, KF, SEQ], F32R)
        late.close()
        fin = ExitStack()
        yo = [alloc(fin, f"yo{i}", [P, SEQ]) for i in range(2)]
        yt = [alloc(fin, f"yt{i}", [P, 4, P]) for i in range(2)]
        fin.close()

        raw_in = [sem(f"raw_in{i}") for i in range(2)]
        hi_ready = sem("hi_ready")
        lo_ready = sem("lo_ready")
        unit_done = sem("unit_done")
        drained = sem("drained")
        par_in = sem("par_in")
        stk_in = sem("stk_in")
        bc_in = sem("bc_in")
        x_in = [sem(f"x_in{i}") for i in range(3)]
        masks_set = sem("masks_set")
        stack_zero = sem("stack_zero")
        stack_full = sem("stack_full")
        cols_t = sem("cols_t")
        cols_set = sem("cols_set")
        ss_x = sem("ss_x")
        rx_ready = sem("rx_ready")
        rb_ps = sem("rb_ps")
        rb_set = sem("rb_set")
        xt_ps = sem("xt_ps")
        xt_copied = sem("xt_copied")
        xn_set = sem("xn_set")
        xh_set = sem("xh_set")
        x_ready = sem("x_ready")
        small_a = sem("small_a")
        small_v = sem("small_v")
        ct_set = sem("ct_set")
        rot_set = sem("rot_set")
        g_ready = sem("g_ready")
        h_ready = sem("h_ready")
        g_t = sem("g_t")
        k_ps = sem("k_ps")
        win_set = sem("win_set")
        kern_set = sem("kern_set")
        kern_out = [sem(f"kern_out{i}") for i in range(ROUNDS)]
        u_out = [sem(f"u_out{i}") for i in range(ROUNDS)]
        u_in = [sem(f"u_in{i}") for i in range(ROUNDS)]
        y_out = [sem(f"y_out{i}") for i in range(ROUNDS)]
        y_in = sem("y_in")
        st_ps = sem("st_ps")
        st_set = sem("st_set")
        y_ps = sem("y_ps")
        y_sq = sem("y_sq")
        y_arg = sem("y_arg")
        yg_set = sem("yg_set")
        sq_ready = sem("sq_ready")
        ss_ps = sem("ss_ps")
        ss_v = sem("ss_v")
        rs_a = sem("rs_a")
        normed = sem("normed")
        qz_set = sem("qz_set")
        z_ps = sem("z_ps")
        z_ln = sem("z_ln")
        soft_set = sem("soft_set")
        suf_ps = sem("suf_ps")
        prob_set = sem("prob_set")
        av_ps = sem("av_ps")
        ath_set = sem("ath_set")
        atl_set = sem("atl_set")
        gate_exp = sem("gate_exp")
        gate_one = sem("gate_one")
        gate_set = sem("gate_set")
        gh_set = sem("gh_set")
        gl_set = sem("gl_set")
        glu_exp = sem("glu_exp")
        glu_val = sem("glu_val")
        sh_set = sem("sh_set")
        sl_set = sem("sl_set")
        m_gated = sem("m_gated")
        m_sum = sem("m_sum")
        mh_set = sem("mh_set")
        ml_set = sem("ml_set")
        h_set = sem("h_set")
        h_sq = sem("h_sq")
        h_acc = sem("h_acc")
        zh_set = sem("zh_set")
        z_ready = sem("z_ready")
        ss2_ps = sem("ss2_ps")
        ss2_v = sem("ss2_v")
        r2_a = sem("r2_a")
        r2_set = sem("r2_set")
        up_v = sem("up_v")
        cv_a = sem("cv_a")
        cv_mid = sem("cv_mid")
        cv_v = sem("cv_v")
        silu_a = sem("silu_a")
        act_p = sem("act_p")
        ah_set = sem("ah_set")
        al_set = sem("al_set")
        y_add = sem("y_add")
        yt_ps = sem("yt_ps")
        yt_set = sem("yt_set")
        out_done = [sem(f"out_done{i}") for i in range(2)]
        act_link = sem("act_link")
        dve_link = sem("dve_link")
        pool_link = sem("pool_link")

        def psum2(bank, width, part=slice(0, P)):
            return ps[part, bank:bank + 2, 0:width]

        def halves(ap, width):
            return ap.rearrange("p (b c) -> p b c", c=width)

        def linker(eng, link):
            count = [0]

            def wait_for(ins):
                count[0] += 1
                ins.then_inc(link, 1)
                eng.wait_ge(link, count[0])
            return wait_for

        block = ctx.enter_context(nc.Block())

        @block.sync
        def _(sp):
            def in_cols(c0):
                return w_in[0].rearrange("(k p) c -> p k c", p=P)[:, :, c0:c0 + P]

            def load(slot, parts):
                at = 0
                for src in parts:
                    n = src.shape[1] * src.shape[2]
                    sp.dma_start(raw[slot][:, at:at + n].rearrange("p (k c) -> p k c", c=src.shape[2]),
                                 src).then_inc(raw_in[slot], 16)
                    at += n

            def halved(src):
                k = src.shape[1]
                return [src[:, 0:(k + 1) // 2, :], src[:, (k + 1) // 2:k, :]]

            def source(unit):
                if unit < U_K:
                    return halved(in_cols(3 * SBW + P * unit))
                if unit < U_V:
                    return halved(in_cols(SBW + P * (unit - U_K)))
                if unit < U_Q:
                    return halved(in_cols(2 * SBW + P * (unit - U_V)))
                if unit < U_GATE:
                    return halved(in_cols(P * (unit - U_Q)))
                if is_gate(unit):
                    return halved(in_cols(3 * SBW + SW + P * gate_of(unit)))
                if unit < U_GATE2:
                    c0 = 2 * P * (unit - U_GLU)
                    return halved(w_glu[0].rearrange("(k p) c -> p k c", p=P)[:, :, c0:c0 + 2 * P])
                if unit < U_WO:
                    c0 = P * (unit - U_PROJ)
                    return [w[0].rearrange("(k p) c -> p k c", p=P)[:, :, c0:c0 + P]
                            for w in (w_attn_proj, w_ssm_proj)]
                c0 = P * (unit - U_WO)
                return halved(w_o[0].rearrange("(k p) c -> p k c", p=P)[:, :, c0:c0 + P])

            def up_source(f, part):
                src = w_up[0].rearrange("(k p) c -> p k c", p=P)
                return halved(src[:, :, bass.ds(f * P + part * FFN, P)])

            def down_source(m, half):
                src = w_down[0].rearrange("(k p) c -> p k c", p=P)[:, half * UT:(half + 1) * UT, :]
                return halved(src[:, :, bass.ds(m * P, P)])

            sp.dma_start(xtok[0:META, 0, :], meta_tokens).then_inc(x_in[0], 16)
            sp.dma_start(xtok[META:TT_ROWS, 0, :], x[0, 0:TT_ROWS - META, :]).then_inc(x_in[0], 16)
            rest = x[0, TT_ROWS - META:SEQ, :].rearrange("(i p) d -> p i d", p=TT_ROWS)
            sp.dma_start(xtok[0:TT_ROWS, 1:3, :], rest[:, 0:2, :]).then_inc(x_in[1], 16)
            sp.dma_start(xtok[0:TT_ROWS, 3:NTT, :], rest[:, 2:NTT - 1, :]).then_inc(x_in[2], 16)
            load(0, source(0))
            load(1, source(1))

            def u_write(r):
                sp.wait_ge(drained, r + 1)
                sp.dma_start(u_dram[r * P:(r + 1) * P], uy[:, r % 2]).then_inc(u_out[r], 16)

            def u_read(r):
                sp.wait_ge(u_out[r], 16)
                if r >= 2:
                    sp.wait_ge(y_ps, r - 1)
                src = u_dram[r * P:(r + 1) * P].rearrange("(g h) j c -> j h g c", h=GH)
                for j in range(T8):
                    p0 = GH * (T8 - 1 - j)
                    sp.dma_start(uc[p0:p0 + GH, r % 2], src[j]).then_inc(u_in[r], 16)

            def toep_move(r):
                sp.wait_ge(kern_set, r + 1)
                for j in range(T8):
                    p0 = GH * (T8 - 1 - j)
                    sp.dma_start(toep[p0:p0 + GH, :, GH * j:P],
                                 kern[:, :, 0:P - GH * j]).then_inc(kern_out[r], 16)

            def y_write(r):
                sp.wait_ge(yg_set, r + 1)
                dst = y_dram[r * P:(r + 1) * P].rearrange("(g h) j c -> j h g c", h=GH)
                for j in range(T8):
                    sp.dma_start(dst[j], yg[GH * j:GH * (j + 1)]).then_inc(y_out[r], 16)

            def y_read(_):
                for r in range(ROUNDS):
                    sp.wait_ge(y_out[r], 16 * T8)
                sp.wait_ge(st_set, ROUNDS)
                sp.wait_ge(y_ps, ROUNDS)
                sp.dma_start(yT[:], y_dram.rearrange("(r p) j c -> p r j c", p=P)).then_inc(y_in, 16)

            move = {"u_write": u_write, "u_read": u_read, "toep": toep_move, "y_write": y_write,
                    "y_read": y_read}
            for done in range(U_UP - 2):
                sp.wait_ge(lo_ready, done + 1)
                load((done + 2) % 2, source(done + 2))
                for name, r in MOVES.get(done, []):
                    move[name](r)

            with sp.Fori(0, KF) as f:
                for part in range(2):
                    sp.wait_ge(lo_ready, f * 2 + (U_UP - 1 + part))
                    load(part, up_source(f, part))

            def store(m, s):
                sp.wait_ge(yt_set, m + 1)
                dst = out[0].rearrange("(t p) c -> p t c", p=P)[:, :, bass.ds(m * P, P)]
                sp.dma_start(dst, yt[s][:]).then_inc(out_done[s], 16)

            def down_load(m):
                for half in range(2):
                    sp.wait_ge(lo_ready, m * 2 + (U_DOWN - 1 + half))
                    load(half, down_source(m, half))

            down_load(0)
            down_load(1)
            with sp.Fori(1, KD // 2) as mm:
                for s in range(2):
                    down_load(mm * 2 + s)
                    store(mm * 2 + (s - 2), s)
            for s in range(2):
                store(KD - 2 + s, s)
            for s in range(2):
                sp.wait_ge(out_done[s], 16 * KD // 2)

        @block.gpsimd
        def _(pool):
            link = linker(pool, pool_link)
            link(pool.memset(stack[:, 0, :], 0.0))
            pool.dma_start(stack[ROW_ARE:ROW_ARE + PAIRS, 0, :],
                           ssm_a_re[0].rearrange("(r g) p -> r (g p)", g=2)).then_inc(stk_in, 16)
            pool.dma_start(stack[ROW_AIM:ROW_AIM + PAIRS, 0, :],
                           ssm_a_im[0].rearrange("(r g) p -> r (g p)", g=2)).then_inc(stk_in, 16)
            pool.dma_start(stack[ROW_SKIP:ROW_SKIP + GROUPS, 0, 0:GH], ssm_d[0]).then_inc(stk_in, 16)
            pool.dma_start(lst[ROW_STEP:ROW_STEP + PAIRS, :],
                           ssm_log_step[0].rearrange("(r g) -> r g", g=2)).then_inc(stk_in, 16)
            link(pool.memset(ident[:], 0.0))
            link(pool.affine_select(out=ident[:], in_=ident[:], compare_op=ALU.not_equal, fill=1.0,
                                    base=0, pattern=[[-1, P]], channel_multiplier=1))
            pool.memset(ones[:], 1.0).then_inc(masks_set, 1)
            pool.wait_ge(masks_set, 1)
            link(pool.memset(blocks[:], 0.0))
            link(pool.memset(blocks[0:DH, 0:DH], 1.0))
            link(pool.memset(blocks[DH:P, DH:P], 1.0))
            link(pool.memset(negones[:], -1.0))
            link(pool.memset(negtri[:], -1.0))
            link(pool.affine_select(out=negtri[:], in_=negtri[:], compare_op=ALU.is_ge, fill=0.0,
                                    base=0, pattern=[[-1, P]], channel_multiplier=1))
            link(pool.tensor_copy(ident_bf[:], ident[:]))
            link(pool.memset(mask[:], NEG))
            link(pool.affine_select(out=mask[:], in_=mask[:], compare_op=ALU.is_ge, fill=0.0,
                                    base=0, pattern=[[-1, P]], channel_multiplier=1))
            first = Q_LAST - KEY0[4]
            link(pool.memset(mask_last[:], 0.0))
            link(pool.affine_select(out=mask_last[:], in_=mask_last[:], compare_op=ALU.is_ge,
                                    fill=NEG, base=-first, pattern=[[0, META]],
                                    channel_multiplier=1))
            link(pool.affine_select(out=mask_last[:], in_=mask_last[:], compare_op=ALU.is_gt,
                                    fill=NEG, base=first, pattern=[[1, META]],
                                    channel_multiplier=-1))
            link(pool.memset(toep[:], 0.0))
            link(pool.memset(decay[:], 0.0))
            link(pool.memset(xst[:], 0.0))
            link(pool.memset(rot[:, 0, :, 0:1], 1.0))
            link(pool.memset(rot[:, 1, :, 0:1], 0.0))
            link(pool.memset(pw[:, 0, 0, :], 1.0))
            pool.memset(pw[:, 1, 0, :], 0.0).then_inc(masks_set, 1)
            pool.wait_ge(masks_set, 2)

            def cmul(o, a, b, t):
                link(pool.tensor_tensor(o[0], a[0], b[0], ALU.mult))
                link(pool.tensor_tensor(t, a[1], b[1], ALU.mult))
                link(pool.tensor_tensor(o[0], o[0], t, ALU.subtract))
                link(pool.tensor_tensor(o[1], a[0], b[1], ALU.mult))
                link(pool.tensor_tensor(t, a[1], b[0], ALU.mult))
                link(pool.tensor_tensor(o[1], o[1], t, ALU.add))

            def both(ap):
                return ap[:, 0], ap[:, 1]

            def tmp(*shape):
                n = 1
                for s in shape:
                    n *= s
                v = pt[:, 0:n]
                if len(shape) == 1:
                    return v
                if len(shape) == 2:
                    return v.rearrange("p (a b) -> p a b", b=shape[1])
                return v.rearrange("p (a b c) -> p a b c", b=shape[1], c=shape[2])

            pool.wait_ge(small_v, 3)
            for n in (1, 2, 4):
                at = (pw[:, 0, n:n + 1, :].broadcast_to([P, n, PAIRS]),
                      pw[:, 1, n:n + 1, :].broadcast_to([P, n, PAIRS]))
                cmul((pw[:, 0, n + 1:2 * n + 1, :], pw[:, 1, n + 1:2 * n + 1, :]),
                     (pw[:, 0, 1:n + 1, :], pw[:, 1, 1:n + 1, :]), at, tmp(n, PAIRS))
            pool.wait_ge(bc_in, 16 * BC_DMAS)
            f = [sm[:, c, :].unsqueeze(2).broadcast_to([P, PAIRS, GH]) for c in (S_FR, S_FI)]
            cmul(both(bb), both(braw), f, tmp(PAIRS, GH))
            pool.wait_ge(ct_set, 1)

            def input_map(r):
                if r:
                    pool.wait_ge(g_t, r)
                pr = slice(r * RP, (r + 1) * RP)
                for i in range(RP):
                    at = r * RP + i
                    cmul([g_in[:, c, i] for c in range(2)],
                         [pw[:, c, 0:T8, at:at + 1].broadcast_to([P, T8, GH]) for c in range(2)],
                         [bb[:, c, at:at + 1, :].broadcast_to([P, T8, GH]) for c in range(2)],
                         tmp(T8, GH))
                pool.nop().then_inc(g_ready, 1)

            def output_map(r):
                if r:
                    pool.wait_ge(y_ps, r)
                for i in range(RP):
                    at = r * RP + i
                    shape = [P, T8 + 1, GH]
                    a = [pw[:, c, :, at:at + 1].broadcast_to(shape) for c in range(2)]
                    b = [ct[:, c, at:at + 1, :].broadcast_to(shape) for c in range(2)]
                    t = tmp(T8 + 1, GH)
                    o = hout[:, 0, i], hout[:, 1, i]
                    link(pool.tensor_tensor(o[0], a[0], b[0], ALU.mult))
                    link(pool.tensor_tensor(t, a[1], b[1], ALU.mult))
                    link(pool.tensor_tensor(o[0], o[0], t, ALU.add))
                    link(pool.tensor_tensor(o[1], a[0], b[1], ALU.mult))
                    link(pool.tensor_tensor(t, a[1], b[0], ALU.mult))
                    link(pool.tensor_tensor(o[1], o[1], t, ALU.subtract))
                pool.nop().then_inc(h_ready, 1)

            input_map(0)
            output_map(0)
            e = [en[:, 0], en[:, 1]]
            n = 1
            k = 0
            link(pool.tensor_copy(en[:, 0, 0], sm[:, S_COS, :]))
            link(pool.tensor_copy(en[:, 0, 1], sm[:, S_SIN, :]))
            for _ in range(3):
                cmul(both(en[:, 1 - k]), both(en[:, k]), both(en[:, k]), tmp(PAIRS))
                k = 1 - k
            while n < NC:
                w = min(n, NC - n)
                shape = [P, PAIRS, w]
                at = [en[:, k, c].unsqueeze(2).broadcast_to(shape) for c in range(2)]
                cmul([rot[:, c, :, n:n + w] for c in range(2)],
                     [rot[:, c, :, 0:w] for c in range(2)], at, tmp(PAIRS, w))
                n *= 2
                if n < NC:
                    cmul(both(en[:, 1 - k]), both(en[:, k]), both(en[:, k]), tmp(PAIRS))
                    k = 1 - k
            link(pool.tensor_tensor(sm[:, S_D2, :], sm[:, S_MAG, :], sm[:, S_MAG, :], ALU.mult))
            link(pool.tensor_tensor(sm[:, S_D4, :], sm[:, S_D2, :], sm[:, S_D2, :], ALU.mult))
            link(pool.tensor_tensor(sm[:, S_D2, :], sm[:, S_D4, :], sm[:, S_D4, :], ALU.mult))
            pool.tensor_copy(decay[:, :, 1:NC], sm[:, S_D2, :].unsqueeze(2)
                             .broadcast_to([P, PAIRS, NC - 1])).then_inc(rot_set, 1)

            def head_q(h):
                if h >= 2:
                    pool.wait_ge(z_ps, h - 1)
                part = slice(DH * (h % 2), DH * (h % 2) + DH)
                pool.tensor_copy(qz[h % 2][part, :], qT[part, h // 2, 0:LL]).then_inc(qz_set, 1)
                pool.wait_ge(qz_set, h + 1)

            for unit in range(U_PROJ):
                for name, i in STEPS.get(unit, []):
                    if name == "prep" and i + 1 < ROUNDS:
                        input_map(i + 1)
                    if name == "readout" and i + 1 < ROUNDS:
                        output_map(i + 1)
                    if name == "readout" and i + 1 == ROUNDS:
                        pool.wait_ge(y_ps, ROUNDS)
                        pool.wait_ge(yg_set, ROUNDS)
                        pool.wait_ge(normed, 4)
                        link(pool.memset(qz[0][DH:P, :], 0.0))
                        link(pool.memset(qz[1][0:DH, :], 0.0))
                        head_q(0)
                        head_q(1)
                    if name == "values" and i + 2 < HEADS:
                        head_q(i + 2)
                if is_gate(unit):
                    i = gate_of(unit)
                    pool.wait_ge(gate_exp, i + 1)
                    pool.tensor_scalar(gate[i], gate[i], 1.0, None, ALU.add).then_inc(gate_one, 1)
                    pool.wait_ge(gate_one, i + 1)
            for m in range(KD):
                pool.wait_ge(m_gated, m + 1)
                pool.tensor_tensor(ma[m % 2][:], ma[m % 2][:], mb[m % 2][:], ALU.add)\
                    .then_inc(m_sum, 1)
            for m in range(KD):
                pool.wait_ge(h_sq, m + 1)
                if m == 0:
                    pool.tensor_copy(acc[:], sqh[0][:]).then_inc(h_acc, 1)
                else:
                    pool.wait_ge(h_acc, m)
                    pool.tensor_tensor(acc[:], acc[:], sqh[m % 2][:], ALU.add).then_inc(h_acc, 1)

            def product(f, s):
                pool.wait_ge(silu_a, f + 1)
                pool.wait_ge(cv_v, f * 2 + 2)
                pool.tensor_tensor(cv[s][:, 1], cv[s][:, 0], cv[s][:, 1], ALU.mult)\
                    .then_inc(act_p, 1)

            with pool.Fori(0, KF // 2) as ff:
                for s in range(2):
                    product(ff * 2 + s, s)

        @block.scalar
        def _(act):
            link = linker(act, act_link)

            def split(unit, slot, n):
                act.wait_ge(raw_in[slot], (unit - slot) * 16 + 32)
                if not isinstance(unit, int) or unit >= 2:
                    act.wait_ge(unit_done, unit - 1)
                act.activation(hi[slot][:, 0:n * P], raw[slot][:, 0:n * P], ACT.Copy)\
                    .then_inc(hi_ready, 1)

            rows = [(stack[:, 1, :], conv_w[0].rearrange("j (m c) -> (j m) c", c=P)[0:P, :]),
                    (stack[0:4, 2, :], conv_w[0].rearrange("j (m c) -> (j m) c", c=P)[P:P + 4, :]),
                    (stack[4:48, 2, :], conv_b[0].rearrange("(m c) -> m c", c=P)),
                    (stack[48:56, 2, :], norm1_g[0].rearrange("(m c) -> m c", c=P)),
                    (stack[56:64, 2, :], norm2_g[0].rearrange("(m c) -> m c", c=P)),
                    (stack[64:68, 2, :], b_glu[0].rearrange("(m c) -> m c", c=P)),
                    (stack[68:69, 2, 0:DH], q_norm_g), (stack[68:69, 2, DH:P], q_norm_g),
                    (stack[69:70, 2, 0:DH], k_norm_g), (stack[69:70, 2, DH:P], k_norm_g)]
            for dst, src in rows:
                act.dma_start(dst, src).then_inc(par_in, 16)
            for c, (b_in, c_in) in enumerate(((ssm_b_re, ssm_c_re), (ssm_b_im, ssm_c_im))):
                act.dma_start(braw[:, c], b_in[0].rearrange("(r g) p h -> (g p) r h", g=2))\
                    .then_inc(bc_in, 16)
                for d in range(2):
                    act.dma_start(cdup[:, c, :, d, :],
                                  c_in[0].rearrange("(t g) h p -> (g h) t p", g=8)).then_inc(bc_in, 16)
            act.preload_act_table_set("natural_log_exp_and_others")

            for i in range(NTT):
                if i in (0, 1, 3):
                    act.wait_ge(x_in[(i + 1) // 2], 32 if i == 0 else 16)
                rows = slice(0, TT_ROWS)
                act.activation(ps[rows, 6:8, :], halves(xtok[rows, i, :], 512), ACT.Square,
                               accum_out=ssx[rows, 0, i:i + 1]).then_inc(ss_x, 1)
                act.wait_ge(ss_x, i + 1)
            act.wait_ge(rx_ready, 1)
            link(act.activation(ssx[rows, 1, :], ssx[rows, 0, :], ACT.Ln))
            act.activation(ssx[rows, 1, :], ssx[rows, 1, :], ACT.Exp, scale=-0.5).then_inc(ss_x, 1)
            act.wait_ge(rb_ps, 1)
            act.activation(halves(rb[:], HL), psum2(6, HL), ACT.Copy).then_inc(rb_set, 1)
            for k in range(KD):
                act.wait_ge(xt_ps, k + 1)
                act.activation(halves(hT[:, k], HL), psum2(4 + 2 * (k % 2), HL), ACT.Copy)\
                    .then_inc(xt_copied, 1)
                act.wait_ge(xn_set, k + 1)
                act.activation(xh[:, k], qT[:, k % 2], ACT.Copy).then_inc(xh_set, 1)
                if k == 1:
                    split(0, 0, KD)
                if k == 3:
                    split(1, 1, KD)

            def small(i):
                if i == 0:
                    act.wait_ge(small_v, 1)
                    act.activation(sm[:, S_STEP, :], colc[:, ROW_STEP:ROW_STEP + PAIRS], ACT.Exp)\
                        .then_inc(small_a, 1)
                    act.wait_ge(small_v, 2)
                    act.activation(sm[:, S_MAG, :], sm[:, S_LST, :], ACT.Exp)
                    act.activation(sm[:, S_SIN, :], sm[:, S_TH, :], ACT.Sin)
                    act.activation(sm[:, S_SINH, :], sm[:, S_TH, :], ACT.Sin, scale=0.5)\
                        .then_inc(small_a, 1)
                    act.preload_act_table_set("natural_log_exp_and_others")

            small(0)

            def norm(i):
                is_k, t, _ = norm_of(i)
                w = L if is_k else LL
                act.wait_ge(ss_v, i + 1)
                link(act.activation(ta[:, 0:w], tb[:, 0:w], ACT.Ln))
                act.activation(ta[:, 0:w], ta[:, 0:w], ACT.Exp, scale=-0.5).then_inc(rs_a, 1)

            def prep(r):
                act.wait_ge(g_t, r + 1)
                for c in range(2):
                    ins = act.activation(win[:, c], ps[:, 4 + c, :], ACT.Copy)
                ins.then_inc(win_set, 1)

            def readout(r):
                act.wait_ge(y_ps, r + 1)
                act.wait_ge(normed, 4 if r else 2)
                if r:
                    act.wait_ge(yg_set, r)
                act.activation(halves(ta, HL), psum2(6, HL), ACT.Square).then_inc(y_sq, 1)
                act.wait_ge(y_arg, r + 1)
                act.activation(ta, ta, ACT.Exp, scale=-1.0).then_inc(y_sq, 1)

            def scores(h):
                act.wait_ge(z_ps, h + 1)
                if h:
                    act.wait_ge(av_ps, h)
                for b in range(4):
                    ins = act.activation(prob[:, BANK_OFF[b]:BANK_OFF[b] + BANK_COLS[b]],
                                         ps[:, 4 + b, 0:BANK_COLS[b]], ACT.Abs)
                link(ins)
                link(act.activation(prob[:], prob[:], ACT.Exp, scale=-1.0))
                act.activation(prob[:], prob[:], ACT.Ln, bias=1.0).then_inc(z_ln, 1)

            def suffix(h):
                act.wait_ge(suf_ps, h + 1)
                act.wait_ge(soft_set, h + 1)
                for b in range(4):
                    ins = act.activation(prob[:, BANK_OFF[b]:BANK_OFF[b] + BANK_COLS[b]],
                                         ps[:, 4 + b, 0:BANK_COLS[b]], ACT.Exp)
                ins.then_inc(prob_set, 1)

            def values(h):
                act.wait_ge(av_ps, h + 1)
                part = slice(DH * (h % 2), DH * (h % 2) + DH)
                act.activation(atth[part, h // 2, 0:Q_SPLIT - LATE0],
                               ps[part, 4, 0:Q_SPLIT - LATE0], ACT.Copy)
                act.activation(atth[part, h // 2, Q_SPLIT - LATE0:LL], ps[part, 5, 0:L - Q_SPLIT],
                               ACT.Copy).then_inc(ath_set, 1)

            def gelu(i):
                if i == 0:
                    act.wait_ge(y_in, 16)
                for r in (2 * i, 2 * i + 1):
                    act.activation(gh[:, r].rearrange("p (c j) -> p c j", j=T8),
                                   yT[:, r].rearrange("p j c -> p c j"), ACT.Copy)\
                        .then_inc(gh_set, 1)

            steps = {"norm": norm, "prep": prep, "readout": readout, "scores": scores,
                     "suffix": suffix, "values": values, "gelu": gelu}

            def evacuate(unit):
                act.wait_ge(unit_done, unit + 1)
                b = 2 * (unit % 2)
                if unit < U_K:
                    if unit >= 2:
                        act.wait_ge(u_out[unit - 2], 16)
                    dst = uy[:, unit % 2].rearrange("p j (k c) -> p k c j", k=2)
                    for k in range(2):
                        ins = act.activation(dst[:, k], ps[:, b + k, 0:HL]
                                             .rearrange("p (c j) -> p c j", j=T8), ACT.Copy)
                    ins.then_inc(drained, 1)
                elif unit < U_V or U_Q <= unit < U_GATE:
                    i = unit - U_K if unit < U_V else unit - U_Q + 2
                    is_k, t, _ = norm_of(i)
                    dst, w = (kT, HL) if is_k else (qT, HLL)
                    ins = act.activation(halves(dst[:, t, 0:2 * w], w), psum2(b, w), ACT.Copy)
                    ins.then_inc(drained, 1)
                    act.wait_ge(drained, unit + 1)
                    act.activation(sq[i][:, 0:2 * w], dst[:, t, 0:2 * w], ACT.Square)\
                        .then_inc(sq_ready, 1)
                elif unit < U_Q:
                    c0 = P * (unit - U_V)
                    act.activation(vt[:, 0:4, c0:c0 + P],
                                   ps[:, b, :].rearrange("p (k c) -> p k c", c=P), ACT.Copy)
                    act.activation(vt[:, 4, c0:c0 + P], ps[:, b + 1, 0:P], ACT.Copy)\
                        .then_inc(drained, 1)
                elif is_gate(unit):
                    act.activation(halves(gate[gate_of(unit)], HLL), psum2(b, HLL), ACT.Exp,
                                   scale=-1.0).then_inc(gate_exp, 1)
                else:
                    for mm in range(2):
                        m = 2 * (unit - U_GLU) + mm
                        if m >= 2:
                            act.wait_ge(sl_set, m - 1)
                        ins = act.activation(halves(gt[mm][:], HL), psum2(2 * mm, HL), ACT.Exp,
                                             bias=nbglu[:, m:m + 1], scale=-1.0)
                        ins.then_inc(glu_exp, 1)
                    for mm in range(2):
                        m = 2 * (unit - U_GLU) + mm
                        act.wait_ge(glu_val, m + 1)
                        act.activation(sh[:, m], gt[mm][:], ACT.Copy).then_inc(sh_set, 1)

            def tiles_of(unit):
                return 6 if U_PROJ <= unit < U_WO else KD

            for unit in range(U_PROJ):
                split(unit + 2, unit % 2, tiles_of(unit + 2))
                evacuate(unit)
                for name, i in STEPS.get(unit, []):
                    if name in steps:
                        steps[name](i)
            for m in range(KD):
                unit = U_PROJ + m
                split(unit + 2, unit % 2, tiles_of(unit + 2))
                act.wait_ge(m_sum, m + 1)
                act.activation(mh[:, m], ma[m % 2][:], ACT.Copy).then_inc(mh_set, 1)
            for m in range(KD):
                unit = U_WO + m
                split(unit + 2, unit % 2, KD)
                act.wait_ge(h_set, m + 1)
                if m >= 2:
                    act.wait_ge(h_acc, m - 1)
                act.activation(sqh[m % 2][:], hT[:, m, LATE0:L], ACT.Square).then_inc(h_sq, 1)
                act.activation(xh[:, m, 0:LL], hT[:, m, LATE0:L], ACT.Copy,
                               scale=cols[:, COL_N2 + m:COL_N2 + m + 1]).then_inc(zh_set, 1)
            act.wait_ge(ss2_v, 1)
            link(act.activation(rb[:, 0:LL], nv[:], ACT.Ln))
            act.activation(rb[:, 0:LL], rb[:, 0:LL], ACT.Exp, scale=-0.5).then_inc(r2_a, 1)
            act.preload_act_table_set("silu_and_others")

            def cast_product(f, s):
                act.wait_ge(act_p, f + 1)
                act.activation(ah[:, bass.ds(f, 1), :].rearrange("p a c -> p (a c)"), cv[s][:, 1],
                               ACT.Copy).then_inc(ah_set, 1)

            def up(f, s, tiles=KD):
                for part in range(2):
                    split(f * 2 + (U_UP + 2 + part), part, tiles)
                    act.wait_ge(up_v, f * 2 + (part + 1))
                    if part == 0 and not (isinstance(f, int) and f < 2):
                        act.wait_ge(al_set, f - 1)
                    m = f + part * KF
                    act.activation(cv[s][:, part], ut[s][:, part, 2:2 + SEQ], ACT.Identity,
                                   bias=cols[:, bass.ds(m + COL_CB, 1)],
                                   scale=cols[:, bass.ds(m + COL_CW, 1)]).then_inc(cv_a, 1)
                if not (isinstance(f, int) and f < 1):
                    cast_product(f - 1, 1 - s)
                act.wait_ge(cv_v, f * 2 + 1)
                act.activation(cv[s][:, 0], cv[s][:, 0], ACT.Silu).then_inc(silu_a, 1)

            up(0, 0)
            up(1, 1)
            with act.Fori(1, KF // 2 - 1) as ff:
                for s in range(2):
                    up(ff * 2 + s, s)
            up(KF - 2, 0)
            up(KF - 1, 1, UT)
            cast_product(KF - 1, 1)

            def turned(m, s, stored):
                act.wait_ge(yt_ps, m + 1)
                if not isinstance(stored, int) or stored:
                    act.wait_ge(out_done[s], 16 * stored)
                act.activation(yt[s][:], ps[:, 4 + s, :].rearrange("p (t c) -> p t c", c=P),
                               ACT.Copy).then_inc(yt_set, 1)

            def down(m, stored, s):
                for half in range(2):
                    split(m * 2 + (U_DOWN + 2 + half), half, UT)
                turned(m - 1, s, stored)

            for half in range(2):
                split(U_DOWN + 2 + half, half, UT)
            down(1, 0, 0)
            down(2, 0, 1)
            with act.Fori(1, KD // 2 - 1) as mm:
                for s in range(2):
                    down(mm * 2 + (1 + s), mm, s)
            for s in range(2):
                turned(KD - 2 + s, s, KD // 2 - 1)

        @block.vector
        def _(dve):
            link = linker(dve, dve_link)

            def split(unit, slot, n):
                dve.wait_ge(hi_ready, unit + 1)
                dve.tensor_tensor(lo[slot][:, 0:n * P], raw[slot][:, 0:n * P],
                                  hi[slot][:, 0:n * P].bitcast(F32), ALU.subtract)\
                   .then_inc(lo_ready, 1)

            def newton(r, v, t, factor=1.0):
                link(dve.tensor_tensor(t, r, r, ALU.mult))
                link(dve.tensor_tensor(t, t, v, ALU.mult))
                link(dve.tensor_scalar(t, t, -0.5 * factor, 1.5 * factor, ALU.mult, ALU.add))
                return dve.tensor_tensor(r, r, t, ALU.mult)

            dve.wait_ge(stk_in, 64)
            sr = slice(ROW_STEP, ROW_STEP + PAIRS)
            dve.tensor_copy(stack[sr, 0, :].rearrange("r (g p) -> r g p", g=2),
                            lst[sr].unsqueeze(2).broadcast_to([PAIRS, 2, ST]))\
               .then_inc(stack_full, 1)

            rows = slice(0, TT_ROWS)
            v, r, t = (ssx[rows, i, :] for i in (0, 1, 2))
            diag = vt[rows].rearrange("p a b -> p (a b)")[:, 0:NTT * TT_ROWS]
            dve.wait_ge(ss_x, NTT)
            dve.tensor_scalar(v, v, 1.0 / D, EPS, ALU.mult, ALU.add).then_inc(rx_ready, 1)
            dve.wait_ge(ss_x, NTT + 1)
            dve.wait_ge(masks_set, 1)
            link(newton(r, v, t))
            dve.tensor_tensor(diag.rearrange("p (i c) -> p i c", c=TT_ROWS),
                              ident[rows, 0:TT_ROWS].unsqueeze(1)
                              .broadcast_to([TT_ROWS, NTT, TT_ROWS]),
                              r.unsqueeze(2).broadcast_to([TT_ROWS, NTT, TT_ROWS]), ALU.mult)\
               .then_inc(rx_ready, 1)
            dve.wait_ge(cols_t, 1)
            link(dve.tensor_copy(colc[:], ps[:, 0, 0:P]))
            link(dve.tensor_copy(cols[:], ps[:, 0, P:P + NCOLS]))
            dve.tensor_scalar(nbglu[:], cols[:, COL_BG:COL_BG + KS], -1.0, None, ALU.mult)\
               .then_inc(cols_set, 1)
            dve.wait_ge(cols_t, 2)
            for c in range(2):
                src = ps[:, 1 + c, :].rearrange("p (r g h) -> p r g h", g=2, h=GH)
                for g in range(2):
                    part = slice(ST * g, ST * g + ST)
                    ins = dve.tensor_scalar(ct[part, c], src[part, :, g, :], 1.0 - 2.0 * c, None,
                                            ALU.mult)
            ins.then_inc(ct_set, 1)

            def x_lo(k):
                dve.wait_ge(xh_set, k + 1)
                dve.tensor_tensor(xl[:, k], qT[:, k % 2], xh[:, k].bitcast(F32), ALU.subtract)\
                   .then_inc(x_ready, 1)

            dve.wait_ge(rb_set, 1)
            for k in range(KD):
                dve.wait_ge(xt_copied, k + 1)
                if k >= 2:
                    dve.wait_ge(x_ready, k - 1)
                dve.scalar_tensor_tensor(qT[:, k % 2], hT[:, k], cols[:, COL_N1 + k:COL_N1 + k + 1],
                                         rb[:], ALU.mult, ALU.mult).then_inc(xn_set, 1)
                if k:
                    x_lo(k - 1)
                if k == 2:
                    split(0, 0, KD)
                if k == 4:
                    split(1, 1, KD)
            x_lo(KD - 1)

            def s(i):
                return sm[:, i, :]

            def tt(o, a, b, op):
                link(dve.tensor_tensor(s(o), s(a), s(b), op))

            are = colc[:, ROW_ARE:ROW_ARE + PAIRS]
            aim = colc[:, ROW_AIM:ROW_AIM + PAIRS]
            dve.tensor_scalar(s(S_LRE), are, A_RE_MAX, None, ALU.min).then_inc(small_v, 1)
            dve.wait_ge(small_v, 1)
            dve.wait_ge(small_a, 1)
            link(dve.tensor_tensor(s(S_LST), s(S_LRE), s(S_STEP), ALU.mult))
            link(dve.tensor_tensor(s(S_TH), aim, s(S_STEP), ALU.mult))
            link(dve.tensor_scalar(s(S_N), s(S_TH), 1.0 / TWO_PI, ROUND_MAGIC, ALU.mult, ALU.add))
            link(dve.tensor_scalar(s(S_N), s(S_N), ROUND_MAGIC, None, ALU.subtract))
            for c in (CW1, CW2, CW3):
                link(dve.scalar_tensor_tensor(s(S_TH), s(S_N), -c, s(S_TH), ALU.mult, ALU.add))
            dve.tensor_scalar(s(S_TH), s(S_TH), PI_BELOW, -PI_BELOW, ALU.min, ALU.max)\
               .then_inc(small_v, 1)
            tt(S_T1, S_LRE, S_LRE, ALU.mult)
            link(dve.tensor_tensor(s(S_T2), aim, aim, ALU.mult))
            tt(S_DEN, S_T1, S_T2, ALU.add)
            link(dve.reciprocal(s(S_DEN), s(S_DEN)))
            link(dve.tensor_tensor(skip_i[:], ident[0:GH, 0:GH].unsqueeze(1)
                                   .broadcast_to([GH, GROUPS, GH]),
                                   colc[0:GH, ROW_SKIP:ROW_SKIP + GROUPS].unsqueeze(2)
                                   .broadcast_to([GH, GROUPS, GH]), ALU.mult))
            dve.wait_ge(small_a, 2)
            tt(S_T1, S_SINH, S_SINH, ALU.mult)
            link(dve.tensor_scalar(s(S_COS), s(S_T1), -2.0, 1.0, ALU.mult, ALU.add))
            dve.wait_ge(masks_set, 2)
            link(dve.tensor_tensor(pw[:, 0, 1, :], s(S_MAG), s(S_COS), ALU.mult))
            link(dve.tensor_tensor(pw[:, 1, 1, :], s(S_MAG), s(S_SIN), ALU.mult))
            link(dve.tensor_scalar(s(S_NR), pw[:, 0, 1, :], 1.0, None, ALU.subtract))
            tt(S_T1, S_NR, S_LRE, ALU.mult)
            link(dve.tensor_tensor(s(S_T2), pw[:, 1, 1, :], aim, ALU.mult))
            tt(S_FR, S_T1, S_T2, ALU.add)
            link(dve.tensor_tensor(s(S_T1), pw[:, 1, 1, :], s(S_LRE), ALU.mult))
            link(dve.tensor_tensor(s(S_T2), s(S_NR), aim, ALU.mult))
            tt(S_FI, S_T1, S_T2, ALU.subtract)
            tt(S_FR, S_FR, S_DEN, ALU.mult)
            dve.tensor_tensor(s(S_FI), s(S_FI), s(S_DEN), ALU.mult).then_inc(small_v, 1)

            def norm(i):
                is_k, tile, _ = norm_of(i)
                w = HL if is_k else HLL
                dst = (kT if is_k else qT)[:, tile, 0:2 * w]
                g = cols[:, (COL_KG if is_k else COL_QG):][:, 0:1]
                dve.wait_ge(ss_ps, i + 1)
                dve.tensor_scalar(halves(tb[:, 0:2 * w], w), psum2(4, w), 1.0 / DH, EPS, ALU.mult,
                                  ALU.add).then_inc(ss_v, 1)
                dve.wait_ge(rs_a, i + 1)
                link(newton(ta[:, 0:2 * w], tb[:, 0:2 * w], sq[i][:, 0:2 * w],
                            1.0 if is_k else DH ** -0.5))
                dve.scalar_tensor_tensor(dst, dst, g, ta[:, 0:2 * w], ALU.mult, ALU.mult)\
                   .then_inc(normed, 1)

            def prep(r):
                dve.wait_ge(k_ps, r + 1)
                if r:
                    dve.wait_ge(kern_out[r - 1], 16 * T8)
                link(dve.tensor_copy(kern[:].rearrange("h (g b) c -> h b g c", b=2),
                                     ps[0:GH, 6:8, :].rearrange("h b (g c) -> h b g c", c=P)))
                dve.tensor_tensor(kern[:, :, 0:GH], kern[:, :, 0:GH],
                                  skip_i[:, 2 * RP * r:2 * RP * (r + 1), :], ALU.add)\
                   .then_inc(kern_set, 1)

            def state(r):
                pr = slice(r * RP, (r + 1) * RP)
                cos, sin = rot[:, 0, pr, :], rot[:, 1, pr, :]
                re, im = (ps[:, 4 + c, 0:RP * NC].rearrange("p (r c) -> p r c", c=NC)
                          for c in range(2))
                m = [mod[:, i] for i in range(4)]
                flat = [x_.rearrange("p r c -> p (r c)") for x_ in m]
                dve.wait_ge(st_ps, r + 1)
                if r == 0:
                    dve.wait_ge(rot_set, 1)
                dve.tensor_tensor(m[0], re, cos, ALU.mult)
                dve.tensor_tensor(m[1], im, sin, ALU.mult)
                dve.tensor_tensor(m[2], im, cos, ALU.mult)
                link(dve.tensor_tensor(m[3], re, sin, ALU.mult))
                dve.tensor_tensor(m[0], m[0], m[1], ALU.add)
                link(dve.tensor_tensor(m[2], m[2], m[3], ALU.subtract))
                dec = decay[:, pr, :].rearrange("p r c -> p (r c)")
                dve.tensor_tensor_scan(flat[1], dec, flat[0], 0.0, ALU.mult, ALU.add)
                link(dve.tensor_tensor_scan(flat[3], dec, flat[2], 0.0, ALU.mult, ALU.add))
                dve.tensor_tensor(m[0], m[1], cos, ALU.mult)
                link(dve.tensor_tensor(m[2], m[3], sin, ALU.mult))
                if r:
                    dve.wait_ge(y_ps, r)

                def forward(c, op):
                    for g in range(2):
                        part = slice(ST * g, ST * g + ST)
                        ins = dve.tensor_tensor(xst[part, c, g, :, 1:NC], m[0][part, :, 0:NC - 1],
                                                m[2][part, :, 0:NC - 1], op)
                    return ins

                link(forward(0, ALU.subtract))
                dve.tensor_tensor(m[0], m[3], cos, ALU.mult)
                link(dve.tensor_tensor(m[2], m[1], sin, ALU.mult))
                forward(1, ALU.add).then_inc(st_set, 1)

            def readout(r):
                y = psum2(6, HL)
                dve.wait_ge(y_sq, 2 * r + 1)
                link(dve.tensor_scalar(ta, ta, GELU_A * GELU_B, GELU_A, ALU.mult, ALU.add))
                link(dve.tensor_tensor(halves(ta, HL), halves(ta, HL), y, ALU.mult))
                dve.tensor_scalar(ta, ta, -80.0, None, ALU.max).then_inc(y_arg, 1)
                dve.wait_ge(y_sq, 2 * r + 2)
                link(dve.tensor_scalar(ta, ta, 1.0, None, ALU.add))
                link(dve.reciprocal(ta, ta))
                if r:
                    dve.wait_ge(y_out[r - 1], 16 * T8)
                dve.tensor_tensor(yg[:].rearrange("p (b g) c -> p b (g c)", b=2), halves(ta, HL), y,
                                  ALU.mult).then_inc(yg_set, 1)

            def scores(h):
                dve.wait_ge(z_ln, h + 1)
                if h:
                    dve.wait_ge(suf_ps, h)
                for b in range(4):
                    o = slice(BANK_OFF[b], BANK_OFF[b] + BANK_COLS[b])
                    ins = dve.scalar_tensor_tensor(soft[:, o], ps[:, 4 + b, 0:BANK_COLS[b]], 0.0,
                                                   prob[:, o], ALU.max, ALU.add)
                ins.then_inc(soft_set, 1)

            def values(h):
                dve.wait_ge(ath_set, h + 1)
                part = slice(DH * (h % 2), DH * (h % 2) + DH)
                for b, a, e in ((4, 0, Q_SPLIT - LATE0), (5, Q_SPLIT - LATE0, LL)):
                    ins = dve.tensor_tensor(attl[part, h // 2, a:e], ps[part, b, 0:e - a],
                                            atth[part, h // 2, a:e].bitcast(F32), ALU.subtract)
                ins.then_inc(atl_set, 1)

            def token_order(ap):
                return ap.rearrange("p j c -> p c j")

            def by_chunk(ap):
                return ap.rearrange("p (c j) -> p c j", j=T8)

            def gelu(i):
                for r in (2 * i, 2 * i + 1):
                    dve.wait_ge(gh_set, r + 1)
                    dve.tensor_tensor(by_chunk(gl[:, r]), token_order(yT[:, r]),
                                      by_chunk(gh[:, r]).bitcast(F32), ALU.subtract)\
                       .then_inc(gl_set, 1)

            def glu(unit):
                tiles = [2 * (unit - U_GLU) + mm for mm in range(2)]
                for mm, m in enumerate(tiles):
                    dve.wait_ge(glu_exp, m + 1)
                    link(dve.tensor_scalar(gt[mm][:], gt[mm][:], 1.0, None, ALU.add))
                    link(dve.reciprocal(gt[mm][:], gt[mm][:]))
                    dve.tensor_tensor(by_chunk(gt[mm][:]), by_chunk(gt[mm][:]),
                                      token_order(yT[:, m]), ALU.mult).then_inc(glu_val, 1)
                for mm, m in enumerate(tiles):
                    dve.wait_ge(sh_set, m + 1)
                    dve.tensor_tensor(sl[:, m], gt[mm][:], sh[:, m].bitcast(F32), ALU.subtract)\
                       .then_inc(sl_set, 1)

            def open_gate(i):
                dve.wait_ge(gate_one, i + 1)
                dve.reciprocal(gate[i], gate[i]).then_inc(gate_set, 1)

            steps = {"norm": norm, "prep": prep, "state": state, "readout": readout,
                     "scores": scores, "values": values, "gelu": gelu}

            def tiles_of(unit):
                return 6 if U_PROJ <= unit < U_WO else KD

            for unit in range(U_PROJ):
                split(unit + 2, unit % 2, tiles_of(unit + 2))
                if is_gate(unit) and gate_of(unit):
                    open_gate(gate_of(unit) - 1)
                if U_GLU <= unit < U_GATE2:
                    glu(unit)
                for name, i in STEPS.get(unit, []):
                    if name in steps:
                        steps[name](i)
            open_gate(2 * KD - 1)

            def mixed_lo(m):
                dve.wait_ge(mh_set, m + 1)
                dve.tensor_tensor(ml[:, m], ma[m % 2][:], mh[:, m].bitcast(F32), ALU.subtract)\
                   .then_inc(ml_set, 1)

            dve.wait_ge(gate_set, 2 * KD)
            for m in range(KD):
                unit = U_PROJ + m
                split(unit + 2, unit % 2, tiles_of(unit + 2))
                dve.wait_ge(unit_done, unit + 1)
                if m >= 2:
                    dve.wait_ge(m_sum, m - 1)
                    dve.wait_ge(ml_set, m - 1)
                b = 4 * (m % 2)
                dve.tensor_tensor(halves(ma[m % 2][:], HLL), psum2(b, HLL), halves(gate[m], HLL),
                                  ALU.mult)
                dve.tensor_tensor(halves(mb[m % 2][:], HLL), psum2(b + 2, HLL),
                                  halves(gate[KD + m], HLL), ALU.mult).then_inc(m_gated, 1)
                if m:
                    mixed_lo(m - 1)
            mixed_lo(KD - 1)

            def z_lo(m):
                dve.wait_ge(zh_set, m + 1)
                dve.scalar_tensor_tensor(xl[:, m, 0:LL], hT[:, m, LATE0:L],
                                         cols[:, COL_N2 + m:COL_N2 + m + 1],
                                         xh[:, m, 0:LL].bitcast(F32), ALU.mult, ALU.subtract)\
                   .then_inc(z_ready, 1)

            for m in range(KD):
                unit = U_WO + m
                split(unit + 2, unit % 2, KD)
                dve.wait_ge(unit_done, unit + 1)
                dve.tensor_tensor(halves(hT[:, m, LATE0:L], HLL), psum2(2 * (m % 2), HLL),
                                  halves(hT[:, m, LATE0:L], HLL), ALU.add).then_inc(h_set, 1)
                if m:
                    z_lo(m - 1)
            z_lo(KD - 1)
            dve.wait_ge(ss2_ps, 1)
            dve.tensor_scalar(halves(nv[:], HLL), psum2(4, HLL), 1.0 / D, EPS, ALU.mult, ALU.add)\
               .then_inc(ss2_v, 1)
            dve.wait_ge(r2_a, 1)
            newton(rb[:, 0:LL], nv[:], sqh[0][:]).then_inc(r2_set, 1)
            dve.wait_ge(r2_set, 1)

            def product_lo(f, s_):
                dve.wait_ge(ah_set, f + 1)
                at = bass.ds(f, 1)
                dve.tensor_tensor(al[:, at, :].rearrange("p a c -> p (a c)"), cv[s_][:, 1],
                                  ah[:, at, :].bitcast(F32).rearrange("p a c -> p (a c)"),
                                  ALU.subtract).then_inc(al_set, 1)

            def up(f, s_, tiles=KD):
                for part in range(2):
                    split(f * 2 + (U_UP + 2 + part), part, tiles)
                    dve.wait_ge(unit_done, f * 2 + (U_UP + 1 + part))
                    if part == 0 and not (isinstance(f, int) and f < 2):
                        dve.wait_ge(cv_v, f * 2 - 2)
                    dve.tensor_tensor(halves(ut[s_][:, part], HLL), psum2(4 * s_ + 2 * part, HLL),
                                      halves(rb[:, 0:LL], HLL), ALU.mult).then_inc(up_v, 1)
                if not (isinstance(f, int) and f < 1):
                    product_lo(f - 1, 1 - s_)
                for tap in (1, 2):
                    for part in range(2):
                        if tap == 1:
                            dve.wait_ge(cv_a, f * 2 + (part + 1))
                        else:
                            dve.wait_ge(cv_mid, f * 2 + (part + 1))
                        w = cols[:, bass.ds(f + (COL_CW + (2 * tap + part) * KF), 1)]
                        dve.scalar_tensor_tensor(cv[s_][:, part],
                                                 ut[s_][:, part, 2 + tap:2 + tap + SEQ], w,
                                                 cv[s_][:, part], ALU.mult, ALU.add)\
                           .then_inc(cv_mid if tap == 1 else cv_v, 1)

            up(0, 0)
            up(1, 1)
            with dve.Fori(1, KF // 2 - 1) as ff:
                for s_ in range(2):
                    up(ff * 2 + s_, s_)
            up(KF - 2, 0)
            up(KF - 1, 1, UT)
            product_lo(KF - 1, 1)

            def down(m, s_):
                for half in range(2):
                    if not isinstance(m, int) or m < KD - 1:
                        split(m * 2 + (U_DOWN + 2 + half), half, UT)
                dve.wait_ge(unit_done, m * 2 + (U_DOWN + 2))
                if not (isinstance(m, int) and m < 2):
                    dve.wait_ge(yt_ps, m - 1)
                dve.tensor_tensor(yo[s_][:], ps[:, s_, :],
                                  hT[:, bass.ds(m, 1), META:L].rearrange("p a c -> p (a c)"),
                                  ALU.add).then_inc(y_add, 1)

            down(0, 0)
            down(1, 1)
            with dve.Fori(1, KD // 2 - 1) as mm:
                for s_ in range(2):
                    down(mm * 2 + s_, s_)
            for s_ in range(2):
                down(KD - 2 + s_, s_)

        @block.tensor
        def _(pe):
            def three(outs, weights, acts, start, stop):
                for i, (w, a) in enumerate(((0, 0), (0, 1), (1, 0))):
                    for c, o in enumerate(outs):
                        ins = pe.matmul(o, weights[w], acts(a, c), start=start and i == 0,
                                        stop=stop and i == 2)
                return ins

            def wtile(slot, i, n=1):
                return [w[slot][:, i * P:(i + n) * P] for w in (hi, lo)]

            def product(slot, tile0, count, bank, width, pair, col0, ready=None, first=0,
                        stride=1, total=None):
                total = count if total is None else total
                for k in range(count):
                    if ready is not None:
                        pe.wait_ge(ready, first + k + 1)
                    ins = three([ps[:, bank + c, 0:width] for c in range(2)],
                                wtile(slot, tile0 + k * stride),
                                lambda a, c: pair[a][:, first + k, col0 + c * width:
                                                     col0 + (c + 1) * width],
                                k == 0, k == count - 1)
                return ins

            pe.wait_ge(masks_set, 1)
            pe.wait_ge(stack_full, 1)
            pe.wait_ge(stk_in, 64)
            pe.wait_ge(par_in, 160)
            pe.transpose(ps[:, 0, 0:P], stack[:, 0, :], ident[:])
            pe.transpose(ps[:, 0, P:2 * P], stack[:, 1, :], ident[:])
            n2 = NCOLS - P
            pe.transpose(ps[:, 0, 2 * P:2 * P + n2], stack[0:n2, 2, :], ident[0:n2, 0:n2])\
              .then_inc(cols_t, 1)
            pe.wait_ge(bc_in, 16 * BC_DMAS)
            for c in range(2):
                for t in range(4):
                    ins = pe.transpose(ps[:, 1 + c, t * P:(t + 1) * P],
                                       cdup[:, c, t].rearrange("p d s -> p (d s)"), ident[:])
            ins.then_inc(cols_t, 1)
            pe.wait_ge(rx_ready, 2)
            rows = slice(0, TT_ROWS)
            diag = vt[rows].rearrange("p a b -> p (a b)")
            for c in range(2):
                ins = pe.matmul(ps[:, 6 + c, 0:HL], ones[rows, :], diag[:, c * HL:(c + 1) * HL],
                                start=True, stop=True)
            ins.then_inc(rb_ps, 1)
            for k in range(KD):
                if k == 1:
                    pe.wait_ge(rb_set, 1)
                if k >= 2:
                    pe.wait_ge(xt_copied, k - 1)
                b = 4 + 2 * (k % 2)
                for i in range(NTT):
                    c0 = (i % 3) * TT_ROWS
                    ins = pe.transpose(ps[:, b + i // 3, c0:c0 + TT_ROWS],
                                       xtok[rows, i, k * P:(k + 1) * P], ident[rows, rows])
                ins.then_inc(xt_ps, 1)

            def norm(i):
                is_k, t, unit = norm_of(i)
                w = HL if is_k else HLL
                pe.wait_ge(sq_ready, i + 1)
                for c in range(2):
                    ins = pe.matmul(ps[:, 4 + c, 0:w], blocks[:], sq[i][:, c * w:(c + 1) * w],
                                    start=True, stop=True)
                ins.then_inc(ss_ps, 1)

            def prep(r):
                pe.wait_ge(g_ready, r + 1)
                for c in range(2):
                    for i in range(RP):
                        ins = pe.transpose(ps[:, 4 + c, i * P:(i + 1) * P],
                                           g_in[:, c, i].rearrange("p j h -> p (j h)"), ident[:])
                ins.then_inc(g_t, 1)
                pe.wait_ge(h_ready, r + 1)
                for g in range(2 * RP):
                    part = slice(ST * (g % 2), ST * (g % 2) + ST)
                    o = ps[0:GH, 6 + g % 2, (g // 2) * P:(g // 2 + 1) * P]
                    for c in range(2):
                        ins = pe.matmul(o, bb[part, c, r * RP + g // 2, :],
                                        hout[part, c, g // 2, 0:T8, :]
                                        .rearrange("p i h -> p (i h)"),
                                        start=c == 0, stop=c == 1)
                ins.then_inc(k_ps, 1)

            def state(r):
                pe.wait_ge(win_set, r + 1)
                pe.wait_ge(u_in[r], 16 * T8)
                for g in range(2 * RP):
                    part = slice(ST * (g % 2), ST * (g % 2) + ST)
                    for c in range(2):
                        w0 = (g // 2) * P + ST * (g % 2)
                        ins = pe.matmul(ps[part, 4 + c, (g // 2) * NC:(g // 2 + 1) * NC],
                                        win[:, c, w0:w0 + ST], uc[:, r % 2, g, :],
                                        start=True, stop=True)
                ins.then_inc(st_ps, 1)

            def readout(r):
                pe.wait_ge(kern_out[r], 16 * T8)
                pe.wait_ge(st_set, r + 1)
                pe.wait_ge(kern_set, r + 1)
                if r:
                    pe.wait_ge(yg_set, r)
                for g in range(2 * RP):
                    o = ps[:, 6 + g // 4, (g % 4) * NC:(g % 4 + 1) * NC]
                    pe.matmul(o, toep[:, g, :], uc[:, r % 2, g, :], start=True, stop=False)
                    for c in range(2):
                        ins = pe.matmul(o, hout[:, c, g // 2, 1:T8 + 1, :]
                                        .rearrange("p i h -> p (i h)"),
                                        xst[:, c, g % 2, g // 2, :], start=False, stop=c == 1)
                ins.then_inc(y_ps, 1)

            def scores(h):
                pe.wait_ge(qz_set, h + 1)
                for bank in range(4):
                    mine = [g for g in REGIONS if g[0] == bank]
                    for n, (_, c0, kb, q0, q1) in enumerate(mine):
                        pe.matmul(ps[:, 4 + bank, c0:c0 + q1 - q0],
                                  kT[:, h // 2, KEY0[kb]:KEY0[kb] + P],
                                  qz[h % 2][:, q0 - LATE0:q1 - LATE0],
                                  start=n == 0, stop=False, skip_group_check=True)
                        if kb == 4:
                            ins = pe.matmul(ps[:, 4 + bank, c0:c0 + META], ident_bf[:],
                                            mask_last[:], start=False, stop=True,
                                            skip_group_check=True)
                        elif q0 < KEY0[kb] + P:
                            n_ = KEY0[kb] + P - q0
                            ins = pe.matmul(ps[:, 4 + bank, c0:c0 + n_], ident_bf[:],
                                            mask[:, P - n_:P], start=False, stop=True,
                                            skip_group_check=True)
                ins.then_inc(z_ps, 1)

            def soft_cols(region, q0, q1):
                a = BANK_OFF[region[0]] + region[1] + q0 - region[3]
                return soft[:, a:a + q1 - q0]

            def suffix(h):
                pe.wait_ge(soft_set, h + 1)
                for g in REGIONS:
                    ins = pe.matmul(ps[:, 4 + g[0], g[1]:g[1] + g[4] - g[3]], negtri[:],
                                    soft_cols(g, g[3], g[4]), start=False, stop=True,
                                    skip_group_check=True)
                    for later in REGIONS:
                        q0, q1 = shared_queries(g, later)
                        if later[2] > g[2] and q0 < q1:
                            o = g[1] + q0 - g[3]
                            ins = pe.matmul(ps[:, 4 + g[0], o:o + q1 - q0], negones[:],
                                            soft_cols(later, q0, q1), start=False, stop=True,
                                            skip_group_check=True)
                ins.then_inc(suf_ps, 1)

            def values(h):
                pe.wait_ge(prob_set, h + 1)
                part = slice(DH * (h % 2), DH * (h % 2) + DH)
                for low, bank, origin in ((True, 4, LATE0), (False, 5, Q_SPLIT)):
                    mine = [g for g in REGIONS if (g[4] == Q_SPLIT) == low]
                    for n, g in enumerate(mine):
                        a = BANK_OFF[g[0]] + g[1]
                        ins = pe.matmul(ps[part, bank, g[3] - origin:g[4] - origin],
                                        vt[:, g[2], h * DH:(h + 1) * DH],
                                        prob[:, a:a + g[4] - g[3]], start=n == 0,
                                        stop=n == len(mine) - 1, skip_group_check=True)
                ins.then_inc(av_ps, 1)

            steps = {"norm": norm, "prep": prep, "state": state, "readout": readout,
                     "scores": scores, "suffix": suffix, "values": values}
            taken = {"norm": (45, ss_v), "prep": (4567, win_set, kern_set), "state": (45, st_set),
                     "readout": (67, yg_set), "values": (4567, atl_set)}
            used45 = [(xt_copied, KD)]
            used67 = [(xt_copied, KD)]

            def run(name, i):
                if name in ("norm", "prep", "state", "scores"):
                    for s_, n in used45:
                        pe.wait_ge(s_, n)
                if name in ("prep", "readout", "scores"):
                    for s_, n in used67:
                        pe.wait_ge(s_, n)
                steps[name](i)
                if name == "norm":
                    used45[:] = [(ss_v, i + 1)]
                if name == "prep":
                    used45[:] = [(win_set, i + 1)]
                    used67[:] = [(kern_set, i + 1)]
                if name == "state":
                    used45[:] = [(st_set, i + 1)]
                if name == "readout":
                    used67[:] = [(yg_set, i + 1)]
                if name == "values":
                    used45[:] = [(atl_set, i + 1)]
                    used67[:] = []

            def left(unit):
                if unit < U_GATE:
                    return drained, unit + 1
                if is_gate(unit):
                    return gate_exp, gate_of(unit) + 1
                return glu_exp, 2 * (unit - U_GLU) + 2

            for unit in range(U_PROJ):
                slot = unit % 2
                glu = U_GLU <= unit < U_GATE2
                pe.wait_ge(lo_ready, unit + 1)
                if unit == 0:
                    pe.wait_ge(cols_set, 1)
                    pe.wait_ge(ct_set, 1)
                if unit >= 2:
                    pe.wait_ge(*left(unit - 2))
                if glu or U_GLU < unit <= U_GATE2:
                    pe.wait_ge(*left(unit - 1))
                bank = 2 * slot
                x_pair = (xh, xl)
                if glu:
                    pe.wait_ge(gl_set, KS)
                    for mm in range(2):
                        ins = product(slot, mm, KS, 2 * mm, HL, (gh, gl), 0, stride=2)
                elif U_V <= unit < U_Q:
                    for kb in range(5):
                        o = ps[:, bank + kb // 4, (kb % 4) * P:(kb % 4 + 1) * P]
                        for k in range(KD):
                            tok = slice(KEY0[kb], KEY0[kb] + P)
                            w = wtile(slot, k)
                            ins = three([o], [xh[:, k, tok], xl[:, k, tok]],
                                        lambda a, c: w[a], k == 0, k == KD - 1)
                else:
                    ready = x_ready if unit == 0 else None
                    width, col0 = (HL, 0) if unit < U_V else (HLL, LATE0)
                    ins = product(slot, 0, KD, bank, width, x_pair, col0, ready=ready)
                ins.then_inc(unit_done, 1)
                for name, i in STEPS.get(unit, []):
                    if name in steps:
                        run(name, i)

            pe.wait_ge(*left(U_PROJ - 2))
            pe.wait_ge(*left(U_PROJ - 1))
            for m in range(KD):
                unit = U_PROJ + m
                b = 4 * (m % 2)
                pe.wait_ge(lo_ready, unit + 1)
                if m == 0:
                    pe.wait_ge(atl_set, HEADS)
                if m == 1:
                    pe.wait_ge(atl_set, HEADS)
                if m >= 2:
                    pe.wait_ge(m_gated, m - 1)
                product(unit % 2, 0, 2, b, HLL, (atth, attl), 0)
                if m == 0:
                    pe.wait_ge(sl_set, KS)
                product(unit % 2, 2, KS, b + 2, HLL, (sh, sl), LATE0).then_inc(unit_done, 1)
            for m in range(KD):
                unit = U_WO + m
                pe.wait_ge(lo_ready, unit + 1)
                if m < 2:
                    pe.wait_ge(m_gated, KD - 1)
                else:
                    pe.wait_ge(h_set, m - 1)
                product(unit % 2, 0, KD, 2 * (m % 2), HLL, (mh, ml), 0,
                        ready=ml_set if m == 0 else None).then_inc(unit_done, 1)

            def up_unit(f, s, part, ready=None):
                pe.wait_ge(lo_ready, f * 2 + (U_UP + 1 + part))
                if not (isinstance(f, int) and f < 2):
                    pe.wait_ge(up_v, f * 2 + (part - 3))
                product(part, 0, KD, 4 * s + 2 * part, HLL, (xh, xl), 0, ready=ready)\
                    .then_inc(unit_done, 1)

            pe.wait_ge(h_set, KD)
            pe.wait_ge(m_gated, KD)
            up_unit(0, 0, 0, ready=z_ready)
            pe.wait_ge(h_acc, KD)
            for c in range(2):
                ins = pe.matmul(ps[:, 4 + c, 0:HLL], ones[:], acc[:, c * HLL:(c + 1) * HLL],
                                start=True, stop=True)
            ins.then_inc(ss2_ps, 1)
            up_unit(0, 0, 1)
            pe.wait_ge(ss2_v, 1)
            up_unit(1, 1, 0)
            up_unit(1, 1, 1)
            with pe.Fori(1, KF // 2) as ff:
                for s in range(2):
                    for part in range(2):
                        up_unit(ff * 2 + s, s, part)

            def turn(m, s):
                pe.wait_ge(y_add, m + 1)
                if not (isinstance(m, int) and m < 2):
                    pe.wait_ge(yt_set, m - 1)
                for t in range(4):
                    ins = pe.transpose(ps[:, 4 + s, t * P:(t + 1) * P], yo[s][:, t * P:(t + 1) * P],
                                       ident[:])
                ins.then_inc(yt_ps, 1)

            def down(m, s):
                if isinstance(m, int) and m < 2:
                    pe.wait_ge(up_v, 2 * KF)
                else:
                    pe.wait_ge(y_add, m - 1)
                for half in range(2):
                    pe.wait_ge(lo_ready, m * 2 + (U_DOWN + 1 + half))
                    for i in range(UT):
                        k = half * UT + i
                        if isinstance(m, int) and m == 0:
                            pe.wait_ge(al_set, k + 1)
                        ins = three([ps[:, s, :]], wtile(half, i),
                                    lambda a, c: (ah, al)[a][:, k, :], k == 0, k == KF - 1)
                    ins.then_inc(unit_done, 1)
                    if half == 0 and not (isinstance(m, int) and m == 0):
                        turn(m - 1, 1 - s)

            down(0, 0)
            down(1, 1)
            with pe.Fori(1, KD // 2) as mm:
                for s in range(2):
                    down(mm * 2 + s, s)
            turn(KD - 1, 1)


_INS = ["x", "meta_tokens", "norm1_g", "w_in", "q_norm_g", "k_norm_g", "ssm_a_re", "ssm_a_im",
        "ssm_log_step", "ssm_b_re", "ssm_b_im", "ssm_c_re", "ssm_c_im", "ssm_d", "w_glu", "b_glu",
        "w_attn_proj", "w_ssm_proj", "w_o", "norm2_g", "w_up", "conv_w", "conv_b", "w_down"]


def kernel(**inputs):
    import numpy as _np
    import concourse.bacc as _bacc
    from concourse import mybir as _mybir
    from concourse.bass_utils import run_bass_kernel_spmd as _run

    nc = _bacc.Bacc("TRN2", target_bir_lowering=False, num_devices=1)
    arrays, args = {}, []
    for name in _INS:
        a = _np.ascontiguousarray(inputs[name])
        arrays[f"in_{name}_dram"] = a
        args.append(nc.dram_tensor(f"in_{name}_dram", a.shape, _mybir.dt.from_np(a.dtype),
                                   kind="ExternalInput").ap())
    args.append(nc.dram_tensor("out_0_dram", (1, SEQ, D), F32, kind="ExternalOutput").ap())
    hybrid_trunk(nc, *args)
    return _run(nc, [arrays], core_ids=[0]).results[0]["out_0_dram"]
```

```python
from contextlib import ExitStack

import concourse.bass as bass
from concourse import mybir

F32 = mybir.dt.float32
F32R = mybir.dt.float32r
BF16 = mybir.dt.bfloat16
ALU = mybir.AluOpType
ACT = mybir.ActivationFunctionType

P = 128
D = 1024
SEQ = 512
META = 16
L = META + SEQ
LATE0 = 12
LL = L - LATE0
HL, HLL = L // 2, LL // 2
KD = D // P
HEADS, DH = 4, 64
SBW = HEADS * DH
SW = 512
GROUPS, GH, ST = 32, 16, 64
KS = SW // P
PAIRS = GROUPS // 2
FFN = 2816
KF = FFN // P
EPS = 1e-6
TT_ROWS = 88
NTT = L // TT_ROWS
T8 = 8
NC = L // T8
RP = PAIRS // 4
ROUNDS = 4
UT = 11
NEG = -1e30
TWO_PI = 6.283185307179586
CW1 = 6.28125
CW2 = 0.0019350051879882812
CW3 = 3.019916050773725e-07
ROUND_MAGIC = 12582912.0
PI_BELOW = 3.1415925
A_RE_MAX = -1e-4
BC_DMAS = 6
Q_LAST = 512

(S_STEP, S_MAG, S_SIN, S_SINH, S_COS, S_TH, S_LST, S_LRE, S_N, S_FR, S_FI, S_D2, S_D4, S_DEN, S_NR,
 S_T1, S_T2) = range(17)

U_SSM, U_K, U_V, U_Q, U_GATE, U_GLU, U_PROJ, U_WO, U_UP, U_DOWN, U_END = \
    0, 4, 6, 8, 10, 26, 28, 36, 44, 88, 104

KEY0 = (0, 128, 256, 384, 400)
REGIONS = ((0, 0, 0, 12, 256), (0, 244, 1, 128, 256),
           (1, 0, 0, 256, 528), (2, 0, 1, 256, 528),
           (3, 0, 2, 256, 528), (3, 272, 3, 384, 528), (3, 416, 4, 512, 528))
BANK_COLS = (372, 272, 272, 432)
BANK_OFF = (0, 372, 644, 916)
ATT_COLS = 1348
HALVES = (slice(0, BANK_OFF[2]), slice(BANK_OFF[2], ATT_COLS))
Q_SPLIT = 256

STEPS = {4: [("norm", 0)], 5: [("prep", 0), ("norm", 1)], 6: [("turn_v", 0)],
         7: [("turn_v", 1), ("state", 0)],
         8: [("readout", 0), ("norm", 2)], 9: [("prep", 1), ("norm", 3)],
         10: [("state", 1)], 11: [("readout", 1)], 12: [("prep", 2)],
         13: [("state", 2)], 14: [("readout", 2)], 15: [("prep", 3)],
         16: [("state", 3)], 17: [("readout", 3)],
         18: [("scores", 0)], 19: [("suffix", 0)], 20: [("values", 0), ("scores", 1)],
         21: [("suffix", 1)], 22: [("values", 1), ("scores", 2), ("gelu", 0)],
         23: [("suffix", 2), ("gelu", 1)], 24: [("values", 2), ("scores", 3)],
         25: [("suffix", 3)], 26: [("values", 3)]}
MOVES = {2: [("u_write", 0)], 3: [("u_write", 1)], 4: [("u_write", 2), ("u_read", 0)],
         5: [("u_write", 3), ("u_read", 1)], 7: [("toep", 0)], 9: [("u_read", 2)],
         10: [("y_write", 0)], 11: [("toep", 1)], 12: [("u_read", 3)], 13: [("y_write", 1)],
         14: [("toep", 2)], 16: [("y_write", 2)], 17: [("toep", 3)], 19: [("y_write", 3)],
         20: [("y_read", 0)]}

ROW_ARE, ROW_AIM, ROW_STEP, ROW_SKIP = 0, 32, 64, 96
COL_CW, COL_CB, COL_N1, COL_N2, COL_BG, COL_QG, COL_KG, NCOLS = 0, 132, 176, 184, 192, 196, 197, 198


def norm_of(i):
    return (True, i, U_K + i) if i < 2 else (False, i - 2, U_Q + i - 2)


def gate_of(unit):
    return unit - U_GATE


def is_gate(unit):
    return U_GATE <= unit < U_GLU


def bank_cols(b):
    return slice(BANK_OFF[b], BANK_OFF[b] + BANK_COLS[b])


def shared_queries(region, other):
    return max(region[3], other[3]), min(region[4], other[4])


def hybrid_trunk(nc, x, meta_tokens, norm1_g, w_in, q_norm_g, k_norm_g, ssm_a_re, ssm_a_im,
                 ssm_log_step, ssm_b_re, ssm_b_im, ssm_c_re, ssm_c_im, ssm_d, w_glu, b_glu,
                 w_attn_proj, w_ssm_proj, w_o, norm2_g, w_up, conv_w, conv_b, w_down, out):
    u_dram = nc.dram_tensor("u_dram", (SW, T8, NC), F32, kind="Internal").ap()
    y_dram = nc.dram_tensor("y_dram", (SW, T8, NC), F32, kind="Internal").ap()

    ctx = ExitStack()
    with ctx:
        def alloc(stack, name, shape, dt=F32):
            return stack.enter_context(nc.sbuf_tensor(name, shape, dt))

        def sb(name, shape, dt=F32):
            return alloc(ctx, name, shape, dt)

        def sem(name):
            return ctx.enter_context(nc.semaphore(name))

        ps = ctx.enter_context(nc.psum_tensor("ps", [P, 8, 512], F32))

        raw = [sb(f"raw{i}", [P, UT * P]) for i in range(2)]
        hi = [sb(f"hi{i}", [P, UT * P], F32R) for i in range(2)]
        lo = [sb(f"lo{i}", [P, UT * P], F32R) for i in range(2)]
        xh = sb("xh", [P, KD, L], F32R)
        xl = sb("xl", [P, KD, L], F32R)
        hT = sb("hT", [P, KD, L])
        ident = sb("ident", [P, P])
        ones = sb("ones", [P, P])
        cols = sb("cols", [P, NCOLS])
        rb = sb("rb", [P, L])

        start = ExitStack()
        xtok = alloc(start, "xtok", [P, NTT, D])
        stack = alloc(start, "stack", [P, 3, P])
        cdup = alloc(start, "cdup", [P, 2, 4, 2, ST])
        start.close()

        mix = ExitStack()
        gates = alloc(mix, "gates", [P, 16 * LL])
        sq = [gates[:, 5088 + i * L:5088 + (i + 1) * L] for i in range(4)]
        ta = gates[:, 16 * LL - 2 * L:16 * LL - L]
        tb = gates[:, 16 * LL - L:16 * LL]
        vT = [gates[:, i * L:(i + 1) * L] for i in range(2)]
        gate = [gates[:, i * LL:(i + 1) * LL] for i in range(16)]
        qk = ExitStack()
        qT = alloc(qk, "qT", [P, 2, L])
        kT = alloc(qk, "kT", [P, 2, L])
        qk.close()
        ma = [alloc(mix, f"ma{i}", [P, LL]) for i in range(2)]
        mb = [alloc(mix, f"mb{i}", [P, LL]) for i in range(2)]
        pad = alloc(mix, "pad", [P, 4 * (L - LL)])
        vh = alloc(mix, "vh", [P, 5, SBW], F32R)
        vl = alloc(mix, "vl", [P, 5, SBW], F32R)
        atth = alloc(mix, "atth", [P, 2, LL], F32R)
        attl = alloc(mix, "attl", [P, 2, LL], F32R)
        blocks = alloc(mix, "blocks", [P, P])
        negtri = alloc(mix, "negtri", [P, P], F32R)
        negones = alloc(mix, "negones", [P, P], F32R)
        ident_bf = alloc(mix, "ident_bf", [P, P], BF16)
        mask = alloc(mix, "mask", [P, P], BF16)
        mask_last = alloc(mix, "mask_last", [P, META], BF16)
        ssx = alloc(mix, "ssx", [P, 4, NTT])

        early = ExitStack()
        turning = ExitStack()
        uy = alloc(turning, "uy", [P, 2, T8, NC])
        turning.close()
        mod = alloc(early, "mod", [P, 4, RP, NC])
        uc = alloc(early, "uc", [P, 2, 2 * RP, NC])
        given = ExitStack()
        braw = alloc(given, "braw", [P, 2, PAIRS, GH])
        given.close()
        yg = alloc(early, "yg", [P, 2 * RP, NC])
        rot = alloc(early, "rot", [P, 2, PAIRS, NC])
        decay = alloc(early, "decay", [P, PAIRS, NC])
        g_in = alloc(early, "g_in", [P, 2, RP, T8, GH])
        win = alloc(early, "win", [P, 2, RP * P])
        hout = alloc(early, "hout", [P, 2, RP, T8 + 1, GH])
        kern = alloc(early, "kern", [GH, 2 * RP, P])
        toep = alloc(early, "toep", [P, 2 * RP, P])
        xst = alloc(early, "xst", [P, 2, 2, RP, NC])
        skip_i = alloc(early, "skip_i", [GH, GROUPS, GH])
        colc = alloc(early, "colc", [P, P])
        sm = alloc(early, "sm", [P, 20, PAIRS])
        pw = alloc(early, "pw", [P, 2, T8 + 1, PAIRS])
        en = alloc(early, "en", [P, 4, 2, PAIRS])
        bb = alloc(early, "bb", [P, 2, PAIRS, GH])
        ct = alloc(early, "ct", [P, 2, PAIRS, GH])
        pt = alloc(early, "pt", [P, RP * (T8 + 1) * GH])
        lst = alloc(early, "lst", [P, 2])
        early.close()
        scr = ExitStack()
        under = ExitStack()
        yT = alloc(under, "yT", [P, KS, T8, NC])
        gh = alloc(under, "gh", [P, KS, L], F32R)
        gl = alloc(under, "gl", [P, KS, L], F32R)
        aw = alloc(under, "aw", [P, ATT_COLS])
        awh = alloc(under, "awh", [P, ATT_COLS], F32R)
        under.close()
        mh = alloc(scr, "mh", [P, KD, LL], F32R)
        ml = alloc(scr, "ml", [P, KD, LL], F32R)
        pad2 = alloc(scr, "pad2", [P, 3 * KS * L + 2 * ATT_COLS - 2 * KD * LL + 16])
        heads = ExitStack()
        awl = alloc(heads, "awl", [P, ATT_COLS], F32R)
        qzl = [alloc(heads, f"qzl{i}", [P, LL], F32R) for i in range(2)]
        kh = alloc(heads, "kh", [P, L], F32R)
        kl = alloc(heads, "kl", [P, L], F32R)
        heads.close()
        sh = alloc(scr, "sh", [P, KS, L], F32R)
        sl = alloc(scr, "sl", [P, KS, L], F32R)
        gt = [alloc(scr, f"gt{i}", [P, L]) for i in range(2)]
        qzh = [alloc(scr, f"qzh{i}", [P, LL], F32R) for i in range(2)]
        scr.close()
        mix.close()

        late = ExitStack()
        sqh = [alloc(late, f"sqh{i}", [P, LL]) for i in range(2)]
        acc = alloc(late, "acc", [P, LL])
        nv = alloc(late, "nv", [P, LL])
        ut = [alloc(late, f"ut{i}", [P, 2, LL]) for i in range(2)]
        cv = [alloc(late, f"cv{i}", [P, 2, SEQ]) for i in range(2)]
        ah = alloc(late, "ah", [P, KF, SEQ], F32R)
        al = alloc(late, "al", [P, KF, SEQ], F32R)
        late.close()
        fin = ExitStack()
        yo = [alloc(fin, f"yo{i}", [P, SEQ]) for i in range(2)]
        yt = [alloc(fin, f"yt{i}", [P, 4, P]) for i in range(2)]
        fin.close()

        raw_in = [sem(f"raw_in{i}") for i in range(2)]
        hi_ready = sem("hi_ready")
        lo_ready = sem("lo_ready")
        unit_done = sem("unit_done")
        drained = sem("drained")
        par_in = sem("par_in")
        stk_in = sem("stk_in")
        bc_in = sem("bc_in")
        x_in = [sem(f"x_in{i}") for i in range(3)]
        masks_set = sem("masks_set")
        stack_zero = sem("stack_zero")
        stack_full = sem("stack_full")
        cols_t = sem("cols_t")
        cols_set = sem("cols_set")
        ss_x = sem("ss_x")
        rx_ready = sem("rx_ready")
        rb_ps = sem("rb_ps")
        rb_set = sem("rb_set")
        xt_ps = sem("xt_ps")
        xt_copied = sem("xt_copied")
        xn_set = sem("xn_set")
        xh_set = sem("xh_set")
        x_ready = sem("x_ready")
        small_a = sem("small_a")
        small_v = sem("small_v")
        ct_set = sem("ct_set")
        rot_set = sem("rot_set")
        g_ready = sem("g_ready")
        h_ready = sem("h_ready")
        g_t = sem("g_t")
        k_ps = sem("k_ps")
        win_set = sem("win_set")
        kern_set = sem("kern_set")
        kern_out = [sem(f"kern_out{i}") for i in range(ROUNDS)]
        u_out = [sem(f"u_out{i}") for i in range(ROUNDS)]
        u_in = [sem(f"u_in{i}") for i in range(ROUNDS)]
        y_out = [sem(f"y_out{i}") for i in range(ROUNDS)]
        y_in = sem("y_in")
        st_ps = sem("st_ps")
        st_set = sem("st_set")
        y_ps = sem("y_ps")
        yg_set = sem("yg_set")
        v_t = sem("v_t")
        vh_set = sem("vh_set")
        vl_set = sem("vl_set")
        sq_ready = sem("sq_ready")
        ss_ps = sem("ss_ps")
        ss_v = sem("ss_v")
        rs_a = sem("rs_a")
        normed = sem("normed")
        qz_zero = sem("qz_zero")
        kh_set = sem("kh_set")
        kl_set = sem("kl_set")
        qh_set = sem("qh_set")
        ql_set = sem("ql_set")
        z_ps = sem("z_ps")
        z_ln = sem("z_ln")
        soft_set = sem("soft_set")
        soft_hi = sem("soft_hi")
        soft_lo = sem("soft_lo")
        suf_ps = sem("suf_ps")
        prob_hi = sem("prob_hi")
        prob_lo = sem("prob_lo")
        av_ps = sem("av_ps")
        ath_set = sem("ath_set")
        atl_set = sem("atl_set")
        gate_raw = sem("gate_raw")
        gate_set = sem("gate_set")
        gh_set = sem("gh_set")
        gl_set = sem("gl_set")
        glu_sig = sem("glu_sig")
        glu_val = sem("glu_val")
        sh_set = sem("sh_set")
        sl_set = sem("sl_set")
        m_gated = sem("m_gated")
        m_sum = sem("m_sum")
        mh_set = sem("mh_set")
        ml_set = sem("ml_set")
        h_set = sem("h_set")
        h_sq = sem("h_sq")
        h_acc = sem("h_acc")
        zh_set = sem("zh_set")
        z_ready = sem("z_ready")
        ss2_ps = sem("ss2_ps")
        ss2_v = sem("ss2_v")
        r2_a = sem("r2_a")
        r2_set = sem("r2_set")
        up_v = sem("up_v")
        cv_a = sem("cv_a")
        cv_mid = sem("cv_mid")
        cv_v = sem("cv_v")
        silu_a = sem("silu_a")
        act_p = sem("act_p")
        ah_set = sem("ah_set")
        al_set = sem("al_set")
        y_add = sem("y_add")
        yt_ps = sem("yt_ps")
        yt_set = sem("yt_set")
        out_done = [sem(f"out_done{i}") for i in range(2)]
        act_link = sem("act_link")
        dve_link = sem("dve_link")
        pool_link = sem("pool_link")

        def psum2(bank, width, part=slice(0, P)):
            return ps[part, bank:bank + 2, 0:width]

        def halves(ap, width):
            return ap.rearrange("p (b c) -> p b c", c=width)

        def linker(eng, link):
            count = [0]

            def wait_for(ins):
                count[0] += 1
                ins.then_inc(link, 1)
                eng.wait_ge(link, count[0])
            return wait_for

        block = ctx.enter_context(nc.Block())

        @block.sync
        def _(sp):
            def in_cols(c0):
                return w_in[0].rearrange("(k p) c -> p k c", p=P)[:, :, c0:c0 + P]

            def load(slot, parts):
                at = 0
                for src in parts:
                    n = src.shape[1] * src.shape[2]
                    sp.dma_start(raw[slot][:, at:at + n].rearrange("p (k c) -> p k c", c=src.shape[2]),
                                 src).then_inc(raw_in[slot], 16)
                    at += n

            def halved(src):
                k = src.shape[1]
                return [src[:, 0:(k + 1) // 2, :], src[:, (k + 1) // 2:k, :]]

            def source(unit):
                if unit < U_K:
                    return halved(in_cols(3 * SBW + P * unit))
                if unit < U_V:
                    return halved(in_cols(SBW + P * (unit - U_K)))
                if unit < U_Q:
                    return halved(in_cols(2 * SBW + P * (unit - U_V)))
                if unit < U_GATE:
                    return halved(in_cols(P * (unit - U_Q)))
                if is_gate(unit):
                    return halved(in_cols(3 * SBW + SW + P * gate_of(unit)))
                if unit < U_PROJ:
                    c0 = 2 * P * (unit - U_GLU)
                    return halved(w_glu[0].rearrange("(k p) c -> p k c", p=P)[:, :, c0:c0 + 2 * P])
                if unit < U_WO:
                    c0 = P * (unit - U_PROJ)
                    return [w[0].rearrange("(k p) c -> p k c", p=P)[:, :, c0:c0 + P]
                            for w in (w_attn_proj, w_ssm_proj)]
                c0 = P * (unit - U_WO)
                return halved(w_o[0].rearrange("(k p) c -> p k c", p=P)[:, :, c0:c0 + P])

            def up_source(f, part):
                src = w_up[0].rearrange("(k p) c -> p k c", p=P)
                return halved(src[:, :, bass.ds(f * P + part * FFN, P)])

            def down_source(m, half):
                src = w_down[0].rearrange("(k p) c -> p k c", p=P)[:, half * UT:(half + 1) * UT, :]
                return halved(src[:, :, bass.ds(m * P, P)])

            sp.dma_start(xtok[0:META, 0, :], meta_tokens).then_inc(x_in[0], 16)
            sp.dma_start(xtok[META:TT_ROWS, 0, :], x[0, 0:TT_ROWS - META, :]).then_inc(x_in[0], 16)
            rest = x[0, TT_ROWS - META:SEQ, :].rearrange("(i p) d -> p i d", p=TT_ROWS)
            sp.dma_start(xtok[0:TT_ROWS, 1:3, :], rest[:, 0:2, :]).then_inc(x_in[1], 16)
            sp.dma_start(xtok[0:TT_ROWS, 3:NTT, :], rest[:, 2:NTT - 1, :]).then_inc(x_in[2], 16)
            load(0, source(0))
            load(1, source(1))

            def u_write(r):
                sp.wait_ge(drained, r + 1)
                sp.dma_start(u_dram[r * P:(r + 1) * P], uy[:, r % 2]).then_inc(u_out[r], 16)

            def u_read(r):
                sp.wait_ge(u_out[r], 16)
                if r >= 2:
                    sp.wait_ge(y_ps, r - 1)
                src = u_dram[r * P:(r + 1) * P].rearrange("(g h) j c -> j h g c", h=GH)
                for j in range(T8):
                    p0 = GH * (T8 - 1 - j)
                    sp.dma_start(uc[p0:p0 + GH, r % 2], src[j]).then_inc(u_in[r], 16)

            def toep_move(r):
                sp.wait_ge(kern_set, r + 1)
                for j in range(T8):
                    p0 = GH * (T8 - 1 - j)
                    sp.dma_start(toep[p0:p0 + GH, :, GH * j:P],
                                 kern[:, :, 0:P - GH * j]).then_inc(kern_out[r], 16)

            def y_write(r):
                sp.wait_ge(yg_set, r + 1)
                dst = y_dram[r * P:(r + 1) * P].rearrange("(g h) j c -> j h g c", h=GH)
                for j in range(T8):
                    sp.dma_start(dst[j], yg[GH * j:GH * (j + 1)]).then_inc(y_out[r], 16)

            def y_read(_):
                for r in range(ROUNDS):
                    sp.wait_ge(y_out[r], 16 * T8)
                sp.wait_ge(st_set, ROUNDS)
                sp.wait_ge(y_ps, ROUNDS)
                sp.dma_start(yT[:], y_dram.rearrange("(r p) j c -> p r j c", p=P)).then_inc(y_in, 16)

            move = {"u_write": u_write, "u_read": u_read, "toep": toep_move, "y_write": y_write,
                    "y_read": y_read}
            for done in range(U_UP - 2):
                sp.wait_ge(lo_ready, done + 1)
                load((done + 2) % 2, source(done + 2))
                for name, r in MOVES.get(done, []):
                    move[name](r)

            with sp.Fori(0, KF) as f:
                for part in range(2):
                    sp.wait_ge(lo_ready, f * 2 + (U_UP - 1 + part))
                    load(part, up_source(f, part))

            def store(m, s):
                sp.wait_ge(yt_set, m + 1)
                dst = out[0].rearrange("(t p) c -> p t c", p=P)[:, :, bass.ds(m * P, P)]
                sp.dma_start(dst, yt[s][:]).then_inc(out_done[s], 16)

            def down_load(m):
                for half in range(2):
                    sp.wait_ge(lo_ready, m * 2 + (U_DOWN - 1 + half))
                    load(half, down_source(m, half))

            down_load(0)
            down_load(1)
            with sp.Fori(1, KD // 2) as mm:
                for s in range(2):
                    down_load(mm * 2 + s)
                    store(mm * 2 + (s - 2), s)
            for s in range(2):
                store(KD - 2 + s, s)
            for s in range(2):
                sp.wait_ge(out_done[s], 16 * KD // 2)

        @block.gpsimd
        def _(pool):
            link = linker(pool, pool_link)
            link(pool.memset(stack[:, 0, :], 0.0))
            pool.dma_start(stack[ROW_ARE:ROW_ARE + PAIRS, 0, :],
                           ssm_a_re[0].rearrange("(r g) p -> r (g p)", g=2)).then_inc(stk_in, 16)
            pool.dma_start(stack[ROW_AIM:ROW_AIM + PAIRS, 0, :],
                           ssm_a_im[0].rearrange("(r g) p -> r (g p)", g=2)).then_inc(stk_in, 16)
            pool.dma_start(stack[ROW_SKIP:ROW_SKIP + GROUPS, 0, 0:GH], ssm_d[0]).then_inc(stk_in, 16)
            pool.dma_start(lst[ROW_STEP:ROW_STEP + PAIRS, :],
                           ssm_log_step[0].rearrange("(r g) -> r g", g=2)).then_inc(stk_in, 16)
            link(pool.memset(ident[:], 0.0))
            link(pool.affine_select(out=ident[:], in_=ident[:], compare_op=ALU.not_equal, fill=1.0,
                                    base=0, pattern=[[-1, P]], channel_multiplier=1))
            pool.memset(ones[:], 1.0).then_inc(masks_set, 1)
            pool.wait_ge(masks_set, 1)
            link(pool.memset(blocks[:], 0.0))
            link(pool.memset(blocks[0:DH, 0:DH], 1.0))
            link(pool.memset(blocks[DH:P, DH:P], 1.0))
            tri = pt[:, 0:P]
            link(pool.memset(tri, -1.0))
            link(pool.tensor_copy(negones[:], tri))
            link(pool.affine_select(out=tri, in_=tri, compare_op=ALU.is_ge, fill=0.0,
                                    base=0, pattern=[[-1, P]], channel_multiplier=1))
            link(pool.tensor_copy(negtri[:], tri))
            link(pool.tensor_copy(ident_bf[:], ident[:]))
            link(pool.memset(mask[:], NEG))
            link(pool.affine_select(out=mask[:], in_=mask[:], compare_op=ALU.is_ge, fill=0.0,
                                    base=0, pattern=[[-1, P]], channel_multiplier=1))
            first = Q_LAST - KEY0[4]
            link(pool.memset(mask_last[:], 0.0))
            link(pool.affine_select(out=mask_last[:], in_=mask_last[:], compare_op=ALU.is_ge,
                                    fill=NEG, base=-first, pattern=[[0, META]],
                                    channel_multiplier=1))
            link(pool.affine_select(out=mask_last[:], in_=mask_last[:], compare_op=ALU.is_gt,
                                    fill=NEG, base=first, pattern=[[1, META]],
                                    channel_multiplier=-1))
            link(pool.memset(toep[:], 0.0))
            link(pool.memset(decay[:], 0.0))
            link(pool.memset(xst[:], 0.0))
            link(pool.memset(rot[:, 0, :, 0:1], 1.0))
            link(pool.memset(rot[:, 1, :, 0:1], 0.0))
            link(pool.memset(pw[:, 0, 0, :], 1.0))
            pool.memset(pw[:, 1, 0, :], 0.0).then_inc(masks_set, 1)
            pool.wait_ge(masks_set, 2)

            def cmul(o, a, b, t):
                link(pool.tensor_tensor(o[0], a[0], b[0], ALU.mult))
                link(pool.tensor_tensor(t, a[1], b[1], ALU.mult))
                link(pool.tensor_tensor(o[0], o[0], t, ALU.subtract))
                link(pool.tensor_tensor(o[1], a[0], b[1], ALU.mult))
                link(pool.tensor_tensor(t, a[1], b[0], ALU.mult))
                link(pool.tensor_tensor(o[1], o[1], t, ALU.add))

            def both(ap):
                return ap[:, 0], ap[:, 1]

            def tmp(*shape):
                n = 1
                for s in shape:
                    n *= s
                v = pt[:, 0:n]
                if len(shape) == 1:
                    return v
                if len(shape) == 2:
                    return v.rearrange("p (a b) -> p a b", b=shape[1])
                return v.rearrange("p (a b c) -> p a b c", b=shape[1], c=shape[2])

            pool.wait_ge(small_v, 3)
            for n in (1, 2, 4):
                at = (pw[:, 0, n:n + 1, :].broadcast_to([P, n, PAIRS]),
                      pw[:, 1, n:n + 1, :].broadcast_to([P, n, PAIRS]))
                cmul((pw[:, 0, n + 1:2 * n + 1, :], pw[:, 1, n + 1:2 * n + 1, :]),
                     (pw[:, 0, 1:n + 1, :], pw[:, 1, 1:n + 1, :]), at, tmp(n, PAIRS))
            pool.wait_ge(bc_in, 16 * BC_DMAS)
            f = [sm[:, c, :].unsqueeze(2).broadcast_to([P, PAIRS, GH]) for c in (S_FR, S_FI)]
            cmul(both(bb), both(braw), f, tmp(PAIRS, GH))
            pool.wait_ge(ct_set, 1)

            def input_map(r):
                if r:
                    pool.wait_ge(g_t, r)
                pr = slice(r * RP, (r + 1) * RP)
                for i in range(RP):
                    at = r * RP + i
                    cmul([g_in[:, c, i] for c in range(2)],
                         [pw[:, c, 0:T8, at:at + 1].broadcast_to([P, T8, GH]) for c in range(2)],
                         [bb[:, c, at:at + 1, :].broadcast_to([P, T8, GH]) for c in range(2)],
                         tmp(T8, GH))
                pool.nop().then_inc(g_ready, 1)

            def output_map(r):
                if r:
                    pool.wait_ge(y_ps, r)
                for i in range(RP):
                    at = r * RP + i
                    shape = [P, T8 + 1, GH]
                    a = [pw[:, c, :, at:at + 1].broadcast_to(shape) for c in range(2)]
                    b = [ct[:, c, at:at + 1, :].broadcast_to(shape) for c in range(2)]
                    t = tmp(T8 + 1, GH)
                    o = hout[:, 0, i], hout[:, 1, i]
                    link(pool.tensor_tensor(o[0], a[0], b[0], ALU.mult))
                    link(pool.tensor_tensor(t, a[1], b[1], ALU.mult))
                    link(pool.tensor_tensor(o[0], o[0], t, ALU.add))
                    link(pool.tensor_tensor(o[1], a[0], b[1], ALU.mult))
                    link(pool.tensor_tensor(t, a[1], b[0], ALU.mult))
                    link(pool.tensor_tensor(o[1], o[1], t, ALU.subtract))
                pool.nop().then_inc(h_ready, 1)

            input_map(0)
            output_map(0)
            e = [en[:, 0], en[:, 1]]
            n = 1
            k = 0
            link(pool.tensor_copy(en[:, 0, 0], sm[:, S_COS, :]))
            link(pool.tensor_copy(en[:, 0, 1], sm[:, S_SIN, :]))
            for _ in range(3):
                cmul(both(en[:, 1 - k]), both(en[:, k]), both(en[:, k]), tmp(PAIRS))
                k = 1 - k
            while n < NC:
                w = min(n, NC - n)
                shape = [P, PAIRS, w]
                at = [en[:, k, c].unsqueeze(2).broadcast_to(shape) for c in range(2)]
                cmul([rot[:, c, :, n:n + w] for c in range(2)],
                     [rot[:, c, :, 0:w] for c in range(2)], at, tmp(PAIRS, w))
                n *= 2
                if n < NC:
                    cmul(both(en[:, 1 - k]), both(en[:, k]), both(en[:, k]), tmp(PAIRS))
                    k = 1 - k
            link(pool.tensor_tensor(sm[:, S_D2, :], sm[:, S_MAG, :], sm[:, S_MAG, :], ALU.mult))
            link(pool.tensor_tensor(sm[:, S_D4, :], sm[:, S_D2, :], sm[:, S_D2, :], ALU.mult))
            link(pool.tensor_tensor(sm[:, S_D2, :], sm[:, S_D4, :], sm[:, S_D4, :], ALU.mult))
            pool.tensor_copy(decay[:, :, 1:NC], sm[:, S_D2, :].unsqueeze(2)
                             .broadcast_to([P, PAIRS, NC - 1])).then_inc(rot_set, 1)

            for unit in range(U_PROJ):
                for name, i in STEPS.get(unit, []):
                    if name == "prep" and i + 1 < ROUNDS:
                        input_map(i + 1)
                    if name == "readout" and i + 1 < ROUNDS:
                        output_map(i + 1)
                    if name == "readout" and i + 1 == ROUNDS:
                        pool.wait_ge(y_ps, ROUNDS)
                        pool.wait_ge(yg_set, ROUNDS)
                        for part, i in ((slice(DH, P), 0), (slice(0, DH), 1)):
                            for q in (qzh[i], qzl[i]):
                                link(pool.memset(q[part, :].bitcast(F32), 0.0))
                        pool.nop().then_inc(qz_zero, 1)
            for m in range(KD):
                pool.wait_ge(m_gated, m + 1)
                pool.tensor_tensor(ma[m % 2][:], ma[m % 2][:], mb[m % 2][:], ALU.add)\
                    .then_inc(m_sum, 1)
            for m in range(KD):
                pool.wait_ge(h_sq, m + 1)
                if m == 0:
                    pool.tensor_copy(acc[:], sqh[0][:]).then_inc(h_acc, 1)
                else:
                    pool.wait_ge(h_acc, m)
                    pool.tensor_tensor(acc[:], acc[:], sqh[m % 2][:], ALU.add).then_inc(h_acc, 1)

            def product(f, s):
                pool.wait_ge(silu_a, f + 1)
                pool.wait_ge(cv_v, f * 2 + 2)
                pool.tensor_tensor(cv[s][:, 1], cv[s][:, 0], cv[s][:, 1], ALU.mult)\
                    .then_inc(act_p, 1)

            with pool.Fori(0, KF // 2) as ff:
                for s in range(2):
                    product(ff * 2 + s, s)

        @block.scalar
        def _(act):
            link = linker(act, act_link)

            def split(unit, slot, n):
                act.wait_ge(raw_in[slot], (unit - slot) * 16 + 32)
                if not isinstance(unit, int) or unit >= 2:
                    act.wait_ge(unit_done, unit - 1)
                act.activation(hi[slot][:, 0:n * P], raw[slot][:, 0:n * P], ACT.Copy)\
                    .then_inc(hi_ready, 1)

            rows = [(stack[:, 1, :], conv_w[0].rearrange("j (m c) -> (j m) c", c=P)[0:P, :]),
                    (stack[0:4, 2, :], conv_w[0].rearrange("j (m c) -> (j m) c", c=P)[P:P + 4, :]),
                    (stack[4:48, 2, :], conv_b[0].rearrange("(m c) -> m c", c=P)),
                    (stack[48:56, 2, :], norm1_g[0].rearrange("(m c) -> m c", c=P)),
                    (stack[56:64, 2, :], norm2_g[0].rearrange("(m c) -> m c", c=P)),
                    (stack[64:68, 2, :], b_glu[0].rearrange("(m c) -> m c", c=P)),
                    (stack[68:69, 2, 0:DH], q_norm_g), (stack[68:69, 2, DH:P], q_norm_g),
                    (stack[69:70, 2, 0:DH], k_norm_g), (stack[69:70, 2, DH:P], k_norm_g)]
            for dst, src in rows:
                act.dma_start(dst, src).then_inc(par_in, 16)
            for c, (b_in, c_in) in enumerate(((ssm_b_re, ssm_c_re), (ssm_b_im, ssm_c_im))):
                act.dma_start(braw[:, c], b_in[0].rearrange("(r g) p h -> (g p) r h", g=2))\
                    .then_inc(bc_in, 16)
                for d in range(2):
                    act.dma_start(cdup[:, c, :, d, :],
                                  c_in[0].rearrange("(t g) h p -> (g h) t p", g=8)).then_inc(bc_in, 16)
            act.preload_act_table_set("natural_log_exp_and_others")

            for i in range(NTT):
                if i in (0, 1, 3):
                    act.wait_ge(x_in[(i + 1) // 2], 32 if i == 0 else 16)
                rows = slice(0, TT_ROWS)
                act.activation(ps[rows, 6:8, :], halves(xtok[rows, i, :], 512), ACT.Square,
                               accum_out=ssx[rows, 0, i:i + 1]).then_inc(ss_x, 1)
                act.wait_ge(ss_x, i + 1)
            act.wait_ge(rx_ready, 1)
            link(act.activation(ssx[rows, 1, :], ssx[rows, 0, :], ACT.Ln))
            act.activation(ssx[rows, 1, :], ssx[rows, 1, :], ACT.Exp, scale=-0.5).then_inc(ss_x, 1)
            act.wait_ge(rb_ps, 1)
            act.activation(halves(rb[:], HL), psum2(6, HL), ACT.Copy).then_inc(rb_set, 1)
            for k in range(KD):
                act.wait_ge(xt_ps, k + 1)
                act.activation(halves(hT[:, k], HL), psum2(4 + 2 * (k % 2), HL), ACT.Copy)\
                    .then_inc(xt_copied, 1)
                act.wait_ge(xn_set, k + 1)
                act.activation(xh[:, k], qT[:, k % 2], ACT.Copy).then_inc(xh_set, 1)
                if k == 1:
                    split(0, 0, KD)
                if k == 3:
                    split(1, 1, KD)

            def small(i):
                if i == 0:
                    act.wait_ge(small_v, 1)
                    act.activation(sm[:, S_STEP, :], colc[:, ROW_STEP:ROW_STEP + PAIRS], ACT.Exp)\
                        .then_inc(small_a, 1)
                    act.wait_ge(small_v, 2)
                    act.activation(sm[:, S_MAG, :], sm[:, S_LST, :], ACT.Exp)
                    act.activation(sm[:, S_SIN, :], sm[:, S_TH, :], ACT.Sin)
                    act.activation(sm[:, S_SINH, :], sm[:, S_TH, :], ACT.Sin, scale=0.5)\
                        .then_inc(small_a, 1)
                    act.preload_act_table_set("natural_log_exp_and_others")

            small(0)

            def norm(i):
                is_k, t, _ = norm_of(i)
                w = L if is_k else LL
                act.wait_ge(ss_v, i + 1)
                link(act.activation(ta[:, 0:w], tb[:, 0:w], ACT.Ln))
                act.activation(ta[:, 0:w], ta[:, 0:w], ACT.Exp, scale=-0.5).then_inc(rs_a, 1)

            def prep(r):
                act.wait_ge(g_t, r + 1)
                for c in range(2):
                    ins = act.activation(win[:, c], ps[:, 4 + c, :], ACT.Copy)
                ins.then_inc(win_set, 1)

            def turn_v(t):
                act.wait_ge(v_t, t + 1)
                c0 = P * t
                act.activation(vh[:, 0:4, c0:c0 + P],
                               ps[:, 4, :].rearrange("p (k c) -> p k c", c=P), ACT.Copy)
                act.activation(vh[:, 4, c0:c0 + P], ps[:, 5, 0:P], ACT.Copy).then_inc(vh_set, 1)

            def readout(r):
                act.preload_act_table_set("gelu_apprx_tanh_and_others")
                act.wait_ge(y_ps, r + 1)
                if r:
                    act.wait_ge(y_out[r - 1], 16 * T8)
                act.activation(yg[:].rearrange("p (b g) c -> p b (g c)", b=2), psum2(6, HL),
                               ACT.Gelu_apprx_tanh).then_inc(yg_set, 1)
                act.preload_act_table_set("natural_log_exp_and_others")
                if r == ROUNDS - 1:
                    act.wait_ge(qz_zero, 1)
                    head_k(0)
                    head_q(0)
                    head_q(1)

            def head_k(t):
                act.wait_ge(normed, 4)
                if t:
                    act.wait_ge(z_ps, 2 * t)
                act.activation(kh[:], kT[:, t], ACT.Copy).then_inc(kh_set, 1)

            def head_q(h):
                if h >= 2:
                    act.wait_ge(z_ps, h - 1)
                part = slice(DH * (h % 2), DH * (h % 2) + DH)
                act.activation(qzh[h % 2][part, :], qT[part, h // 2, 0:LL], ACT.Copy)\
                    .then_inc(qh_set, 1)

            def scores(h):
                act.wait_ge(z_ps, h + 1)
                if h:
                    act.wait_ge(prob_lo, 2 * h)
                for b in range(4):
                    ins = act.activation(aw[:, bank_cols(b)], ps[:, 4 + b, 0:BANK_COLS[b]], ACT.Abs)
                link(ins)
                for cols_ in HALVES:
                    ins = act.activation(aw[:, cols_], aw[:, cols_], ACT.Exp, scale=-1.0)
                link(ins)
                for cols_ in HALVES:
                    act.activation(aw[:, cols_], aw[:, cols_], ACT.Ln, bias=1.0).then_inc(z_ln, 1)
                if h:
                    act.wait_ge(av_ps, h)
                for i, cols_ in enumerate(HALVES):
                    act.wait_ge(soft_set, 2 * h + i + 1)
                    act.activation(awh[:, cols_], aw[:, cols_], ACT.Copy).then_inc(soft_hi, 1)

            def suffix(h):
                if h == 1:
                    head_k(1)
                    head_q(2)
                    head_q(3)
                act.wait_ge(suf_ps, h + 1)
                act.wait_ge(soft_lo, 2 * h + 2)
                for b in range(4):
                    ins = act.activation(aw[:, bank_cols(b)], ps[:, 4 + b, 0:BANK_COLS[b]], ACT.Exp)
                link(ins)
                for cols_ in HALVES:
                    act.activation(awh[:, cols_], aw[:, cols_], ACT.Copy).then_inc(prob_hi, 1)

            def values(h):
                act.wait_ge(av_ps, h + 1)
                part = slice(DH * (h % 2), DH * (h % 2) + DH)
                act.activation(atth[part, h // 2, 0:Q_SPLIT - LATE0],
                               ps[part, 4, 0:Q_SPLIT - LATE0], ACT.Copy)
                act.activation(atth[part, h // 2, Q_SPLIT - LATE0:LL], ps[part, 5, 0:L - Q_SPLIT],
                               ACT.Copy).then_inc(ath_set, 1)

            def gelu(i):
                if i == 0:
                    act.wait_ge(y_in, 16)
                for r in (2 * i, 2 * i + 1):
                    act.activation(gh[:, r].rearrange("p (c j) -> p c j", j=T8),
                                   yT[:, r].rearrange("p j c -> p c j"), ACT.Copy)\
                        .then_inc(gh_set, 1)

            steps = {"norm": norm, "prep": prep, "readout": readout, "scores": scores,
                     "suffix": suffix, "values": values, "gelu": gelu, "turn_v": turn_v}

            def evacuate(unit):
                act.wait_ge(unit_done, unit + 1)
                b = 2 * (unit % 2)
                if unit < U_K:
                    if unit >= 2:
                        act.wait_ge(u_out[unit - 2], 16)
                    dst = uy[:, unit % 2].rearrange("p j (k c) -> p k c j", k=2)
                    for k in range(2):
                        ins = act.activation(dst[:, k], ps[:, b + k, 0:HL]
                                             .rearrange("p (c j) -> p c j", j=T8), ACT.Copy)
                    ins.then_inc(drained, 1)
                elif unit < U_V or U_Q <= unit < U_GATE:
                    i = unit - U_K if unit < U_V else unit - U_Q + 2
                    is_k, t, _ = norm_of(i)
                    dst, w = (kT, HL) if is_k else (qT, HLL)
                    ins = act.activation(halves(dst[:, t, 0:2 * w], w), psum2(b, w), ACT.Copy)
                    ins.then_inc(drained, 1)
                    act.wait_ge(drained, unit + 1)
                    act.activation(sq[i][:, 0:2 * w], dst[:, t, 0:2 * w], ACT.Square)\
                        .then_inc(sq_ready, 1)
                elif unit < U_Q:
                    act.activation(halves(vT[unit - U_V], HL), psum2(b, HL), ACT.Copy)\
                       .then_inc(drained, 1)
                elif is_gate(unit):
                    act.activation(halves(gate[gate_of(unit)], HLL), psum2(b, HLL), ACT.Copy)\
                       .then_inc(gate_raw, 1)
                else:
                    if unit == U_GLU:
                        act.preload_act_table_set("sigmoid_and_others")
                    for mm in range(2):
                        m = 2 * (unit - U_GLU) + mm
                        if m >= 2:
                            act.wait_ge(sl_set, m - 1)
                        act.activation(halves(gt[mm][:], HL), psum2(2 * mm, HL), ACT.Sigmoid,
                                       bias=cols[:, COL_BG + m:COL_BG + m + 1])\
                           .then_inc(glu_sig, 1)
                    act.wait_ge(av_ps, HEADS)
                    for mm in range(2):
                        m = 2 * (unit - U_GLU) + mm
                        act.wait_ge(glu_val, m + 1)
                        act.activation(sh[:, m], gt[mm][:], ACT.Copy).then_inc(sh_set, 1)

            def open_gates(m):
                if m == 0:
                    act.wait_ge(gate_raw, 2 * KD)
                for i in (m, KD + m):
                    ins = act.activation(gate[i], gate[i], ACT.Sigmoid)
                ins.then_inc(gate_set, 1)

            def tiles_of(unit):
                return 6 if U_PROJ <= unit < U_WO else KD

            for unit in range(U_PROJ):
                split(unit + 2, unit % 2, tiles_of(unit + 2))
                evacuate(unit)
                for name, i in STEPS.get(unit, []):
                    if name in steps:
                        steps[name](i)
            open_gates(0)
            open_gates(1)
            for m in range(KD):
                unit = U_PROJ + m
                split(unit + 2, unit % 2, tiles_of(unit + 2))
                if m + 2 < KD:
                    open_gates(m + 2)
                act.wait_ge(m_sum, m + 1)
                act.activation(mh[:, m], ma[m % 2][:], ACT.Copy).then_inc(mh_set, 1)
            for m in range(KD):
                unit = U_WO + m
                split(unit + 2, unit % 2, KD)
                act.wait_ge(h_set, m + 1)
                if m >= 2:
                    act.wait_ge(h_acc, m - 1)
                act.activation(sqh[m % 2][:], hT[:, m, LATE0:L], ACT.Square).then_inc(h_sq, 1)
                act.activation(xh[:, m, 0:LL], hT[:, m, LATE0:L], ACT.Copy,
                               scale=cols[:, COL_N2 + m:COL_N2 + m + 1]).then_inc(zh_set, 1)
            act.preload_act_table_set("natural_log_exp_and_others")
            act.wait_ge(ss2_v, 1)
            link(act.activation(rb[:, 0:LL], nv[:], ACT.Ln))
            act.activation(rb[:, 0:LL], rb[:, 0:LL], ACT.Exp, scale=-0.5).then_inc(r2_a, 1)
            act.preload_act_table_set("silu_and_others")

            def cast_product(f, s):
                act.wait_ge(act_p, f + 1)
                act.activation(ah[:, bass.ds(f, 1), :].rearrange("p a c -> p (a c)"), cv[s][:, 1],
                               ACT.Copy).then_inc(ah_set, 1)

            def up(f, s, tiles=KD):
                for part in range(2):
                    split(f * 2 + (U_UP + 2 + part), part, tiles)
                    act.wait_ge(up_v, f * 2 + (part + 1))
                    if part == 0 and not (isinstance(f, int) and f < 2):
                        act.wait_ge(al_set, f - 1)
                    m = f + part * KF
                    act.activation(cv[s][:, part], ut[s][:, part, 2:2 + SEQ], ACT.Identity,
                                   bias=cols[:, bass.ds(m + COL_CB, 1)],
                                   scale=cols[:, bass.ds(m + COL_CW, 1)]).then_inc(cv_a, 1)
                    if part == 0:
                        if not (isinstance(f, int) and f < 1):
                            cast_product(f - 1, 1 - s)
                        act.wait_ge(cv_v, f * 2 + 1)
                        act.activation(cv[s][:, 0], cv[s][:, 0], ACT.Silu).then_inc(silu_a, 1)

            up(0, 0)
            up(1, 1)
            with act.Fori(1, KF // 2 - 1) as ff:
                for s in range(2):
                    up(ff * 2 + s, s)
            up(KF - 2, 0)
            up(KF - 1, 1, UT)
            cast_product(KF - 1, 1)

            def turned(m, s, stored):
                act.wait_ge(yt_ps, m + 1)
                if not isinstance(stored, int) or stored:
                    act.wait_ge(out_done[s], 16 * stored)
                act.activation(yt[s][:], ps[:, 4 + s, :].rearrange("p (t c) -> p t c", c=P),
                               ACT.Copy).then_inc(yt_set, 1)

            def down(m, stored, s):
                for half in range(2):
                    split(m * 2 + (U_DOWN + 2 + half), half, UT)
                turned(m - 1, s, stored)

            for half in range(2):
                split(U_DOWN + 2 + half, half, UT)
            down(1, 0, 0)
            down(2, 0, 1)
            with act.Fori(1, KD // 2 - 1) as mm:
                for s in range(2):
                    down(mm * 2 + (1 + s), mm, s)
            for s in range(2):
                turned(KD - 2 + s, s, KD // 2 - 1)

        @block.vector
        def _(dve):
            link = linker(dve, dve_link)

            def split(unit, slot, n):
                dve.wait_ge(hi_ready, unit + 1)
                dve.tensor_tensor(lo[slot][:, 0:n * P], raw[slot][:, 0:n * P],
                                  hi[slot][:, 0:n * P].bitcast(F32), ALU.subtract)\
                   .then_inc(lo_ready, 1)

            def newton(r, v, t, factor=1.0):
                link(dve.tensor_tensor(t, r, r, ALU.mult))
                link(dve.tensor_tensor(t, t, v, ALU.mult))
                link(dve.tensor_scalar(t, t, -0.5 * factor, 1.5 * factor, ALU.mult, ALU.add))
                return dve.tensor_tensor(r, r, t, ALU.mult)

            dve.wait_ge(stk_in, 64)
            sr = slice(ROW_STEP, ROW_STEP + PAIRS)
            dve.tensor_copy(stack[sr, 0, :].rearrange("r (g p) -> r g p", g=2),
                            lst[sr].unsqueeze(2).broadcast_to([PAIRS, 2, ST]))\
               .then_inc(stack_full, 1)

            rows = slice(0, TT_ROWS)
            v, r, t = (ssx[rows, i, :] for i in (0, 1, 2))
            diag = tb[rows]
            dve.wait_ge(ss_x, NTT)
            dve.tensor_scalar(v, v, 1.0 / D, EPS, ALU.mult, ALU.add).then_inc(rx_ready, 1)
            dve.wait_ge(ss_x, NTT + 1)
            dve.wait_ge(masks_set, 1)
            link(newton(r, v, t))
            dve.tensor_tensor(diag.rearrange("p (i c) -> p i c", c=TT_ROWS),
                              ident[rows, 0:TT_ROWS].unsqueeze(1)
                              .broadcast_to([TT_ROWS, NTT, TT_ROWS]),
                              r.unsqueeze(2).broadcast_to([TT_ROWS, NTT, TT_ROWS]), ALU.mult)\
               .then_inc(rx_ready, 1)
            dve.wait_ge(cols_t, 1)
            link(dve.tensor_copy(colc[:], ps[:, 0, 0:P]))
            dve.tensor_copy(cols[:], ps[:, 0, P:P + NCOLS]).then_inc(cols_set, 1)
            dve.wait_ge(cols_t, 2)
            for c in range(2):
                src = ps[:, 1 + c, :].rearrange("p (r g h) -> p r g h", g=2, h=GH)
                for g in range(2):
                    part = slice(ST * g, ST * g + ST)
                    ins = dve.tensor_scalar(ct[part, c], src[part, :, g, :], 1.0 - 2.0 * c, None,
                                            ALU.mult)
            ins.then_inc(ct_set, 1)

            def x_lo(k):
                dve.wait_ge(xh_set, k + 1)
                dve.tensor_tensor(xl[:, k], qT[:, k % 2], xh[:, k].bitcast(F32), ALU.subtract)\
                   .then_inc(x_ready, 1)

            dve.wait_ge(rb_set, 1)
            dve.wait_ge(cols_set, 1)
            for k in range(KD):
                dve.wait_ge(xt_copied, k + 1)
                if k >= 2:
                    dve.wait_ge(x_ready, k - 1)
                dve.scalar_tensor_tensor(qT[:, k % 2], hT[:, k], cols[:, COL_N1 + k:COL_N1 + k + 1],
                                         rb[:], ALU.mult, ALU.mult).then_inc(xn_set, 1)
                if k:
                    x_lo(k - 1)
                if k == 2:
                    split(0, 0, KD)
                if k == 4:
                    split(1, 1, KD)
            x_lo(KD - 1)

            def s(i):
                return sm[:, i, :]

            def tt(o, a, b, op):
                link(dve.tensor_tensor(s(o), s(a), s(b), op))

            are = colc[:, ROW_ARE:ROW_ARE + PAIRS]
            aim = colc[:, ROW_AIM:ROW_AIM + PAIRS]
            dve.tensor_scalar(s(S_LRE), are, A_RE_MAX, None, ALU.min).then_inc(small_v, 1)
            dve.wait_ge(small_v, 1)
            dve.wait_ge(small_a, 1)
            link(dve.tensor_tensor(s(S_LST), s(S_LRE), s(S_STEP), ALU.mult))
            link(dve.tensor_tensor(s(S_TH), aim, s(S_STEP), ALU.mult))
            link(dve.tensor_scalar(s(S_N), s(S_TH), 1.0 / TWO_PI, ROUND_MAGIC, ALU.mult, ALU.add))
            link(dve.tensor_scalar(s(S_N), s(S_N), ROUND_MAGIC, None, ALU.subtract))
            for c in (CW1, CW2, CW3):
                link(dve.scalar_tensor_tensor(s(S_TH), s(S_N), -c, s(S_TH), ALU.mult, ALU.add))
            dve.tensor_scalar(s(S_TH), s(S_TH), PI_BELOW, -PI_BELOW, ALU.min, ALU.max)\
               .then_inc(small_v, 1)
            tt(S_T1, S_LRE, S_LRE, ALU.mult)
            link(dve.tensor_tensor(s(S_T2), aim, aim, ALU.mult))
            tt(S_DEN, S_T1, S_T2, ALU.add)
            link(dve.reciprocal(s(S_DEN), s(S_DEN)))
            link(dve.tensor_tensor(skip_i[:], ident[0:GH, 0:GH].unsqueeze(1)
                                   .broadcast_to([GH, GROUPS, GH]),
                                   colc[0:GH, ROW_SKIP:ROW_SKIP + GROUPS].unsqueeze(2)
                                   .broadcast_to([GH, GROUPS, GH]), ALU.mult))
            dve.wait_ge(small_a, 2)
            tt(S_T1, S_SINH, S_SINH, ALU.mult)
            link(dve.tensor_scalar(s(S_COS), s(S_T1), -2.0, 1.0, ALU.mult, ALU.add))
            dve.wait_ge(masks_set, 2)
            link(dve.tensor_tensor(pw[:, 0, 1, :], s(S_MAG), s(S_COS), ALU.mult))
            link(dve.tensor_tensor(pw[:, 1, 1, :], s(S_MAG), s(S_SIN), ALU.mult))
            link(dve.tensor_scalar(s(S_NR), pw[:, 0, 1, :], 1.0, None, ALU.subtract))
            tt(S_T1, S_NR, S_LRE, ALU.mult)
            link(dve.tensor_tensor(s(S_T2), pw[:, 1, 1, :], aim, ALU.mult))
            tt(S_FR, S_T1, S_T2, ALU.add)
            link(dve.tensor_tensor(s(S_T1), pw[:, 1, 1, :], s(S_LRE), ALU.mult))
            link(dve.tensor_tensor(s(S_T2), s(S_NR), aim, ALU.mult))
            tt(S_FI, S_T1, S_T2, ALU.subtract)
            tt(S_FR, S_FR, S_DEN, ALU.mult)
            dve.tensor_tensor(s(S_FI), s(S_FI), s(S_DEN), ALU.mult).then_inc(small_v, 1)

            def norm(i):
                is_k, tile, _ = norm_of(i)
                w = HL if is_k else HLL
                dst = (kT if is_k else qT)[:, tile, 0:2 * w]
                g = cols[:, (COL_KG if is_k else COL_QG):][:, 0:1]
                dve.wait_ge(ss_ps, i + 1)
                dve.tensor_scalar(halves(tb[:, 0:2 * w], w), psum2(4, w), 1.0 / DH, EPS, ALU.mult,
                                  ALU.add).then_inc(ss_v, 1)
                dve.wait_ge(rs_a, i + 1)
                link(newton(ta[:, 0:2 * w], tb[:, 0:2 * w], sq[i][:, 0:2 * w],
                            1.0 if is_k else DH ** -0.5))
                dve.scalar_tensor_tensor(dst, dst, g, ta[:, 0:2 * w], ALU.mult, ALU.mult)\
                   .then_inc(normed, 1)

            def prep(r):
                dve.wait_ge(k_ps, r + 1)
                if r:
                    dve.wait_ge(kern_out[r - 1], 16 * T8)
                link(dve.tensor_copy(kern[:].rearrange("h (g b) c -> h b g c", b=2),
                                     ps[0:GH, 6:8, :].rearrange("h b (g c) -> h b g c", c=P)))
                dve.tensor_tensor(kern[:, :, 0:GH], kern[:, :, 0:GH],
                                  skip_i[:, 2 * RP * r:2 * RP * (r + 1), :], ALU.add)\
                   .then_inc(kern_set, 1)

            def state(r):
                pr = slice(r * RP, (r + 1) * RP)
                cos, sin = rot[:, 0, pr, :], rot[:, 1, pr, :]
                re, im = (ps[:, 4 + c, 0:RP * NC].rearrange("p (r c) -> p r c", c=NC)
                          for c in range(2))
                m = [mod[:, i] for i in range(4)]
                flat = [x_.rearrange("p r c -> p (r c)") for x_ in m]
                dve.wait_ge(st_ps, r + 1)
                if r == 0:
                    dve.wait_ge(rot_set, 1)
                    for u in u_out:
                        dve.wait_ge(u, 16)
                dve.tensor_tensor(m[0], re, cos, ALU.mult)
                dve.tensor_tensor(m[1], im, sin, ALU.mult)
                dve.tensor_tensor(m[2], im, cos, ALU.mult)
                link(dve.tensor_tensor(m[3], re, sin, ALU.mult))
                dve.tensor_tensor(m[0], m[0], m[1], ALU.add)
                link(dve.tensor_tensor(m[2], m[2], m[3], ALU.subtract))
                dec = decay[:, pr, :].rearrange("p r c -> p (r c)")
                dve.tensor_tensor_scan(flat[1], dec, flat[0], 0.0, ALU.mult, ALU.add)
                link(dve.tensor_tensor_scan(flat[3], dec, flat[2], 0.0, ALU.mult, ALU.add))
                dve.tensor_tensor(m[0], m[1], cos, ALU.mult)
                link(dve.tensor_tensor(m[2], m[3], sin, ALU.mult))
                if r:
                    dve.wait_ge(y_ps, r)

                def forward(c, op):
                    for g in range(2):
                        part = slice(ST * g, ST * g + ST)
                        ins = dve.tensor_tensor(xst[part, c, g, :, 1:NC], m[0][part, :, 0:NC - 1],
                                                m[2][part, :, 0:NC - 1], op)
                    return ins

                link(forward(0, ALU.subtract))
                dve.tensor_tensor(m[0], m[3], cos, ALU.mult)
                link(dve.tensor_tensor(m[2], m[1], sin, ALU.mult))
                forward(1, ALU.add).then_inc(st_set, 1)

            def turn_v(t):
                dve.wait_ge(vh_set, t + 1)
                c = slice(P * t, P * t + P)
                dve.tensor_tensor(vl[:, 0:4, c], ps[:, 4, :].rearrange("p (k c) -> p k c", c=P),
                                  vh[:, 0:4, c].bitcast(F32), ALU.subtract)
                dve.tensor_tensor(vl[:, 4, c], ps[:, 5, 0:P], vh[:, 4, c].bitcast(F32),
                                  ALU.subtract).then_inc(vl_set, 1)

            def readout(r):
                if r == ROUNDS - 1:
                    head_k(0)
                    head_q(0)
                    head_q(1)

            def head_k(t):
                dve.wait_ge(kh_set, t + 1)
                dve.tensor_tensor(kl[:], kT[:, t], kh[:].bitcast(F32), ALU.subtract)\
                   .then_inc(kl_set, 1)

            def head_q(h):
                dve.wait_ge(qh_set, h + 1)
                part = slice(DH * (h % 2), DH * (h % 2) + DH)
                dve.tensor_tensor(qzl[h % 2][part, :], qT[part, h // 2, 0:LL],
                                  qzh[h % 2][part, :].bitcast(F32), ALU.subtract)\
                   .then_inc(ql_set, 1)

            def scores(h):
                for i in range(2):
                    dve.wait_ge(z_ln, 2 * h + i + 1)
                    for b in (2 * i, 2 * i + 1):
                        o = bank_cols(b)
                        ins = dve.scalar_tensor_tensor(aw[:, o], ps[:, 4 + b, 0:BANK_COLS[b]], 0.0,
                                                       aw[:, o], ALU.max, ALU.add)
                    ins.then_inc(soft_set, 1)
                for i, o in enumerate(HALVES):
                    dve.wait_ge(soft_hi, 2 * h + i + 1)
                    dve.tensor_tensor(awl[:, o], aw[:, o], awh[:, o].bitcast(F32), ALU.subtract)\
                       .then_inc(soft_lo, 1)

            def suffix(h):
                if h == 1:
                    head_k(1)
                    head_q(2)
                    head_q(3)
                for i, o in enumerate(HALVES):
                    dve.wait_ge(prob_hi, 2 * h + i + 1)
                    dve.tensor_tensor(awl[:, o], aw[:, o], awh[:, o].bitcast(F32), ALU.subtract)\
                       .then_inc(prob_lo, 1)

            def values(h):
                dve.wait_ge(ath_set, h + 1)
                part = slice(DH * (h % 2), DH * (h % 2) + DH)
                for b, a, e in ((4, 0, Q_SPLIT - LATE0), (5, Q_SPLIT - LATE0, LL)):
                    ins = dve.tensor_tensor(attl[part, h // 2, a:e], ps[part, b, 0:e - a],
                                            atth[part, h // 2, a:e].bitcast(F32), ALU.subtract)
                ins.then_inc(atl_set, 1)

            def token_order(ap):
                return ap.rearrange("p j c -> p c j")

            def by_chunk(ap):
                return ap.rearrange("p (c j) -> p c j", j=T8)

            def gelu(i):
                for r in (2 * i, 2 * i + 1):
                    dve.wait_ge(gh_set, r + 1)
                    dve.tensor_tensor(by_chunk(gl[:, r]), token_order(yT[:, r]),
                                      by_chunk(gh[:, r]).bitcast(F32), ALU.subtract)\
                       .then_inc(gl_set, 1)

            def glu(unit):
                tiles = [2 * (unit - U_GLU) + mm for mm in range(2)]
                for mm, m in enumerate(tiles):
                    dve.wait_ge(glu_sig, m + 1)
                    dve.tensor_tensor(by_chunk(gt[mm][:]), by_chunk(gt[mm][:]),
                                      token_order(yT[:, m]), ALU.mult).then_inc(glu_val, 1)
                for mm, m in enumerate(tiles):
                    dve.wait_ge(sh_set, m + 1)
                    dve.tensor_tensor(sl[:, m], gt[mm][:], sh[:, m].bitcast(F32), ALU.subtract)\
                       .then_inc(sl_set, 1)

            steps = {"norm": norm, "prep": prep, "state": state, "readout": readout,
                     "scores": scores, "suffix": suffix, "values": values, "gelu": gelu,
                     "turn_v": turn_v}

            def tiles_of(unit):
                return 6 if U_PROJ <= unit < U_WO else KD

            for unit in range(U_PROJ):
                split(unit + 2, unit % 2, tiles_of(unit + 2))
                if U_GLU <= unit:
                    glu(unit)
                for name, i in STEPS.get(unit, []):
                    if name in steps:
                        steps[name](i)

            def mixed_lo(m):
                dve.wait_ge(mh_set, m + 1)
                dve.tensor_tensor(ml[:, m], ma[m % 2][:], mh[:, m].bitcast(F32), ALU.subtract)\
                   .then_inc(ml_set, 1)

            for m in range(KD):
                unit = U_PROJ + m
                split(unit + 2, unit % 2, tiles_of(unit + 2))
                dve.wait_ge(gate_set, m + 1)
                dve.wait_ge(unit_done, unit + 1)
                if m >= 2:
                    dve.wait_ge(m_sum, m - 1)
                    dve.wait_ge(ml_set, m - 1)
                b = 4 * (m % 2)
                dve.tensor_tensor(halves(ma[m % 2][:], HLL), psum2(b, HLL), halves(gate[m], HLL),
                                  ALU.mult)
                dve.tensor_tensor(halves(mb[m % 2][:], HLL), psum2(b + 2, HLL),
                                  halves(gate[KD + m], HLL), ALU.mult).then_inc(m_gated, 1)
                if m:
                    mixed_lo(m - 1)
            mixed_lo(KD - 1)

            def z_lo(m):
                dve.wait_ge(zh_set, m + 1)
                dve.scalar_tensor_tensor(xl[:, m, 0:LL], hT[:, m, LATE0:L],
                                         cols[:, COL_N2 + m:COL_N2 + m + 1],
                                         xh[:, m, 0:LL].bitcast(F32), ALU.mult, ALU.subtract)\
                   .then_inc(z_ready, 1)

            for m in range(KD):
                unit = U_WO + m
                split(unit + 2, unit % 2, KD)
                dve.wait_ge(unit_done, unit + 1)
                dve.tensor_tensor(halves(hT[:, m, LATE0:L], HLL), psum2(2 * (m % 2), HLL),
                                  halves(hT[:, m, LATE0:L], HLL), ALU.add).then_inc(h_set, 1)
                if m:
                    z_lo(m - 1)
            z_lo(KD - 1)
            dve.wait_ge(ss2_ps, 1)
            dve.tensor_scalar(halves(nv[:], HLL), psum2(4, HLL), 1.0 / D, EPS, ALU.mult, ALU.add)\
               .then_inc(ss2_v, 1)
            dve.wait_ge(r2_a, 1)
            newton(rb[:, 0:LL], nv[:], sqh[0][:]).then_inc(r2_set, 1)
            dve.wait_ge(r2_set, 1)

            def product_lo(f, s_):
                dve.wait_ge(ah_set, f + 1)
                at = bass.ds(f, 1)
                dve.tensor_tensor(al[:, at, :].rearrange("p a c -> p (a c)"), cv[s_][:, 1],
                                  ah[:, at, :].bitcast(F32).rearrange("p a c -> p (a c)"),
                                  ALU.subtract).then_inc(al_set, 1)

            def up(f, s_, tiles=KD):
                for part in range(2):
                    dve.wait_ge(unit_done, f * 2 + (U_UP + 1 + part))
                    if part == 0 and not (isinstance(f, int) and f < 2):
                        dve.wait_ge(cv_v, f * 2 - 2)
                    dve.tensor_tensor(halves(ut[s_][:, part], HLL), psum2(4 * s_ + 2 * part, HLL),
                                      halves(rb[:, 0:LL], HLL), ALU.mult).then_inc(up_v, 1)
                    split(f * 2 + (U_UP + 2 + part), part, tiles)
                    for tap in (1, 2):
                        if tap == 1:
                            dve.wait_ge(cv_a, f * 2 + (part + 1))
                        else:
                            dve.wait_ge(cv_mid, f * 2 + (part + 1))
                        w = cols[:, bass.ds(f + (COL_CW + (2 * tap + part) * KF), 1)]
                        dve.scalar_tensor_tensor(cv[s_][:, part],
                                                 ut[s_][:, part, 2 + tap:2 + tap + SEQ], w,
                                                 cv[s_][:, part], ALU.mult, ALU.add)\
                           .then_inc(cv_mid if tap == 1 else cv_v, 1)
                    if part == 0 and not (isinstance(f, int) and f < 1):
                        product_lo(f - 1, 1 - s_)

            up(0, 0)
            up(1, 1)
            with dve.Fori(1, KF // 2 - 1) as ff:
                for s_ in range(2):
                    up(ff * 2 + s_, s_)
            up(KF - 2, 0)
            up(KF - 1, 1, UT)
            product_lo(KF - 1, 1)

            def down(m, s_):
                for half in range(2):
                    if not isinstance(m, int) or m < KD - 1:
                        split(m * 2 + (U_DOWN + 2 + half), half, UT)
                dve.wait_ge(unit_done, m * 2 + (U_DOWN + 2))
                if not (isinstance(m, int) and m < 2):
                    dve.wait_ge(yt_ps, m - 1)
                dve.tensor_tensor(yo[s_][:], ps[:, s_, :],
                                  hT[:, bass.ds(m, 1), META:L].rearrange("p a c -> p (a c)"),
                                  ALU.add).then_inc(y_add, 1)

            down(0, 0)
            down(1, 1)
            with dve.Fori(1, KD // 2 - 1) as mm:
                for s_ in range(2):
                    down(mm * 2 + s_, s_)
            for s_ in range(2):
                down(KD - 2 + s_, s_)

        @block.tensor
        def _(pe):
            def three(outs, weights, acts, start, stop):
                for i, (w, a) in enumerate(((0, 0), (0, 1), (1, 0))):
                    for c, o in enumerate(outs):
                        ins = pe.matmul(o, weights[w], acts(a, c), start=start and i == 0,
                                        stop=stop and i == 2)
                return ins

            def wtile(slot, i, n=1):
                return [w[slot][:, i * P:(i + n) * P] for w in (hi, lo)]

            def product(slot, tile0, count, bank, width, pair, col0, ready=None, first=0,
                        stride=1, total=None):
                total = count if total is None else total
                for k in range(count):
                    if ready is not None:
                        pe.wait_ge(ready, first + k + 1)
                    ins = three([ps[:, bank + c, 0:width] for c in range(2)],
                                wtile(slot, tile0 + k * stride),
                                lambda a, c: pair[a][:, first + k, col0 + c * width:
                                                     col0 + (c + 1) * width],
                                k == 0, k == count - 1)
                return ins

            pe.wait_ge(masks_set, 1)
            pe.wait_ge(stack_full, 1)
            pe.wait_ge(stk_in, 64)
            pe.wait_ge(par_in, 160)
            pe.transpose(ps[:, 0, 0:P], stack[:, 0, :], ident[:])
            pe.transpose(ps[:, 0, P:2 * P], stack[:, 1, :], ident[:])
            n2 = NCOLS - P
            pe.transpose(ps[:, 0, 2 * P:2 * P + n2], stack[0:n2, 2, :], ident[0:n2, 0:n2])\
              .then_inc(cols_t, 1)
            pe.wait_ge(bc_in, 16 * BC_DMAS)
            for c in range(2):
                for t in range(4):
                    ins = pe.transpose(ps[:, 1 + c, t * P:(t + 1) * P],
                                       cdup[:, c, t].rearrange("p d s -> p (d s)"), ident[:])
            ins.then_inc(cols_t, 1)
            pe.wait_ge(rx_ready, 2)
            rows = slice(0, TT_ROWS)
            diag = tb[rows]
            for c in range(2):
                ins = pe.matmul(ps[:, 6 + c, 0:HL], ones[rows, :], diag[:, c * HL:(c + 1) * HL],
                                start=True, stop=True)
            ins.then_inc(rb_ps, 1)
            for k in range(KD):
                if k == 1:
                    pe.wait_ge(rb_set, 1)
                if k >= 2:
                    pe.wait_ge(xt_copied, k - 1)
                b = 4 + 2 * (k % 2)
                for i in range(NTT):
                    c0 = (i % 3) * TT_ROWS
                    ins = pe.transpose(ps[:, b + i // 3, c0:c0 + TT_ROWS],
                                       xtok[rows, i, k * P:(k + 1) * P], ident[rows, rows])
                ins.then_inc(xt_ps, 1)

            def norm(i):
                is_k, t, unit = norm_of(i)
                w = HL if is_k else HLL
                pe.wait_ge(sq_ready, i + 1)
                for c in range(2):
                    ins = pe.matmul(ps[:, 4 + c, 0:w], blocks[:], sq[i][:, c * w:(c + 1) * w],
                                    start=True, stop=True)
                ins.then_inc(ss_ps, 1)

            def prep(r):
                pe.wait_ge(g_ready, r + 1)
                for c in range(2):
                    for i in range(RP):
                        ins = pe.transpose(ps[:, 4 + c, i * P:(i + 1) * P],
                                           g_in[:, c, i].rearrange("p j h -> p (j h)"), ident[:])
                ins.then_inc(g_t, 1)
                pe.wait_ge(h_ready, r + 1)
                for g in range(2 * RP):
                    part = slice(ST * (g % 2), ST * (g % 2) + ST)
                    o = ps[0:GH, 6 + g % 2, (g // 2) * P:(g // 2 + 1) * P]
                    for c in range(2):
                        ins = pe.matmul(o, bb[part, c, r * RP + g // 2, :],
                                        hout[part, c, g // 2, 0:T8, :]
                                        .rearrange("p i h -> p (i h)"),
                                        start=c == 0, stop=c == 1)
                ins.then_inc(k_ps, 1)

            def state(r):
                pe.wait_ge(win_set, r + 1)
                pe.wait_ge(u_in[r], 16 * T8)
                for g in range(2 * RP):
                    part = slice(ST * (g % 2), ST * (g % 2) + ST)
                    for c in range(2):
                        w0 = (g // 2) * P + ST * (g % 2)
                        ins = pe.matmul(ps[part, 4 + c, (g // 2) * NC:(g // 2 + 1) * NC],
                                        win[:, c, w0:w0 + ST], uc[:, r % 2, g, :],
                                        start=True, stop=True)
                ins.then_inc(st_ps, 1)

            def readout(r):
                pe.wait_ge(kern_out[r], 16 * T8)
                pe.wait_ge(st_set, r + 1)
                pe.wait_ge(kern_set, r + 1)
                if r:
                    pe.wait_ge(yg_set, r)
                for g in range(2 * RP):
                    o = ps[:, 6 + g // 4, (g % 4) * NC:(g % 4 + 1) * NC]
                    pe.matmul(o, toep[:, g, :], uc[:, r % 2, g, :], start=True, stop=False)
                    for c in range(2):
                        ins = pe.matmul(o, hout[:, c, g // 2, 1:T8 + 1, :]
                                        .rearrange("p i h -> p (i h)"),
                                        xst[:, c, g % 2, g // 2, :], start=False, stop=c == 1)
                ins.then_inc(y_ps, 1)

            def turn_v(t):
                pe.wait_ge(drained, U_V + t + 1)
                for kb in range(5):
                    ins = pe.transpose(ps[:, 4 + kb // 4, (kb % 4) * P:(kb % 4 + 1) * P],
                                       vT[t][:, KEY0[kb]:KEY0[kb] + P], ident[:])
                ins.then_inc(v_t, 1)

            def scores(h):
                pe.wait_ge(kl_set, h // 2 + 1)
                pe.wait_ge(ql_set, h + 1)
                for bank in range(4):
                    mine = [g for g in REGIONS if g[0] == bank]
                    for n, (_, c0, kb, q0, q1) in enumerate(mine):
                        for i, (kk, qq) in enumerate(((kh, qzh), (kh, qzl), (kl, qzh))):
                            pe.matmul(ps[:, 4 + bank, c0:c0 + q1 - q0],
                                      kk[:, KEY0[kb]:KEY0[kb] + P],
                                      qq[h % 2][:, q0 - LATE0:q1 - LATE0],
                                      start=n == 0 and i == 0, stop=False, skip_group_check=True)
                        if kb == 4:
                            ins = pe.matmul(ps[:, 4 + bank, c0:c0 + META], ident_bf[:],
                                            mask_last[:], start=False, stop=True,
                                            skip_group_check=True)
                        elif q0 < KEY0[kb] + P:
                            n_ = KEY0[kb] + P - q0
                            ins = pe.matmul(ps[:, 4 + bank, c0:c0 + n_], ident_bf[:],
                                            mask[:, P - n_:P], start=False, stop=True,
                                            skip_group_check=True)
                ins.then_inc(z_ps, 1)

            def soft_cols(part, region, q0, q1):
                a = BANK_OFF[region[0]] + region[1] + q0 - region[3]
                return part[:, a:a + q1 - q0]

            def suffix(h):
                pe.wait_ge(soft_lo, 2 * h + 2)
                for g in REGIONS:
                    for part in (awh, awl):
                        ins = pe.matmul(ps[:, 4 + g[0], g[1]:g[1] + g[4] - g[3]], negtri[:],
                                        soft_cols(part, g, g[3], g[4]), start=False, stop=True,
                                        skip_group_check=True)
                    for later in REGIONS:
                        q0, q1 = shared_queries(g, later)
                        if later[2] > g[2] and q0 < q1:
                            o = g[1] + q0 - g[3]
                            for part in (awh, awl):
                                ins = pe.matmul(ps[:, 4 + g[0], o:o + q1 - q0], negones[:],
                                                soft_cols(part, later, q0, q1), start=False,
                                                stop=True, skip_group_check=True)
                ins.then_inc(suf_ps, 1)

            def values(h):
                if h == 0:
                    pe.wait_ge(vl_set, 2)
                pe.wait_ge(prob_lo, 2 * h + 2)
                t = h // 2
                for low, bank, origin in ((True, 4, LATE0), (False, 5, Q_SPLIT)):
                    mine = [g for g in REGIONS if (g[4] == Q_SPLIT) == low]
                    for n, g in enumerate(mine):
                        a = BANK_OFF[g[0]] + g[1]
                        for i, (vv, ww) in enumerate(((vh, awh), (vh, awl), (vl, awh))):
                            ins = pe.matmul(ps[:, bank, g[3] - origin:g[4] - origin],
                                            vv[:, g[2], t * P:(t + 1) * P],
                                            ww[:, a:a + g[4] - g[3]], start=n == 0 and i == 0,
                                            stop=n == len(mine) - 1 and i == 2,
                                            skip_group_check=True)
                ins.then_inc(av_ps, 1)

            steps = {"norm": norm, "prep": prep, "state": state, "readout": readout,
                     "scores": scores, "suffix": suffix, "values": values, "turn_v": turn_v}
            used45 = [(xt_copied, KD)]
            used67 = [(xt_copied, KD)]

            def run(name, i):
                if name in ("norm", "turn_v", "prep", "state", "scores"):
                    for s_, n in used45:
                        pe.wait_ge(s_, n)
                if name in ("prep", "readout", "scores"):
                    for s_, n in used67:
                        pe.wait_ge(s_, n)
                steps[name](i)
                if name == "norm":
                    used45[:] = [(ss_v, i + 1)]
                if name == "turn_v":
                    used45[:] = [(vl_set, i + 1)]
                if name == "prep":
                    used45[:] = [(win_set, i + 1)]
                    used67[:] = [(kern_set, i + 1)]
                if name == "state":
                    used45[:] = [(st_set, i + 1)]
                if name == "readout":
                    used67[:] = [(yg_set, i + 1)]
                if name == "values":
                    used45[:] = [(atl_set, i + 1)]
                    used67[:] = []

            def left(unit):
                if unit < U_GATE:
                    return drained, unit + 1
                if is_gate(unit):
                    return gate_raw, gate_of(unit) + 1
                return glu_sig, 2 * (unit - U_GLU) + 2

            for unit in range(U_PROJ):
                slot = unit % 2
                glu = U_GLU <= unit
                pe.wait_ge(lo_ready, unit + 1)
                if unit == 0:
                    pe.wait_ge(cols_set, 1)
                    pe.wait_ge(ct_set, 1)
                if unit >= 2:
                    pe.wait_ge(*left(unit - 2))
                if glu:
                    pe.wait_ge(*left(unit - 1))
                bank = 2 * slot
                x_pair = (xh, xl)
                if glu:
                    pe.wait_ge(gl_set, KS)
                    for mm in range(2):
                        ins = product(slot, mm, KS, 2 * mm, HL, (gh, gl), 0, stride=2)
                else:
                    ready = x_ready if unit == 0 else None
                    width, col0 = (HL, 0) if unit < U_Q else (HLL, LATE0)
                    ins = product(slot, 0, KD, bank, width, x_pair, col0, ready=ready)
                ins.then_inc(unit_done, 1)
                for name, i in STEPS.get(unit, []):
                    if name in steps:
                        run(name, i)

            pe.wait_ge(*left(U_PROJ - 2))
            pe.wait_ge(*left(U_PROJ - 1))
            for m in range(KD):
                unit = U_PROJ + m
                b = 4 * (m % 2)
                pe.wait_ge(lo_ready, unit + 1)
                if m == 0:
                    pe.wait_ge(atl_set, HEADS)
                if m == 1:
                    pe.wait_ge(atl_set, HEADS)
                if m >= 2:
                    pe.wait_ge(m_gated, m - 1)
                product(unit % 2, 0, 2, b, HLL, (atth, attl), 0)
                if m == 0:
                    pe.wait_ge(sl_set, KS)
                product(unit % 2, 2, KS, b + 2, HLL, (sh, sl), LATE0).then_inc(unit_done, 1)
            for m in range(KD):
                unit = U_WO + m
                pe.wait_ge(lo_ready, unit + 1)
                if m < 2:
                    pe.wait_ge(m_gated, KD - 1)
                else:
                    pe.wait_ge(h_set, m - 1)
                product(unit % 2, 0, KD, 2 * (m % 2), HLL, (mh, ml), 0,
                        ready=ml_set if m == 0 else None).then_inc(unit_done, 1)

            def up_unit(f, s, part, ready=None):
                pe.wait_ge(lo_ready, f * 2 + (U_UP + 1 + part))
                if not (isinstance(f, int) and f < 2):
                    pe.wait_ge(up_v, f * 2 + (part - 3))
                product(part, 0, KD, 4 * s + 2 * part, HLL, (xh, xl), 0, ready=ready)\
                    .then_inc(unit_done, 1)

            pe.wait_ge(h_set, KD)
            pe.wait_ge(m_gated, KD)
            up_unit(0, 0, 0, ready=z_ready)
            pe.wait_ge(h_acc, KD)
            for c in range(2):
                ins = pe.matmul(ps[:, 4 + c, 0:HLL], ones[:], acc[:, c * HLL:(c + 1) * HLL],
                                start=True, stop=True)
            ins.then_inc(ss2_ps, 1)
            up_unit(0, 0, 1)
            pe.wait_ge(ss2_v, 1)
            up_unit(1, 1, 0)
            up_unit(1, 1, 1)
            with pe.Fori(1, KF // 2) as ff:
                for s in range(2):
                    for part in range(2):
                        up_unit(ff * 2 + s, s, part)

            def turn(m, s):
                pe.wait_ge(y_add, m + 1)
                if not (isinstance(m, int) and m < 2):
                    pe.wait_ge(yt_set, m - 1)
                for t in range(4):
                    ins = pe.transpose(ps[:, 4 + s, t * P:(t + 1) * P], yo[s][:, t * P:(t + 1) * P],
                                       ident[:])
                ins.then_inc(yt_ps, 1)

            def down(m, s):
                if isinstance(m, int) and m < 2:
                    pe.wait_ge(up_v, 2 * KF - 2 + 2 * m)
                else:
                    pe.wait_ge(y_add, m - 1)
                for half in range(2):
                    pe.wait_ge(lo_ready, m * 2 + (U_DOWN + 1 + half))
                    for i in range(UT):
                        k = half * UT + i
                        if isinstance(m, int) and m == 0:
                            pe.wait_ge(al_set, k + 1)
                        ins = three([ps[:, s, :]], wtile(half, i),
                                    lambda a, c: (ah, al)[a][:, k, :], k == 0, k == KF - 1)
                    ins.then_inc(unit_done, 1)
                    if half == 0 and not (isinstance(m, int) and m == 0):
                        turn(m - 1, 1 - s)

            down(0, 0)
            down(1, 1)
            with pe.Fori(1, KD // 2) as mm:
                for s in range(2):
                    down(mm * 2 + s, s)
            turn(KD - 1, 1)


_INS = ["x", "meta_tokens", "norm1_g", "w_in", "q_norm_g", "k_norm_g", "ssm_a_re", "ssm_a_im",
        "ssm_log_step", "ssm_b_re", "ssm_b_im", "ssm_c_re", "ssm_c_im", "ssm_d", "w_glu", "b_glu",
        "w_attn_proj", "w_ssm_proj", "w_o", "norm2_g", "w_up", "conv_w", "conv_b", "w_down"]


def kernel(**inputs):
    import numpy as _np
    import concourse.bacc as _bacc
    from concourse import mybir as _mybir
    from concourse.bass_utils import run_bass_kernel_spmd as _run

    nc = _bacc.Bacc("TRN2", target_bir_lowering=False, num_devices=1)
    arrays, args = {}, []
    for name in _INS:
        a = _np.ascontiguousarray(inputs[name])
        arrays[f"in_{name}_dram"] = a
        args.append(nc.dram_tensor(f"in_{name}_dram", a.shape, _mybir.dt.from_np(a.dtype),
                                   kind="ExternalInput").ap())
    args.append(nc.dram_tensor("out_0_dram", (1, SEQ, D), F32, kind="ExternalOutput").ap())
    hybrid_trunk(nc, *args)
    return _run(nc, [arrays], core_ids=[0]).results[0]["out_0_dram"]
```

```python
from contextlib import ExitStack

import concourse.bass as bass
from concourse import mybir

F32 = mybir.dt.float32
F32R = mybir.dt.float32r
BF16 = mybir.dt.bfloat16
ALU = mybir.AluOpType
ACT = mybir.ActivationFunctionType

P = 128
D = 1024
SEQ = 512
META = 16
L = META + SEQ
LATE0 = 12
LL = L - LATE0
HL, HLL = L // 2, LL // 2
KD = D // P
HEADS, DH = 4, 64
SBW = HEADS * DH
SW = 512
GROUPS, GH, ST = 32, 16, 64
KS = SW // P
PAIRS = GROUPS // 2
FFN = 2816
KF = FFN // P
EPS = 1e-6
TT_ROWS = 88
NTT = L // TT_ROWS
T8 = 8
NC = L // T8
RP = PAIRS // 4
ROUNDS = 4
UT = 11
NEG = -1e30
TWO_PI = 6.283185307179586
CW1 = 6.28125
CW2 = 0.0019350051879882812
CW3 = 3.019916050773725e-07
ROUND_MAGIC = 12582912.0
PI_BELOW = 3.1415925
A_RE_MAX = -1e-4
BC_DMAS = 6
PAR_DMAS = 9
STK_DMAS = 4
Q_LAST = 512

(S_STEP, S_MAG, S_SIN, S_SINH, S_COS, S_TH, S_LST, S_LRE, S_N, S_FR, S_FI, S_D2, S_D4, S_DEN, S_NR,
 S_T1, S_T2) = range(17)

U_SSM, U_K, U_V, U_Q, U_GATE, U_GLU, U_PROJ, U_WO, U_UP, U_DOWN, U_END = \
    0, 4, 6, 8, 10, 26, 28, 36, 44, 88, 104

KEY0 = (0, 128, 256, 384, 400)
REGIONS = ((0, 0, 0, 12, 256), (0, 244, 1, 128, 256),
           (1, 0, 0, 256, 528), (2, 0, 1, 256, 528),
           (3, 0, 2, 256, 528), (3, 272, 3, 384, 528), (3, 416, 4, 512, 528))
BANK_COLS = (372, 272, 272, 432)
BANK_OFF = (0, 372, 644, 916)
ATT_COLS = 1348
AB = 4
BANKS = (2, 3, 0, 1)
Q_SPLIT = 256

STEPS = {0: [("spread", 0), ("columns", 0), ("small", 0)],
         1: [("columns", 1), ("powers", 0)], 2: [("b_factor", 0)], 5: [("norm", 0), ("prep", 0)],
         6: [("norm", 1), ("turn_v", 0)], 7: [("turn_v", 1), ("turns", 0), ("state", 0)],
         8: [("prep", 1)], 9: [("norm", 2), ("readout", 0)],
         10: [("norm", 3), ("state", 1)], 11: [("prep", 2)], 12: [("readout", 1)],
         13: [("state", 2)], 14: [("prep", 3)], 15: [("readout", 2)],
         16: [("state", 3)], 17: [("readout", 3)],
         18: [("scores", 0)], 19: [("suffix", 0)], 20: [("values", 0), ("scores", 1)],
         21: [("suffix", 1)], 22: [("values", 1), ("scores", 2), ("gelu", 0)],
         23: [("suffix", 2), ("gelu", 1)], 24: [("values", 2), ("scores", 3)],
         25: [("suffix", 3)], 26: [("values", 3)]}
MOVES = {2: [("u_write", 0)], 3: [("u_write", 1)], 4: [("u_write", 2), ("u_read", 0)],
         5: [("u_write", 3), ("u_read", 1)], 6: [("toep", 0)], 10: [("y_write", 0), ("toep", 1)],
         11: [("u_read", 2)], 13: [("y_write", 1), ("toep", 2)], 14: [("u_read", 3)],
         16: [("y_write", 2), ("toep", 3)], 19: [("y_write", 3)], 20: [("y_read", 0)]}

ROW_ARE, ROW_AIM, ROW_STEP, ROW_SKIP = 0, 32, 64, 96
COL_CW, COL_CB, COL_N2, COL_BG, COL_QG, COL_KG, NCOLS = 0, 132, 176, 184, 188, 189, 190


def norm_of(i):
    return (True, i, U_K + i) if i < 2 else (False, i - 2, U_Q + i - 2)


def gate_of(unit):
    return unit - U_GATE


def is_gate(unit):
    return U_GATE <= unit < U_GLU


def bank_cols(b):
    return slice(BANK_OFF[b], BANK_OFF[b] + BANK_COLS[b])


def shared_queries(region, other):
    return max(region[3], other[3]), min(region[4], other[4])


def hybrid_trunk(nc, x, meta_tokens, norm1_g, w_in, q_norm_g, k_norm_g, ssm_a_re, ssm_a_im,
                 ssm_log_step, ssm_b_re, ssm_b_im, ssm_c_re, ssm_c_im, ssm_d, w_glu, b_glu,
                 w_attn_proj, w_ssm_proj, w_o, norm2_g, w_up, conv_w, conv_b, w_down, out):
    u_dram = nc.dram_tensor("u_dram", (SW, T8, NC), F32, kind="Internal").ap()
    y_dram = nc.dram_tensor("y_dram", (SW, T8, NC), F32, kind="Internal").ap()

    ctx = ExitStack()
    with ctx:
        def alloc(stack, name, shape, dt=F32):
            return stack.enter_context(nc.sbuf_tensor(name, shape, dt))

        def sb(name, shape, dt=F32):
            return alloc(ctx, name, shape, dt)

        def sem(name):
            return ctx.enter_context(nc.semaphore(name))

        ps = ctx.enter_context(nc.psum_tensor("ps", [P, 8, 512], F32))

        raw = [sb(f"raw{i}", [P, UT * P]) for i in range(2)]
        hi = [sb(f"hi{i}", [P, UT * P], F32R) for i in range(2)]
        lo = [sb(f"lo{i}", [P, UT * P], F32R) for i in range(2)]
        xh = sb("xh", [P, KD, L], F32R)
        xl = sb("xl", [P, KD, L], F32R)
        hT = sb("hT", [P, KD, L])
        ident = sb("ident", [P, P])
        ones = sb("ones", [P, P])
        cols = sb("cols", [P, NCOLS])
        rb = sb("rb", [P, L])

        start = ExitStack()
        xtok = alloc(start, "xtok", [P, NTT, D])
        stack = alloc(start, "stack", [P, 3, P])
        gain = alloc(start, "gain", [KD, P])
        cdup = alloc(start, "cdup", [P, 2, 4, 2, ST])
        start.close()

        mix = ExitStack()
        gates = alloc(mix, "gates", [P, 16 * LL])
        ta, tb, sq0, sq1 = (gates[:, 16 * LL - (i + 1) * L:16 * LL - i * L] for i in range(4))
        sq = [sq0, sq1]
        hout_end = 16 * LL - 4 * L
        HOUT = 2 * RP * (T8 + 1) * GH
        vT = [gates[:, i * L:(i + 1) * L] for i in range(2)]
        gate = [gates[:, i * LL:(i + 1) * LL] for i in range(16)]
        qk = ExitStack()
        qT = alloc(qk, "qT", [P, 2, L])
        kT = alloc(qk, "kT", [P, 2, L])
        qk.close()
        ma = [alloc(mix, f"ma{i}", [P, LL]) for i in range(2)]
        mb = [alloc(mix, f"mb{i}", [P, LL]) for i in range(2)]
        pad = alloc(mix, "pad", [P, 4 * (L - LL)])
        vh = alloc(mix, "vh", [P, 5, SBW], F32R)
        vl = alloc(mix, "vl", [P, 5, SBW], F32R)
        atth = alloc(mix, "atth", [P, 2, LL], F32R)
        attl = alloc(mix, "attl", [P, 2, LL], F32R)
        blocks = alloc(mix, "blocks", [P, P])
        negtri = alloc(mix, "negtri", [P, P], F32R)
        negones = alloc(mix, "negones", [P, P], F32R)
        ident_bf = alloc(mix, "ident_bf", [P, P], BF16)
        mask = alloc(mix, "mask", [P, P], BF16)
        mask_last = alloc(mix, "mask_last", [P, META], BF16)
        g1 = alloc(mix, "g1", [P, KD])

        early = ExitStack()
        turning = ExitStack()
        uy = alloc(turning, "uy", [P, 2, T8, NC])
        turning.close()
        mod = alloc(early, "mod", [P, 4, RP, NC])
        uc = alloc(early, "uc", [P, 2, 2 * RP, NC])
        given = ExitStack()
        braw = alloc(given, "braw", [P, 2, PAIRS, GH])
        given.close()
        yg = alloc(early, "yg", [P, 2 * RP, NC])
        rot = alloc(early, "rot", [P, 2, PAIRS, NC])
        decay = alloc(early, "decay", [P, PAIRS, NC])
        g_in = alloc(early, "g_in", [P, 2, RP, T8, GH])
        win = alloc(early, "win", [P, 2, RP * P])
        hout = [gates[:, hout_end - (2 - i) * HOUT:hout_end - (1 - i) * HOUT]
                .rearrange("p (c r n h) -> p c r n h", c=2, r=RP, h=GH) for i in range(2)]
        kern = alloc(early, "kern", [GH, 2 * RP, P])
        toep = alloc(early, "toep", [P, 2 * RP, P])
        xst = alloc(early, "xst", [P, 2, 2, RP, NC])
        skip_i = alloc(early, "skip_i", [GH, GROUPS, GH])
        colc = alloc(early, "colc", [P, P])
        sm = alloc(early, "sm", [P, 17, PAIRS])
        pw = alloc(early, "pw", [P, 2, T8 + 1, PAIRS])
        en = alloc(early, "en", [P, 7, 2, PAIRS])
        bb = alloc(early, "bb", [P, 2, PAIRS, GH])
        bpair = alloc(early, "bpair", [P, 2, PAIRS, 3 * GH])
        ct = alloc(early, "ct", [P, 2, PAIRS, GH])
        pt = alloc(early, "pt", [P, RP * (T8 + 1) * GH])
        lst = alloc(early, "lst", [P, 2])
        early.close()
        scr = ExitStack()
        under = ExitStack()
        yT = alloc(under, "yT", [P, KS, T8, NC])
        gh = alloc(under, "gh", [P, KS, L], F32R)
        gl = alloc(under, "gl", [P, KS, L], F32R)
        aw = alloc(under, "aw", [P, ATT_COLS])
        awh = alloc(under, "awh", [P, ATT_COLS], F32R)
        under.close()
        mh = alloc(scr, "mh", [P, KD, LL], F32R)
        ml = alloc(scr, "ml", [P, KD, LL], F32R)
        pad2 = alloc(scr, "pad2", [P, 3 * KS * L + 2 * ATT_COLS - 2 * KD * LL + 16])
        heads = ExitStack()
        awl = alloc(heads, "awl", [P, ATT_COLS], F32R)
        qzl = [alloc(heads, f"qzl{i}", [P, LL], F32R) for i in range(2)]
        kh = alloc(heads, "kh", [P, L], F32R)
        kl = alloc(heads, "kl", [P, L], F32R)
        heads.close()
        sh = alloc(scr, "sh", [P, KS, L], F32R)
        sl = alloc(scr, "sl", [P, KS, L], F32R)
        gt = [alloc(scr, f"gt{i}", [P, L]) for i in range(2)]
        qzh = [alloc(scr, f"qzh{i}", [P, LL], F32R) for i in range(2)]
        scr.close()
        mix.close()

        late = ExitStack()
        sqh = [alloc(late, f"sqh{i}", [P, LL]) for i in range(2)]
        acc = alloc(late, "acc", [P, LL])
        nv = alloc(late, "nv", [P, LL])
        ut = [alloc(late, f"ut{i}", [P, 2, LL]) for i in range(2)]
        cv = [alloc(late, f"cv{i}", [P, 2, SEQ]) for i in range(2)]
        ah = alloc(late, "ah", [P, KF, SEQ], F32R)
        al = alloc(late, "al", [P, KF, SEQ], F32R)
        late.close()
        fin = ExitStack()
        yo = [alloc(fin, f"yo{i}", [P, SEQ]) for i in range(2)]
        yt = [alloc(fin, f"yt{i}", [P, 4, P]) for i in range(2)]
        fin.close()

        raw_in = [sem(f"raw_in{i}") for i in range(2)]
        hi_ready = sem("hi_ready")
        lo_ready = sem("lo_ready")
        unit_done = sem("unit_done")
        drained = sem("drained")
        par_in = sem("par_in")
        stk_in = sem("stk_in")
        bc_in = sem("bc_in")
        x_in = [sem(f"x_in{i}") for i in range(3)]
        masks_set = sem("masks_set")
        stack_zero = sem("stack_zero")
        gain_in = sem("gain_in")
        stack_full = sem("stack_full")
        cols_t = sem("cols_t")
        g1_set = sem("g1_set")
        cols_set = sem("cols_set")
        xt_ps = sem("xt_ps")
        xt_copied = sem("xt_copied")
        xh_set = sem("xh_set")
        x_ready = sem("x_ready")
        x_sq = sem("x_sq")
        x_acc = sem("x_acc")
        rb_ps = sem("rb_ps")
        rb_v = sem("rb_v")
        rb_a = sem("rb_a")
        rb_set = sem("rb_set")
        small_a = sem("small_a")
        small_v = sem("small_v")
        ct_set = sem("ct_set")
        pw_set = sem("pw_set")
        b_set = sem("b_set")
        rot_set = sem("rot_set")
        g_ready = sem("g_ready")
        h_ready = sem("h_ready")
        g_t = sem("g_t")
        k_ps = sem("k_ps")
        win_set = sem("win_set")
        kern_set = sem("kern_set")
        kern_out = [sem(f"kern_out{i}") for i in range(ROUNDS)]
        u_out = [sem(f"u_out{i}") for i in range(ROUNDS)]
        u_in = [sem(f"u_in{i}") for i in range(ROUNDS)]
        y_out = [sem(f"y_out{i}") for i in range(ROUNDS)]
        y_in = sem("y_in")
        st_ps = sem("st_ps")
        st_read = sem("st_read")
        st_set = sem("st_set")
        y_ps = sem("y_ps")
        yg_set = sem("yg_set")
        v_t = sem("v_t")
        vh_set = sem("vh_set")
        vl_set = sem("vl_set")
        sq_ready = sem("sq_ready")
        ss_ps = sem("ss_ps")
        ss_v = sem("ss_v")
        rs_a = sem("rs_a")
        normed = sem("normed")
        qz_zero = sem("qz_zero")
        kh_set = sem("kh_set")
        kl_set = sem("kl_set")
        qh_set = sem("qh_set")
        ql_set = sem("ql_set")
        z_ps = sem("z_ps")
        z_part = sem("z_part")
        z_abs = sem("z_abs")
        z_ln = sem("z_ln")
        soft_set = sem("soft_set")
        soft_hi = sem("soft_hi")
        soft_lo = sem("soft_lo")
        suf_ps = sem("suf_ps")
        prob_set = sem("prob_set")
        prob_hi = sem("prob_hi")
        prob_lo = sem("prob_lo")
        av_ps = sem("av_ps")
        ath_set = sem("ath_set")
        atl_set = sem("atl_set")
        gate_raw = sem("gate_raw")
        gate_set = sem("gate_set")
        gh_set = sem("gh_set")
        gl_set = sem("gl_set")
        glu_sig = sem("glu_sig")
        glu_val = sem("glu_val")
        sh_set = sem("sh_set")
        sl_set = sem("sl_set")
        m_gated = sem("m_gated")
        m_sum = sem("m_sum")
        mh_set = sem("mh_set")
        ml_set = sem("ml_set")
        h_set = sem("h_set")
        h_sq = sem("h_sq")
        h_acc = sem("h_acc")
        zh_set = sem("zh_set")
        z_ready = sem("z_ready")
        ss2_ps = sem("ss2_ps")
        ss2_v = sem("ss2_v")
        r2_a = sem("r2_a")
        r2_set = sem("r2_set")
        up_v = sem("up_v")
        cv_a = sem("cv_a")
        cv_mid = sem("cv_mid")
        cv_v = sem("cv_v")
        silu_a = sem("silu_a")
        act_p = sem("act_p")
        ah_set = sem("ah_set")
        al_set = sem("al_set")
        y_add = sem("y_add")
        yt_ps = sem("yt_ps")
        yt_set = sem("yt_set")
        out_done = [sem(f"out_done{i}") for i in range(2)]
        act_link = sem("act_link")
        dve_link = sem("dve_link")
        pool_link = sem("pool_link")

        def psum2(bank, width, part=slice(0, P)):
            return ps[part, bank:bank + 2, 0:width]

        def halves(ap, width):
            return ap.rearrange("p (b c) -> p b c", c=width)

        def linker(eng, link):
            count = [0]

            def wait_for(ins):
                count[0] += 1
                ins.then_inc(link, 1)
                eng.wait_ge(link, count[0])
            return wait_for

        def both(ap):
            return ap[:, 0], ap[:, 1]

        def cmul(eng, link, o, a, b, t):
            link(eng.tensor_tensor(o[0], a[0], b[0], ALU.mult))
            link(eng.tensor_tensor(t, a[1], b[1], ALU.mult))
            link(eng.tensor_tensor(o[0], o[0], t, ALU.subtract))
            link(eng.tensor_tensor(o[1], a[0], b[1], ALU.mult))
            link(eng.tensor_tensor(t, a[1], b[0], ALU.mult))
            link(eng.tensor_tensor(o[1], o[1], t, ALU.add))

        def extend_turns(eng, link, j, t):
            n = 1 << j
            w = min(n, NC - n)
            shape = [P, PAIRS, w]
            cmul(eng, link, [rot[:, c, :, n:n + w] for c in range(2)],
                 [rot[:, c, :, 0:w] for c in range(2)],
                 [en[:, j, c].unsqueeze(2).broadcast_to(shape) for c in range(2)],
                 t[:, 0:PAIRS * w].rearrange("p (r c) -> p r c", c=w))

        def move_taps(eng, r):
            eng.wait_ge(kern_set, r + 1)
            if r:
                eng.wait_ge(y_ps, r)
            eng.wait_ge(masks_set, 3)
            for j in range(T8):
                p0 = GH * (T8 - 1 - j)
                eng.dma_start(toep[p0:p0 + GH, :, GH * j:P],
                              kern[:, :, 0:P - GH * j]).then_inc(kern_out[r], 16)

        block = ctx.enter_context(nc.Block())

        @block.sync
        def _(sp):
            def in_cols(c0):
                return w_in[0].rearrange("(k p) c -> p k c", p=P)[:, :, c0:c0 + P]

            def load(slot, parts):
                at = 0
                for src in parts:
                    n = src.shape[1] * src.shape[2]
                    sp.dma_start(raw[slot][:, at:at + n].rearrange("p (k c) -> p k c", c=src.shape[2]),
                                 src).then_inc(raw_in[slot], 16)
                    at += n

            def halved(src):
                k = src.shape[1]
                return [src[:, 0:(k + 1) // 2, :], src[:, (k + 1) // 2:k, :]]

            def source(unit):
                if unit < U_K:
                    return halved(in_cols(3 * SBW + P * unit))
                if unit < U_V:
                    return halved(in_cols(SBW + P * (unit - U_K)))
                if unit < U_Q:
                    return halved(in_cols(2 * SBW + P * (unit - U_V)))
                if unit < U_GATE:
                    return halved(in_cols(P * (unit - U_Q)))
                if is_gate(unit):
                    return halved(in_cols(3 * SBW + SW + P * gate_of(unit)))
                if unit < U_PROJ:
                    c0 = 2 * P * (unit - U_GLU)
                    return halved(w_glu[0].rearrange("(k p) c -> p k c", p=P)[:, :, c0:c0 + 2 * P])
                if unit < U_WO:
                    c0 = P * (unit - U_PROJ)
                    return [w[0].rearrange("(k p) c -> p k c", p=P)[:, :, c0:c0 + P]
                            for w in (w_attn_proj, w_ssm_proj)]
                c0 = P * (unit - U_WO)
                return halved(w_o[0].rearrange("(k p) c -> p k c", p=P)[:, :, c0:c0 + P])

            def up_source(f, part):
                src = w_up[0].rearrange("(k p) c -> p k c", p=P)
                return halved(src[:, :, bass.ds(f * P + part * FFN, P)])

            def down_source(m, half):
                src = w_down[0].rearrange("(k p) c -> p k c", p=P)[:, half * UT:(half + 1) * UT, :]
                return halved(src[:, :, bass.ds(m * P, P)])

            sp.dma_start(xtok[META:TT_ROWS, 0, :], x[0, 0:TT_ROWS - META, :]).then_inc(x_in[0], 16)
            sp.dma_start(xtok[0:META, 0, :], meta_tokens).then_inc(x_in[0], 16)
            rest = x[0, TT_ROWS - META:SEQ, :].rearrange("(i p) d -> p i d", p=TT_ROWS)
            for i in range(2):
                sp.dma_start(xtok[0:TT_ROWS, 1 + i, :], rest[:, i, :]).then_inc(x_in[1], 16)
            sp.dma_start(xtok[0:TT_ROWS, 3:NTT, :], rest[:, 2:NTT - 1, :]).then_inc(x_in[2], 16)
            load(0, source(0))
            load(1, source(1))
            for c, (b_in, c_in) in enumerate(((ssm_b_re, ssm_c_re), (ssm_b_im, ssm_c_im))):
                sp.dma_start(braw[:, c], b_in[0].rearrange("(r g) p h -> (g p) r h", g=2))\
                    .then_inc(bc_in, 16)
                for d in range(2):
                    sp.dma_start(cdup[:, c, :, d, :],
                                 c_in[0].rearrange("(t g) h p -> (g h) t p", g=8)).then_inc(bc_in, 16)
            rows = [(stack[:, 1, :], conv_w[0].rearrange("j (m c) -> (j m) c", c=P)[0:P, :]),
                    (stack[0:4, 2, :], conv_w[0].rearrange("j (m c) -> (j m) c", c=P)[P:P + 4, :]),
                    (stack[4:48, 2, :], conv_b[0].rearrange("(m c) -> m c", c=P)),
                    (stack[48:56, 2, :], norm2_g[0].rearrange("(m c) -> m c", c=P)),
                    (stack[56:60, 2, :], b_glu[0].rearrange("(m c) -> m c", c=P)),
                    (stack[60:61, 2, 0:DH], q_norm_g), (stack[60:61, 2, DH:P], q_norm_g),
                    (stack[61:62, 2, 0:DH], k_norm_g), (stack[61:62, 2, DH:P], k_norm_g)]
            for dst, src in rows:
                sp.dma_start(dst, src).then_inc(par_in, 16)

            def u_write(r):
                sp.wait_ge(drained, r + 1)
                sp.dma_start(u_dram[r * P:(r + 1) * P], uy[:, r % 2]).then_inc(u_out[r], 16)

            def u_read(r):
                sp.wait_ge(u_out[r], 16)
                if r >= 2:
                    sp.wait_ge(y_ps, r - 1)
                src = u_dram[r * P:(r + 1) * P].rearrange("(g h) j c -> j h g c", h=GH)
                for j in range(T8):
                    p0 = GH * (T8 - 1 - j)
                    sp.dma_start(uc[p0:p0 + GH, r % 2], src[j]).then_inc(u_in[r], 16)

            def toep_move(r):
                move_taps(sp, r)

            def y_write(r):
                sp.wait_ge(yg_set, r + 1)
                dst = y_dram[r * P:(r + 1) * P].rearrange("(g h) j c -> j h g c", h=GH)
                for j in range(T8):
                    sp.dma_start(dst[j], yg[GH * j:GH * (j + 1)]).then_inc(y_out[r], 16)

            def y_read(_):
                for r in range(ROUNDS):
                    sp.wait_ge(y_out[r], 16 * T8)
                sp.wait_ge(st_set, ROUNDS)
                sp.wait_ge(y_ps, ROUNDS)
                sp.dma_start(yT[:], y_dram.rearrange("(r p) j c -> p r j c", p=P)).then_inc(y_in, 16)

            move = {"u_write": u_write, "u_read": u_read, "toep": toep_move, "y_write": y_write,
                    "y_read": y_read}
            for done in range(U_UP - 2):
                sp.wait_ge(lo_ready, done + 1)
                load((done + 2) % 2, source(done + 2))
                for name, r in MOVES.get(done, []):
                    move[name](r)

            with sp.Fori(0, KF) as f:
                for part in range(2):
                    sp.wait_ge(lo_ready, f * 2 + (U_UP - 1 + part))
                    load(part, up_source(f, part))

            def store(m, s):
                sp.wait_ge(yt_set, m + 1)
                dst = out[0].rearrange("(t p) c -> p t c", p=P)[:, :, bass.ds(m * P, P)]
                sp.dma_start(dst, yt[s][:]).then_inc(out_done[s], 16)

            def down_load(m):
                for half in range(2):
                    sp.wait_ge(lo_ready, m * 2 + (U_DOWN - 1 + half))
                    load(half, down_source(m, half))

            down_load(0)
            down_load(1)
            with sp.Fori(1, KD // 2) as mm:
                for s in range(2):
                    down_load(mm * 2 + s)
                    store(mm * 2 + (s - 2), s)
            for s in range(2):
                store(KD - 2 + s, s)
            for s in range(2):
                sp.wait_ge(out_done[s], 16 * KD // 2)

        @block.gpsimd
        def _(pool):
            link = linker(pool, pool_link)
            pool.memset(stack[:, 0, :], 0.0).then_inc(stack_zero, 1)
            link(pool.memset(ident[:], 0.0))
            link(pool.affine_select(out=ident[:], in_=ident[:], compare_op=ALU.not_equal, fill=1.0,
                                    base=0, pattern=[[-1, P]], channel_multiplier=1))
            pool.memset(ones[:], 1.0).then_inc(masks_set, 1)
            pool.wait_ge(masks_set, 1)
            link(pool.memset(rot[:, 0, :, 0:1], 1.0))
            link(pool.memset(rot[:, 1, :, 0:1], 0.0))
            link(pool.memset(pw[:, 0, 0, :], 1.0))
            link(pool.memset(bpair[:], 0.0))
            link(pool.memset(blocks[:], 0.0))
            link(pool.memset(blocks[0:DH, 0:DH], 1.0))
            link(pool.memset(blocks[DH:P, DH:P], 1.0))
            pool.memset(pw[:, 1, 0, :], 0.0).then_inc(masks_set, 1)
            pool.wait_ge(masks_set, 2)
            link(pool.memset(toep[:], 0.0))
            link(pool.memset(decay[:], 0.0))
            pool.memset(xst[:], 0.0).then_inc(masks_set, 1)
            pool.wait_ge(masks_set, 3)
            for k in range(KD):
                pool.wait_ge(xt_copied, k + 1)
                if k >= 2:
                    pool.wait_ge(x_acc, k - 1)
                pool.tensor_tensor(kT[:, k % 2], hT[:, k], hT[:, k], ALU.mult).then_inc(x_sq, 1)

            def tmp(*shape):
                n = 1
                for s in shape:
                    n *= s
                v = pt[:, 0:n]
                if len(shape) == 1:
                    return v
                if len(shape) == 2:
                    return v.rearrange("p (a b) -> p a b", b=shape[1])
                return v.rearrange("p (a b c) -> p a b c", b=shape[1], c=shape[2])

            def square(o, a):
                o, a = en[:, o], en[:, a]
                t = tmp(3, PAIRS)
                pool.tensor_tensor(t[:, 0:2], a, a, ALU.mult)
                link(pool.tensor_tensor(t[:, 2], a[:, 0], a[:, 1], ALU.mult))
                pool.tensor_tensor(o[:, 0], t[:, 0], t[:, 1], ALU.subtract)
                link(pool.tensor_scalar(o[:, 1], t[:, 2], 2.0, None, ALU.mult))

            pool.wait_ge(small_v, 3)
            pool.tensor_copy(en[:, 1, 0], sm[:, S_COS, :])
            link(pool.tensor_copy(en[:, 1, 1], sm[:, S_SIN, :]))
            square(2, 1)
            square(1, 2)
            square(0, 1)

            def input_map(r):
                if r:
                    pool.wait_ge(g_t, r)
                pr = slice(r * RP, (r + 1) * RP)
                shape = [P, RP, T8, GH]
                cmul(pool, link, both(g_in),
                     [pw[:, c, 0:T8, pr].rearrange("p n r -> p r n").unsqueeze(3)
                      .broadcast_to(shape) for c in range(2)],
                     [bb[:, c, pr, :].unsqueeze(2).broadcast_to(shape) for c in range(2)],
                     tmp(RP, T8, GH))
                pool.nop().then_inc(g_ready, 1)

            def output_map(r):
                if r >= 2:
                    pool.wait_ge(y_ps, r - 1)
                pr = slice(r * RP, (r + 1) * RP)
                shape = [P, RP, T8 + 1, GH]
                a = [pw[:, c, :, pr].rearrange("p n r -> p r n").unsqueeze(3).broadcast_to(shape)
                     for c in range(2)]
                b = [ct[:, c, pr, :].unsqueeze(2).broadcast_to(shape) for c in range(2)]
                t = tmp(RP, T8 + 1, GH)
                o = both(hout[r % 2])
                link(pool.tensor_tensor(o[0], a[0], b[0], ALU.mult))
                link(pool.tensor_tensor(t, a[1], b[1], ALU.mult))
                link(pool.tensor_tensor(o[0], o[0], t, ALU.add))
                link(pool.tensor_tensor(o[1], a[0], b[1], ALU.mult))
                link(pool.tensor_tensor(t, a[1], b[0], ALU.mult))
                link(pool.tensor_tensor(o[1], o[1], t, ALU.subtract))
                pool.nop().then_inc(h_ready, 1)

            for j in range(6):
                square(j + 1, j)
            pool.wait_ge(pw_set, 1)
            pool.wait_ge(b_set, 1)
            input_map(0)
            pool.wait_ge(ct_set, 1)
            output_map(0)
            for j in range(5):
                extend_turns(pool, link, j, pt)
            pool.nop().then_inc(rot_set, 1)
            pool.wait_ge(rot_set, 1)
            input_map(1)
            output_map(1)
            tri = pt[:, 0:P]
            link(pool.memset(tri, -1.0))
            link(pool.tensor_copy(negones[:], tri))
            link(pool.affine_select(out=tri, in_=tri, compare_op=ALU.is_ge, fill=0.0,
                                    base=0, pattern=[[-1, P]], channel_multiplier=1))
            link(pool.tensor_copy(negtri[:], tri))
            link(pool.tensor_copy(ident_bf[:], ident[:]))
            link(pool.memset(mask[:], NEG))
            link(pool.affine_select(out=mask[:], in_=mask[:], compare_op=ALU.is_ge, fill=0.0,
                                    base=0, pattern=[[-1, P]], channel_multiplier=1))
            first = Q_LAST - KEY0[4]
            link(pool.memset(mask_last[:], 0.0))
            link(pool.affine_select(out=mask_last[:], in_=mask_last[:], compare_op=ALU.is_ge,
                                    fill=NEG, base=-first, pattern=[[0, META]],
                                    channel_multiplier=1))
            pool.affine_select(out=mask_last[:], in_=mask_last[:], compare_op=ALU.is_gt,
                               fill=NEG, base=first, pattern=[[1, META]],
                               channel_multiplier=-1).then_inc(masks_set, 1)
            pool.wait_ge(masks_set, 4)

            for unit in range(U_PROJ):
                for name, i in STEPS.get(unit, []):
                    if name == "prep" and 1 <= i < ROUNDS - 1:
                        input_map(i + 1)
                        output_map(i + 1)
                    if name == "readout" and i + 1 == ROUNDS:
                        pool.wait_ge(y_ps, ROUNDS)
                        pool.wait_ge(yg_set, ROUNDS)
                        for part, i in ((slice(DH, P), 0), (slice(0, DH), 1)):
                            for q in (qzh[i], qzl[i]):
                                link(pool.memset(q[part, :].bitcast(F32), 0.0))
                        pool.nop().then_inc(qz_zero, 1)
            for m in range(KD):
                pool.wait_ge(m_gated, m + 1)
                pool.tensor_tensor(ma[m % 2][:], ma[m % 2][:], mb[m % 2][:], ALU.add)\
                    .then_inc(m_sum, 1)
            for m in range(KD):
                pool.wait_ge(h_sq, m + 1)
                if m == 0:
                    pool.tensor_copy(acc[:], sqh[0][:]).then_inc(h_acc, 1)
                else:
                    pool.wait_ge(h_acc, m)
                    pool.tensor_tensor(acc[:], acc[:], sqh[m % 2][:], ALU.add).then_inc(h_acc, 1)

            def product(f, s):
                pool.wait_ge(silu_a, f + 1)
                pool.wait_ge(cv_v, f * 2 + 2)
                pool.tensor_tensor(cv[s][:, 1], cv[s][:, 0], cv[s][:, 1], ALU.mult)\
                    .then_inc(act_p, 1)

            with pool.Fori(0, KF // 2) as ff:
                for s in range(2):
                    product(ff * 2 + s, s)

        @block.scalar
        def _(act):
            link = linker(act, act_link)

            def split(unit, slot, n):
                act.wait_ge(raw_in[slot], (unit - slot) * 16 + 32)
                if not isinstance(unit, int) or unit >= 2:
                    act.wait_ge(unit_done, unit - 1)
                act.activation(hi[slot][:, 0:n * P], raw[slot][:, 0:n * P], ACT.Copy)\
                    .then_inc(hi_ready, 1)

            act.dma_start(gain[:], norm1_g[0].rearrange("(m c) -> m c", c=P)).then_inc(gain_in, 16)
            act.dma_start(lst[ROW_STEP:ROW_STEP + PAIRS, :],
                          ssm_log_step[0].rearrange("(r g) -> r g", g=2)).then_inc(stk_in, 16)
            act.wait_ge(stack_zero, 1)
            act.dma_start(stack[ROW_ARE:ROW_ARE + PAIRS, 0, :],
                          ssm_a_re[0].rearrange("(r g) p -> r (g p)", g=2)).then_inc(stk_in, 16)
            act.dma_start(stack[ROW_AIM:ROW_AIM + PAIRS, 0, :],
                          ssm_a_im[0].rearrange("(r g) p -> r (g p)", g=2)).then_inc(stk_in, 16)
            act.dma_start(stack[ROW_SKIP:ROW_SKIP + GROUPS, 0, 0:GH], ssm_d[0])\
                .then_inc(stk_in, 16)
            act.preload_act_table_set("natural_log_exp_and_others")
            act.wait_ge(small_v, 1)
            act.activation(sm[:, S_STEP, :], colc[:, ROW_STEP:ROW_STEP + PAIRS], ACT.Exp)\
                .then_inc(small_a, 1)
            split(0, 0, KD)
            act.wait_ge(g1_set, 1)
            for k in range(KD):
                act.wait_ge(xt_ps, k + 1)
                act.activation(halves(hT[:, k], HL), psum2(4 + 2 * (k % 2), HL), ACT.Copy)\
                    .then_inc(xt_copied, 1)
                act.activation(halves(xh[:, k], HL), psum2(4 + 2 * (k % 2), HL), ACT.Copy,
                               scale=g1[:, k:k + 1]).then_inc(xh_set, 1)
                if k == 4:
                    split(1, 1, KD)
                if k == 5:
                    act.wait_ge(small_v, 2)
                    act.activation(sm[:, S_MAG, :], sm[:, S_LST, :], ACT.Exp)
                    act.activation(sm[:, S_SIN, :], sm[:, S_TH, :], ACT.Sin)
                    act.activation(sm[:, S_SINH, :], sm[:, S_TH, :], ACT.Sin, scale=0.5)\
                        .then_inc(small_a, 1)
            act.preload_act_table_set("natural_log_exp_and_others")

            def spread(_):
                act.wait_ge(rb_v, 1)
                link(act.activation(rb[:], kT[:, 0], ACT.Ln))
                act.activation(rb[:], rb[:], ACT.Exp, scale=-0.5).then_inc(rb_a, 1)

            def squares(i):
                is_k, t, unit = norm_of(i)
                w = L if is_k else LL
                act.wait_ge(drained, unit + 1)
                if i >= 2:
                    act.wait_ge(normed, i - 1)
                act.activation(sq[i % 2][:, 0:w], (kT if is_k else qT)[:, t, 0:w], ACT.Square)\
                    .then_inc(sq_ready, 1)

            def norm(i):
                is_k, t, _ = norm_of(i)
                w = L if is_k else LL
                act.wait_ge(ss_v, i + 1)
                link(act.activation(ta[:, 0:w], tb[:, 0:w], ACT.Ln))
                act.activation(ta[:, 0:w], ta[:, 0:w], ACT.Exp, scale=-0.5).then_inc(rs_a, 1)

            def prep(r):
                act.wait_ge(g_t, r + 1)
                for c in range(2):
                    ins = act.activation(win[:, c], ps[:, 4 + c, :], ACT.Copy)
                ins.then_inc(win_set, 1)

            def turn_v(t):
                act.wait_ge(v_t, t + 1)
                c0 = P * t
                act.activation(vh[:, 0:4, c0:c0 + P],
                               ps[:, 4, :].rearrange("p (k c) -> p k c", c=P), ACT.Copy)
                act.activation(vh[:, 4, c0:c0 + P], ps[:, 5, 0:P], ACT.Copy).then_inc(vh_set, 1)

            def readout(r):
                act.preload_act_table_set("gelu_apprx_tanh_and_others")
                act.wait_ge(y_ps, r + 1)
                if r:
                    act.wait_ge(y_out[r - 1], 16 * T8)
                act.activation(yg[:].rearrange("p (b g) c -> p b (g c)", b=2), psum2(6, HL),
                               ACT.Gelu_apprx_tanh).then_inc(yg_set, 1)
                act.preload_act_table_set("natural_log_exp_and_others")
                if r == ROUNDS - 1:
                    act.wait_ge(qz_zero, 1)
                    head_k(0)
                    head_q(0)
                    head_q(1)

            def head_k(t):
                act.wait_ge(normed, 4)
                if t:
                    act.wait_ge(z_ps, 2 * t)
                act.activation(kh[:], kT[:, t], ACT.Copy).then_inc(kh_set, 1)

            def head_q(h):
                if h >= 2:
                    act.wait_ge(z_ps, h - 1)
                part = slice(DH * (h % 2), DH * (h % 2) + DH)
                act.activation(qzh[h % 2][part, :], qT[part, h // 2, 0:LL], ACT.Copy)\
                    .then_inc(qh_set, 1)

            def scores(h):
                for two in (BANKS[0:2], BANKS[2:4]):
                    for b in two:
                        act.wait_ge(z_abs, AB * h + BANKS.index(b) + 1)
                        o = bank_cols(b)
                        ins = act.activation(aw[:, o], aw[:, o], ACT.Exp)
                    link(ins)
                    for b in two:
                        o = bank_cols(b)
                        act.activation(aw[:, o], aw[:, o], ACT.Ln, bias=1.0).then_inc(z_ln, 1)
                if h:
                    act.wait_ge(av_ps, h)
                for n, b in enumerate(BANKS):
                    act.wait_ge(soft_set, AB * h + n + 1)
                    act.activation(awh[:, bank_cols(b)], aw[:, bank_cols(b)], ACT.Copy)\
                        .then_inc(soft_hi, 1)

            def suffix(h):
                if h == 1:
                    head_k(1)
                    head_q(2)
                    head_q(3)
                act.wait_ge(suf_ps, h + 1)
                act.wait_ge(soft_lo, AB * h + AB)
                for b in range(AB):
                    act.activation(aw[:, bank_cols(b)], ps[:, 4 + b, 0:BANK_COLS[b]], ACT.Exp)\
                        .then_inc(prob_set, 1)
                for b in range(AB):
                    act.wait_ge(prob_set, AB * h + b + 1)
                    act.activation(awh[:, bank_cols(b)], aw[:, bank_cols(b)], ACT.Copy)\
                        .then_inc(prob_hi, 1)
                if h == HEADS - 1:
                    act.preload_act_table_set("sigmoid_and_others")

            def values(h):
                act.wait_ge(av_ps, h + 1)
                part = slice(DH * (h % 2), DH * (h % 2) + DH)
                act.activation(atth[part, h // 2, 0:Q_SPLIT - LATE0],
                               ps[part, 4, 0:Q_SPLIT - LATE0], ACT.Copy)
                act.activation(atth[part, h // 2, Q_SPLIT - LATE0:LL], ps[part, 5, 0:L - Q_SPLIT],
                               ACT.Copy).then_inc(ath_set, 1)

            def gelu(i):
                if i == 0:
                    act.wait_ge(y_in, 16)
                for r in (2 * i, 2 * i + 1):
                    act.activation(gh[:, r].rearrange("p (c j) -> p c j", j=T8),
                                   yT[:, r].rearrange("p j c -> p c j"), ACT.Copy)\
                        .then_inc(gh_set, 1)

            steps = {"spread": spread, "norm": norm, "prep": prep, "readout": readout,
                     "scores": scores,
                     "suffix": suffix, "values": values, "gelu": gelu, "turn_v": turn_v}

            def evacuate(unit):
                if unit >= U_GLU:
                    act.wait_ge(unit_done, unit + 1)
                    for mm in range(2):
                        m = 2 * (unit - U_GLU) + mm
                        if m >= 2:
                            act.wait_ge(sl_set, m - 1)
                        act.activation(halves(gt[mm][:], HL), psum2(2 * mm, HL), ACT.Sigmoid,
                                       bias=cols[:, COL_BG + m:COL_BG + m + 1])\
                           .then_inc(glu_sig, 1)
                    act.wait_ge(av_ps, HEADS)
                    for mm in range(2):
                        m = 2 * (unit - U_GLU) + mm
                        act.wait_ge(glu_val, m + 1)
                        act.activation(sh[:, m], gt[mm][:], ACT.Copy).then_inc(sh_set, 1)

            def open_gates(m):
                if m == 0:
                    act.wait_ge(gate_raw, 2 * KD)
                for i in (m, KD + m):
                    ins = act.activation(gate[i], gate[i], ACT.Sigmoid)
                ins.then_inc(gate_set, 1)

            def tiles_of(unit):
                return 6 if U_PROJ <= unit < U_WO else KD

            for unit in range(U_PROJ):
                for name, i in STEPS.get(unit, []):
                    if name == "norm":
                        squares(i)
                split(unit + 2, unit % 2, tiles_of(unit + 2))
                evacuate(unit)
                for name, i in STEPS.get(unit, []):
                    if name in steps:
                        steps[name](i)
            def mixed_hi(m):
                act.wait_ge(m_sum, m + 1)
                act.activation(mh[:, m], ma[m % 2][:], ACT.Copy).then_inc(mh_set, 1)

            open_gates(0)
            open_gates(1)
            for m in range(KD):
                unit = U_PROJ + m
                split(unit + 2, unit % 2, tiles_of(unit + 2))
                if m + 2 < KD:
                    open_gates(m + 2)
                if m:
                    mixed_hi(m - 1)
            mixed_hi(KD - 1)
            for m in range(KD):
                unit = U_WO + m
                if m < KD - 1:
                    split(unit + 2, unit % 2, KD)
                act.wait_ge(h_set, m + 1)
                act.activation(xh[:, m, 0:LL], hT[:, m, LATE0:L], ACT.Copy,
                               scale=cols[:, COL_N2 + m:COL_N2 + m + 1]).then_inc(zh_set, 1)
                if m >= 2:
                    act.wait_ge(h_acc, m - 1)
                act.activation(sqh[m % 2][:], hT[:, m, LATE0:L], ACT.Square).then_inc(h_sq, 1)
            split(U_UP + 1, 1, KD)
            act.preload_act_table_set("natural_log_exp_and_others")
            split(U_UP + 2, 0, KD)
            act.wait_ge(ss2_v, 1)
            link(act.activation(rb[:, 0:LL], nv[:], ACT.Ln))
            act.activation(rb[:, 0:LL], rb[:, 0:LL], ACT.Exp, scale=-0.5).then_inc(r2_a, 1)
            act.preload_act_table_set("silu_and_others")

            def cast_product(f, s):
                act.wait_ge(act_p, f + 1)
                act.activation(ah[:, bass.ds(f, 1), :].rearrange("p a c -> p (a c)"), cv[s][:, 1],
                               ACT.Copy).then_inc(ah_set, 1)

            def up(f, s, tiles=KD):
                for part in range(2):
                    if not (isinstance(f, int) and f == 0 and part == 0):
                        split(f * 2 + (U_UP + 2 + part), part, tiles)
                    act.wait_ge(up_v, f * 2 + (part + 1))
                    if part == 0 and not (isinstance(f, int) and f < 2):
                        act.wait_ge(al_set, f - 1)
                    m = f + part * KF
                    act.activation(cv[s][:, part], ut[s][:, part, 2:2 + SEQ], ACT.Identity,
                                   bias=cols[:, bass.ds(m + COL_CB, 1)],
                                   scale=cols[:, bass.ds(m + COL_CW, 1)]).then_inc(cv_a, 1)
                    if part == 0:
                        if not (isinstance(f, int) and f < 1):
                            cast_product(f - 1, 1 - s)
                        act.wait_ge(cv_v, f * 2 + 1)
                        act.activation(cv[s][:, 0], cv[s][:, 0], ACT.Silu).then_inc(silu_a, 1)

            up(0, 0)
            up(1, 1)
            with act.Fori(1, KF // 2 - 1) as ff:
                for s in range(2):
                    up(ff * 2 + s, s)
            up(KF - 2, 0)
            up(KF - 1, 1, UT)
            cast_product(KF - 1, 1)

            def turned(m, s, stored):
                act.wait_ge(yt_ps, m + 1)
                if not isinstance(stored, int) or stored:
                    act.wait_ge(out_done[s], 16 * stored)
                act.activation(yt[s][:], ps[:, 4 + s, :].rearrange("p (t c) -> p t c", c=P),
                               ACT.Copy).then_inc(yt_set, 1)

            def down(m, stored, s):
                for half in range(2):
                    split(m * 2 + (U_DOWN + 2 + half), half, UT)
                turned(m - 1, s, stored)

            for half in range(2):
                split(U_DOWN + 2 + half, half, UT)
            down(1, 0, 0)
            down(2, 0, 1)
            with act.Fori(1, KD // 2 - 1) as mm:
                for s in range(2):
                    down(mm * 2 + (1 + s), mm, s)
            for s in range(2):
                turned(KD - 2 + s, s, KD // 2 - 1)

        @block.vector
        def _(dve):
            link = linker(dve, dve_link)

            def split(unit, slot, n):
                dve.wait_ge(hi_ready, unit + 1)
                dve.tensor_tensor(lo[slot][:, 0:n * P], raw[slot][:, 0:n * P],
                                  hi[slot][:, 0:n * P].bitcast(F32), ALU.subtract)\
                   .then_inc(lo_ready, 1)

            def newton(r, v, t, factor=1.0):
                link(dve.tensor_tensor(t, r, r, ALU.mult))
                link(dve.tensor_tensor(t, t, v, ALU.mult))
                link(dve.tensor_scalar(t, t, -0.5 * factor, 1.5 * factor, ALU.mult, ALU.add))
                return dve.tensor_tensor(r, r, t, ALU.mult)

            dve.wait_ge(stk_in, 16 * STK_DMAS)
            sr = slice(ROW_STEP, ROW_STEP + PAIRS)
            dve.tensor_copy(stack[sr, 0, :].rearrange("r (g p) -> r g p", g=2),
                            lst[sr].unsqueeze(2).broadcast_to([PAIRS, 2, ST]))\
               .then_inc(stack_full, 1)

            dve.wait_ge(cols_t, 1)
            dve.tensor_copy(g1[:], ps[:, 0, P:P + KD]).then_inc(g1_set, 1)
            link(dve.tensor_copy(colc[:], ps[:, 0, 0:P]))

            def x_lo(k):
                dve.wait_ge(xh_set, k + 1)
                dve.scalar_tensor_tensor(xl[:, k], hT[:, k], g1[:, k:k + 1],
                                         xh[:, k].bitcast(F32), ALU.mult, ALU.subtract)\
                   .then_inc(x_ready, 1)

            def add_square(k):
                dve.wait_ge(x_sq, k + 1)
                if k == 0:
                    dve.tensor_copy(qT[:, 0], kT[:, 0]).then_inc(x_acc, 1)
                else:
                    dve.wait_ge(x_acc, k)
                    dve.tensor_tensor(qT[:, 0], qT[:, 0], kT[:, k % 2], ALU.add)\
                       .then_inc(x_acc, 1)

            def s(i):
                return sm[:, i, :]

            def tt(o, a, b, op):
                link(dve.tensor_tensor(s(o), s(a), s(b), op))

            are = colc[:, ROW_ARE:ROW_ARE + PAIRS]
            aim = colc[:, ROW_AIM:ROW_AIM + PAIRS]
            dve.tensor_scalar(s(S_LRE), are, A_RE_MAX, None, ALU.min).then_inc(small_v, 1)
            dve.wait_ge(small_v, 1)
            dve.wait_ge(small_a, 1)
            link(dve.tensor_tensor(s(S_LST), s(S_LRE), s(S_STEP), ALU.mult))
            link(dve.tensor_tensor(s(S_TH), aim, s(S_STEP), ALU.mult))
            link(dve.tensor_scalar(s(S_N), s(S_TH), 1.0 / TWO_PI, ROUND_MAGIC, ALU.mult, ALU.add))
            link(dve.tensor_scalar(s(S_N), s(S_N), ROUND_MAGIC, None, ALU.subtract))
            for c in (CW1, CW2, CW3):
                link(dve.scalar_tensor_tensor(s(S_TH), s(S_N), -c, s(S_TH), ALU.mult, ALU.add))
            dve.tensor_scalar(s(S_TH), s(S_TH), PI_BELOW, -PI_BELOW, ALU.min, ALU.max)\
               .then_inc(small_v, 1)
            split(0, 0, KD)
            dve.wait_ge(g1_set, 1)
            for k in range(KD):
                x_lo(k)
                if k:
                    add_square(k - 1)
                if k == 4:
                    split(1, 1, KD)
            add_square(KD - 1)
            tt(S_T1, S_LRE, S_LRE, ALU.mult)
            link(dve.tensor_tensor(s(S_T2), aim, aim, ALU.mult))
            tt(S_DEN, S_T1, S_T2, ALU.add)
            link(dve.reciprocal(s(S_DEN), s(S_DEN)))
            link(dve.tensor_tensor(skip_i[:], ident[0:GH, 0:GH].unsqueeze(1)
                                   .broadcast_to([GH, GROUPS, GH]),
                                   colc[0:GH, ROW_SKIP:ROW_SKIP + GROUPS].unsqueeze(2)
                                   .broadcast_to([GH, GROUPS, GH]), ALU.mult))

            def small(_):
                dve.wait_ge(small_a, 2)
                tt(S_T1, S_SINH, S_SINH, ALU.mult)
                link(dve.tensor_scalar(s(S_COS), s(S_T1), -2.0, 1.0, ALU.mult, ALU.add))
                dve.wait_ge(masks_set, 2)
                link(dve.tensor_tensor(pw[:, 0, 1, :], s(S_MAG), s(S_COS), ALU.mult))
                link(dve.tensor_tensor(pw[:, 1, 1, :], s(S_MAG), s(S_SIN), ALU.mult))
                link(dve.tensor_scalar(s(S_NR), pw[:, 0, 1, :], 1.0, None, ALU.subtract))
                tt(S_T1, S_NR, S_LRE, ALU.mult)
                link(dve.tensor_tensor(s(S_T2), pw[:, 1, 1, :], aim, ALU.mult))
                tt(S_FR, S_T1, S_T2, ALU.add)
                link(dve.tensor_tensor(s(S_T1), pw[:, 1, 1, :], s(S_LRE), ALU.mult))
                link(dve.tensor_tensor(s(S_T2), s(S_NR), aim, ALU.mult))
                tt(S_FI, S_T1, S_T2, ALU.subtract)
                tt(S_FR, S_FR, S_DEN, ALU.mult)
                link(dve.tensor_tensor(s(S_FI), s(S_FI), s(S_DEN), ALU.mult))
                tt(S_D2, S_MAG, S_MAG, ALU.mult)
                tt(S_D4, S_D2, S_D2, ALU.mult)
                dve.tensor_tensor(s(S_D2), s(S_D4), s(S_D4), ALU.mult).then_inc(small_v, 1)
                dve.wait_ge(small_v, 3)

            def powers(_):
                for n in (1, 2, 4):
                    at = [pw[:, c, n:n + 1, :].broadcast_to([P, n, PAIRS]) for c in range(2)]
                    t = uc[:, 1].rearrange("p g c -> p (g c)")[:, 0:n * PAIRS]
                    cmul(dve, link, [pw[:, c, n + 1:2 * n + 1, :] for c in range(2)],
                         [pw[:, c, 1:n + 1, :] for c in range(2)], at,
                         t.rearrange("p (n r) -> p n r", r=PAIRS))
                dve.nop().then_inc(pw_set, 1)

            def b_factor(_):
                dve.wait_ge(bc_in, 16 * BC_DMAS)
                f = [sm[:, c, :].unsqueeze(2).broadcast_to([P, PAIRS, GH]) for c in (S_FR, S_FI)]
                t = uc[:, 1].rearrange("p g c -> p (g c)")[:, 0:PAIRS * GH]
                cmul(dve, link, both(bb), both(braw), f, t.rearrange("p (r h) -> p r h", h=GH))
                for g in range(2):
                    part = slice(ST * g, ST * g + ST)
                    ins = dve.tensor_copy(bpair[part, :, :, 2 * GH * g:2 * GH * g + GH], bb[part])
                    if g == 0:
                        link(ins)
                ins.then_inc(b_set, 1)

            def turns(_):
                dve.wait_ge(rot_set, 1)
                t = yg[:].rearrange("p g c -> p (g c)")
                for j in (5, 6):
                    extend_turns(dve, link, j, t)
                link(dve.tensor_copy(decay[:, :, 1:NC], sm[:, S_D2, :].unsqueeze(2)
                                     .broadcast_to([P, PAIRS, NC - 1])))

            def spread(_):
                dve.wait_ge(rb_ps, 1)
                dve.tensor_scalar(halves(kT[:, 0], HL), psum2(6, HL), 1.0 / D, EPS, ALU.mult,
                                  ALU.add).then_inc(rb_v, 1)
                dve.wait_ge(rb_a, 1)
                newton(rb[:], kT[:, 0], kT[:, 1]).then_inc(rb_set, 1)
                dve.wait_ge(rb_set, 1)

            def columns(i):
                dve.wait_ge(cols_t, 2 + i)
                if i:
                    dve.tensor_copy(cols[:], ps[:, 6, 0:NCOLS]).then_inc(cols_set, 1)
                    dve.wait_ge(cols_set, 1)
                    return
                for c in range(2):
                    src = ps[:, 4 + c, :].rearrange("p (r g h) -> p r g h", g=2, h=GH)
                    for g in range(2):
                        part = slice(ST * g, ST * g + ST)
                        ins = dve.tensor_scalar(ct[part, c], src[part, :, g, :], 1.0 - 2.0 * c,
                                                None, ALU.mult)
                ins.then_inc(ct_set, 1)

            def norm(i):
                is_k, tile, _ = norm_of(i)
                w = HL if is_k else HLL
                dst = (kT if is_k else qT)[:, tile, 0:2 * w]
                g = cols[:, (COL_KG if is_k else COL_QG):][:, 0:1]
                dve.wait_ge(ss_ps, i + 1)
                dve.tensor_scalar(halves(tb[:, 0:2 * w], w), psum2(4, w), 1.0 / DH, EPS, ALU.mult,
                                  ALU.add).then_inc(ss_v, 1)
                dve.wait_ge(rs_a, i + 1)
                link(newton(ta[:, 0:2 * w], tb[:, 0:2 * w], sq[i % 2][:, 0:2 * w],
                            1.0 if is_k else DH ** -0.5))
                dve.scalar_tensor_tensor(dst, dst, g, ta[:, 0:2 * w], ALU.mult, ALU.mult)\
                   .then_inc(normed, 1)

            def prep(r):
                dve.wait_ge(k_ps, r + 1)
                if r:
                    dve.wait_ge(kern_out[r - 1], 16 * T8)
                for g in range(2):
                    ins = dve.tensor_copy(kern[:].rearrange("h (r g) c -> h g r c", g=2)[:, g],
                                          ps[2 * GH * g:2 * GH * g + GH, 6, :]
                                          .rearrange("h (r c) -> h r c", c=P))
                link(ins)
                dve.tensor_tensor(kern[:, :, 0:GH], kern[:, :, 0:GH],
                                  skip_i[:, 2 * RP * r:2 * RP * (r + 1), :], ALU.add)\
                   .then_inc(kern_set, 1)

            def state(r):
                pr = slice(r * RP, (r + 1) * RP)
                cos, sin = rot[:, 0, pr, :], rot[:, 1, pr, :]
                re, im = (ps[:, 4 + c, 0:RP * NC].rearrange("p (r c) -> p r c", c=NC)
                          for c in range(2))
                m = [mod[:, i] for i in range(4)]
                flat = [x_.rearrange("p r c -> p (r c)") for x_ in m]
                dve.wait_ge(st_ps, r + 1)
                if r == 0:
                    for u in u_out:
                        dve.wait_ge(u, 16)
                dve.tensor_tensor(m[0], re, cos, ALU.mult)
                dve.tensor_tensor(m[1], im, sin, ALU.mult)
                dve.tensor_tensor(m[2], im, cos, ALU.mult)
                dve.tensor_tensor(m[3], re, sin, ALU.mult).then_inc(st_read, 1)
                dve.wait_ge(st_read, r + 1)
                dve.tensor_tensor(m[0], m[0], m[1], ALU.add)
                link(dve.tensor_tensor(m[2], m[2], m[3], ALU.subtract))
                dec = decay[:, pr, :].rearrange("p r c -> p (r c)")
                dve.tensor_tensor_scan(flat[1], dec, flat[0], 0.0, ALU.mult, ALU.add)
                link(dve.tensor_tensor_scan(flat[3], dec, flat[2], 0.0, ALU.mult, ALU.add))
                dve.tensor_tensor(m[0], m[1], cos, ALU.mult)
                link(dve.tensor_tensor(m[2], m[3], sin, ALU.mult))
                if r:
                    dve.wait_ge(y_ps, r)

                def forward(c, op):
                    for g in range(2):
                        part = slice(ST * g, ST * g + ST)
                        ins = dve.tensor_tensor(xst[part, c, g, :, 1:NC], m[0][part, :, 0:NC - 1],
                                                m[2][part, :, 0:NC - 1], op)
                    return ins

                link(forward(0, ALU.subtract))
                dve.tensor_tensor(m[0], m[3], cos, ALU.mult)
                link(dve.tensor_tensor(m[2], m[1], sin, ALU.mult))
                forward(1, ALU.add).then_inc(st_set, 1)

            def turn_v(t):
                dve.wait_ge(vh_set, t + 1)
                c = slice(P * t, P * t + P)
                dve.tensor_tensor(vl[:, 0:4, c], ps[:, 4, :].rearrange("p (k c) -> p k c", c=P),
                                  vh[:, 0:4, c].bitcast(F32), ALU.subtract)
                dve.tensor_tensor(vl[:, 4, c], ps[:, 5, 0:P], vh[:, 4, c].bitcast(F32),
                                  ALU.subtract).then_inc(vl_set, 1)

            def readout(r):
                if r == ROUNDS - 1:
                    head_k(0)
                    head_q(0)
                    head_q(1)

            def head_k(t):
                dve.wait_ge(kh_set, t + 1)
                dve.tensor_tensor(kl[:], kT[:, t], kh[:].bitcast(F32), ALU.subtract)\
                   .then_inc(kl_set, 1)

            def head_q(h):
                dve.wait_ge(qh_set, h + 1)
                part = slice(DH * (h % 2), DH * (h % 2) + DH)
                dve.tensor_tensor(qzl[h % 2][part, :], qT[part, h // 2, 0:LL],
                                  qzh[h % 2][part, :].bitcast(F32), ALU.subtract)\
                   .then_inc(ql_set, 1)

            def scores(h):
                def soft_part(n):
                    dve.wait_ge(soft_hi, AB * h + n + 1)
                    o = bank_cols(BANKS[n])
                    dve.tensor_tensor(awl[:, o], aw[:, o], awh[:, o].bitcast(F32), ALU.subtract)\
                       .then_inc(soft_lo, 1)

                dve.wait_ge(z_part, h + 1)
                if h:
                    dve.wait_ge(prob_lo, AB * h)
                for two in (BANKS[0:2], BANKS[2:4]):
                    if two == BANKS[2:4]:
                        dve.wait_ge(z_ps, h + 1)
                    for b in two:
                        z = ps[:, 4 + b, 0:BANK_COLS[b]]
                        ins = dve.tensor_scalar(aw[:, bank_cols(b)], z, 0.0, None, ALU.min)
                    link(ins)
                    for b in two:
                        o = bank_cols(b)
                        dve.scalar_tensor_tensor(aw[:, o], aw[:, o], 2.0,
                                                 ps[:, 4 + b, 0:BANK_COLS[b]],
                                                 ALU.mult, ALU.subtract).then_inc(z_abs, 1)
                for n, b in enumerate(BANKS):
                    dve.wait_ge(z_ln, AB * h + n + 1)
                    o = bank_cols(b)
                    dve.scalar_tensor_tensor(aw[:, o], ps[:, 4 + b, 0:BANK_COLS[b]], 0.0,
                                             aw[:, o], ALU.max, ALU.add).then_inc(soft_set, 1)
                    if n >= 2:
                        soft_part(n - 2)
                for n in (AB - 2, AB - 1):
                    soft_part(n)

            def suffix(h):
                if h == 1:
                    head_k(1)
                    head_q(2)
                    head_q(3)
                for b in range(AB):
                    dve.wait_ge(prob_hi, AB * h + b + 1)
                    o = bank_cols(b)
                    dve.tensor_tensor(awl[:, o], aw[:, o], awh[:, o].bitcast(F32), ALU.subtract)\
                       .then_inc(prob_lo, 1)

            def values(h):
                dve.wait_ge(ath_set, h + 1)
                part = slice(DH * (h % 2), DH * (h % 2) + DH)
                for b, a, e in ((4, 0, Q_SPLIT - LATE0), (5, Q_SPLIT - LATE0, LL)):
                    ins = dve.tensor_tensor(attl[part, h // 2, a:e], ps[part, b, 0:e - a],
                                            atth[part, h // 2, a:e].bitcast(F32), ALU.subtract)
                ins.then_inc(atl_set, 1)

            def token_order(ap):
                return ap.rearrange("p j c -> p c j")

            def by_chunk(ap):
                return ap.rearrange("p (c j) -> p c j", j=T8)

            def gelu(i):
                for r in (2 * i, 2 * i + 1):
                    dve.wait_ge(gh_set, r + 1)
                    dve.tensor_tensor(by_chunk(gl[:, r]), token_order(yT[:, r]),
                                      by_chunk(gh[:, r]).bitcast(F32), ALU.subtract)\
                       .then_inc(gl_set, 1)

            def glu(unit):
                tiles = [2 * (unit - U_GLU) + mm for mm in range(2)]
                for mm, m in enumerate(tiles):
                    dve.wait_ge(glu_sig, m + 1)
                    dve.tensor_tensor(by_chunk(gt[mm][:]), by_chunk(gt[mm][:]),
                                      token_order(yT[:, m]), ALU.mult).then_inc(glu_val, 1)
                for mm, m in enumerate(tiles):
                    dve.wait_ge(sh_set, m + 1)
                    dve.tensor_tensor(sl[:, m], gt[mm][:], sh[:, m].bitcast(F32), ALU.subtract)\
                       .then_inc(sl_set, 1)

            def evacuate(unit):
                dve.wait_ge(unit_done, unit + 1)
                b = 2 * (unit % 2)
                if unit < U_K:
                    if unit >= 2:
                        dve.wait_ge(u_out[unit - 2], 16)
                    dst = uy[:, unit % 2].rearrange("p j (k c) -> p k c j", k=2)
                    for k in range(2):
                        ins = dve.tensor_tensor(dst[:, k], by_chunk(ps[:, b + k, 0:HL]),
                                                by_chunk(rb[:, k * HL:(k + 1) * HL]), ALU.mult)
                    ins.then_inc(drained, 1)
                    return
                late_ = unit >= U_Q
                w = HLL if late_ else HL
                if unit < U_V:
                    dst = kT[:, unit - U_K]
                elif unit < U_Q:
                    dst = vT[unit - U_V]
                elif unit < U_GATE:
                    dst = qT[:, unit - U_Q, 0:LL]
                else:
                    dst = gate[gate_of(unit)]
                dve.tensor_tensor(halves(dst, w), psum2(b, w),
                                  halves(rb[:, LATE0 if late_ else 0:L], w), ALU.mult)\
                   .then_inc(gate_raw if is_gate(unit) else drained, 1)

            steps = {"spread": spread, "columns": columns, "small": small, "powers": powers,
                     "b_factor": b_factor,
                     "turns": turns,
                     "norm": norm, "prep": prep, "state": state, "readout": readout,
                     "scores": scores, "suffix": suffix, "values": values, "gelu": gelu,
                     "turn_v": turn_v}

            def tiles_of(unit):
                return 6 if U_PROJ <= unit < U_WO else KD

            for unit in range(U_PROJ):
                if unit == 0:
                    split(2, 0, KD)
                    spread(0)
                if unit < U_GLU:
                    evacuate(unit)
                if unit:
                    split(unit + 2, unit % 2, tiles_of(unit + 2))
                if U_GLU <= unit:
                    glu(unit)
                for name, i in STEPS.get(unit, []):
                    if name in steps and name != "spread":
                        steps[name](i)

            def mixed_lo(m):
                dve.wait_ge(mh_set, m + 1)
                dve.tensor_tensor(ml[:, m], ma[m % 2][:], mh[:, m].bitcast(F32), ALU.subtract)\
                   .then_inc(ml_set, 1)

            for m in range(KD):
                unit = U_PROJ + m
                split(unit + 2, unit % 2, tiles_of(unit + 2))
                if m >= 2:
                    mixed_lo(m - 2)
                dve.wait_ge(gate_set, m + 1)
                dve.wait_ge(unit_done, unit + 1)
                if m >= 2:
                    dve.wait_ge(m_sum, m - 1)
                    dve.wait_ge(ml_set, m - 1)
                b = 4 - 4 * (m % 2)
                dve.tensor_tensor(halves(ma[m % 2][:], HLL), psum2(b, HLL), halves(gate[m], HLL),
                                  ALU.mult)
                dve.tensor_tensor(halves(mb[m % 2][:], HLL), psum2(b + 2, HLL),
                                  halves(gate[KD + m], HLL), ALU.mult).then_inc(m_gated, 1)
            mixed_lo(KD - 2)
            mixed_lo(KD - 1)

            def z_lo(m):
                dve.wait_ge(zh_set, m + 1)
                dve.scalar_tensor_tensor(xl[:, m, 0:LL], hT[:, m, LATE0:L],
                                         cols[:, COL_N2 + m:COL_N2 + m + 1],
                                         xh[:, m, 0:LL].bitcast(F32), ALU.mult, ALU.subtract)\
                   .then_inc(z_ready, 1)

            for m in range(KD):
                unit = U_WO + m
                dve.wait_ge(unit_done, unit + 1)
                dve.tensor_tensor(halves(hT[:, m, LATE0:L], HLL), psum2(4 + 2 * (m % 2), HLL),
                                  halves(hT[:, m, LATE0:L], HLL), ALU.add).then_inc(h_set, 1)
                if m < KD - 1:
                    split(unit + 2, unit % 2, KD)
                if m:
                    z_lo(m - 1)
            z_lo(KD - 1)
            split(U_UP + 1, 1, KD)
            dve.wait_ge(ss2_ps, 1)
            dve.tensor_scalar(halves(nv[:], HLL), psum2(4, HLL), 1.0 / D, EPS, ALU.mult, ALU.add)\
               .then_inc(ss2_v, 1)
            split(U_UP + 2, 0, KD)
            dve.wait_ge(r2_a, 1)
            newton(rb[:, 0:LL], nv[:], sqh[0][:]).then_inc(r2_set, 1)
            dve.wait_ge(r2_set, 1)

            def product_lo(f, s_):
                dve.wait_ge(ah_set, f + 1)
                at = bass.ds(f, 1)
                dve.tensor_tensor(al[:, at, :].rearrange("p a c -> p (a c)"), cv[s_][:, 1],
                                  ah[:, at, :].bitcast(F32).rearrange("p a c -> p (a c)"),
                                  ALU.subtract).then_inc(al_set, 1)

            def up(f, s_, tiles=KD):
                for part in range(2):
                    dve.wait_ge(unit_done, f * 2 + (U_UP + 1 + part))
                    if part == 0 and not (isinstance(f, int) and f < 2):
                        dve.wait_ge(cv_v, f * 2 - 2)
                    dve.tensor_tensor(halves(ut[s_][:, part], HLL), psum2(4 * s_ + 2 * part, HLL),
                                      halves(rb[:, 0:LL], HLL), ALU.mult).then_inc(up_v, 1)
                    if not (isinstance(f, int) and f == 0 and part == 0):
                        split(f * 2 + (U_UP + 2 + part), part, tiles)
                    for tap in (1, 2):
                        if tap == 1:
                            dve.wait_ge(cv_a, f * 2 + (part + 1))
                        else:
                            dve.wait_ge(cv_mid, f * 2 + (part + 1))
                        w = cols[:, bass.ds(f + (COL_CW + (2 * tap + part) * KF), 1)]
                        dve.scalar_tensor_tensor(cv[s_][:, part],
                                                 ut[s_][:, part, 2 + tap:2 + tap + SEQ], w,
                                                 cv[s_][:, part], ALU.mult, ALU.add)\
                           .then_inc(cv_mid if tap == 1 else cv_v, 1)
                    if part == 0 and not (isinstance(f, int) and f < 1):
                        product_lo(f - 1, 1 - s_)

            up(0, 0)
            up(1, 1)
            with dve.Fori(1, KF // 2 - 1) as ff:
                for s_ in range(2):
                    up(ff * 2 + s_, s_)
            up(KF - 2, 0)
            up(KF - 1, 1, UT)
            product_lo(KF - 1, 1)

            def down(m, s_):
                for half in range(2):
                    if not isinstance(m, int) or m < KD - 1:
                        split(m * 2 + (U_DOWN + 2 + half), half, UT)
                dve.wait_ge(unit_done, m * 2 + (U_DOWN + 2))
                if not (isinstance(m, int) and m < 2):
                    dve.wait_ge(yt_ps, m - 1)
                dve.tensor_tensor(yo[s_][:], ps[:, s_, :],
                                  hT[:, bass.ds(m, 1), META:L].rearrange("p a c -> p (a c)"),
                                  ALU.add).then_inc(y_add, 1)

            down(0, 0)
            down(1, 1)
            with dve.Fori(1, KD // 2 - 1) as mm:
                for s_ in range(2):
                    down(mm * 2 + s_, s_)
            for s_ in range(2):
                down(KD - 2 + s_, s_)

        @block.tensor
        def _(pe):
            def three(outs, weights, acts, start, stop):
                for i, (w, a) in enumerate(((0, 0), (0, 1), (1, 0))):
                    for c, o in enumerate(outs):
                        ins = pe.matmul(o, weights[w], acts(a, c), start=start and i == 0,
                                        stop=stop and i == 2)
                return ins

            def wtile(slot, i, n=1):
                return [w[slot][:, i * P:(i + n) * P] for w in (hi, lo)]

            def product(slot, tile0, count, bank, width, pair, col0, ready=None, first=0,
                        stride=1, total=None):
                total = count if total is None else total
                for k in range(count):
                    if ready is not None:
                        pe.wait_ge(ready, first + k + 1)
                    ins = three([ps[:, bank + c, 0:width] for c in range(2)],
                                wtile(slot, tile0 + k * stride),
                                lambda a, c: pair[a][:, first + k, col0 + c * width:
                                                     col0 + (c + 1) * width],
                                k == 0, k == count - 1)
                return ins

            pe.wait_ge(masks_set, 1)
            pe.wait_ge(stack_full, 1)
            pe.wait_ge(stk_in, 16 * STK_DMAS)
            pe.wait_ge(gain_in, 16)
            pe.transpose(ps[:, 0, 0:P], stack[:, 0, :], ident[:])
            pe.transpose(ps[:, 0, P:P + KD], gain[:], ident[0:KD, 0:KD]).then_inc(cols_t, 1)
            rows = slice(0, TT_ROWS)
            for n, x_sem in ((32, x_in[0]), (32, x_in[1]), (16, x_in[2])):
                pe.wait_ge(x_sem, n)
            for k in range(KD):
                if k >= 2:
                    pe.wait_ge(xt_copied, k - 1)
                    pe.wait_ge(xh_set, k - 1)
                b = 4 + 2 * (k % 2)
                for i in range(NTT):
                    c0 = (i % 3) * TT_ROWS
                    ins = pe.transpose(ps[:, b + i // 3, c0:c0 + TT_ROWS],
                                       xtok[rows, i, k * P:(k + 1) * P], ident[rows, rows])
                ins.then_inc(xt_ps, 1)

            def spread(_):
                pe.wait_ge(x_acc, KD)
                for c in range(2):
                    ins = pe.matmul(ps[:, 6 + c, 0:HL], ones[:], qT[:, 0, c * HL:(c + 1) * HL],
                                    start=True, stop=True)
                ins.then_inc(rb_ps, 1)

            def columns(i):
                if i:
                    pe.wait_ge(par_in, 16 * PAR_DMAS)
                    pe.transpose(ps[:, 6, 0:P], stack[:, 1, :], ident[:])
                    n2 = NCOLS - P
                    pe.transpose(ps[:, 6, P:P + n2], stack[0:n2, 2, :], ident[0:n2, 0:n2])\
                      .then_inc(cols_t, 1)
                    return
                pe.wait_ge(bc_in, 16 * BC_DMAS)
                for c in range(2):
                    for t in range(4):
                        ins = pe.transpose(ps[:, 4 + c, t * P:(t + 1) * P],
                                           cdup[:, c, t].rearrange("p d s -> p (d s)"), ident[:])
                ins.then_inc(cols_t, 1)

            def norm(i):
                is_k, t, unit = norm_of(i)
                w = HL if is_k else HLL
                pe.wait_ge(sq_ready, i + 1)
                for c in range(2):
                    ins = pe.matmul(ps[:, 4 + c, 0:w], blocks[:], sq[i % 2][:, c * w:(c + 1) * w],
                                    start=True, stop=True)
                ins.then_inc(ss_ps, 1)

            def prep(r):
                pe.wait_ge(g_ready, r + 1)
                for c in range(2):
                    for i in range(RP):
                        ins = pe.transpose(ps[:, 4 + c, i * P:(i + 1) * P],
                                           g_in[:, c, i].rearrange("p j h -> p (j h)"), ident[:])
                ins.then_inc(g_t, 1)
                pe.wait_ge(h_ready, r + 1)
                for i in range(RP):
                    for c in range(2):
                        ins = pe.matmul(ps[0:3 * GH, 6, i * P:(i + 1) * P],
                                        bpair[:, c, r * RP + i, :],
                                        hout[r % 2][:, c, i, 0:T8, :].rearrange("p i h -> p (i h)"),
                                        start=c == 0, stop=c == 1)
                ins.then_inc(k_ps, 1)

            def state(r):
                pe.wait_ge(win_set, r + 1)
                pe.wait_ge(u_in[r], 16 * T8)
                for g in range(2 * RP):
                    part = slice(ST * (g % 2), ST * (g % 2) + ST)
                    for c in range(2):
                        w0 = (g // 2) * P + ST * (g % 2)
                        ins = pe.matmul(ps[part, 4 + c, (g // 2) * NC:(g // 2 + 1) * NC],
                                        win[:, c, w0:w0 + ST], uc[:, r % 2, g, :],
                                        start=True, stop=True)
                ins.then_inc(st_ps, 1)

            def readout(r):
                pe.wait_ge(kern_out[r], 16 * T8)
                pe.wait_ge(st_set, r + 1)
                for g in range(2 * RP):
                    o = ps[:, 6 + g // 4, (g % 4) * NC:(g % 4 + 1) * NC]
                    pe.matmul(o, toep[:, g, :], uc[:, r % 2, g, :], start=True, stop=False)
                    for c in range(2):
                        ins = pe.matmul(o, hout[r % 2][:, c, g // 2, 1:T8 + 1, :]
                                        .rearrange("p i h -> p (i h)"),
                                        xst[:, c, g % 2, g // 2, :], start=False, stop=c == 1)
                ins.then_inc(y_ps, 1)

            def turn_v(t):
                pe.wait_ge(drained, U_V + t + 1)
                for kb in range(5):
                    ins = pe.transpose(ps[:, 4 + kb // 4, (kb % 4) * P:(kb % 4 + 1) * P],
                                       vT[t][:, KEY0[kb]:KEY0[kb] + P], ident[:])
                ins.then_inc(v_t, 1)

            used45 = [(xt_copied, KD), (xh_set, KD)]
            used67 = [(xt_copied, KD), (xh_set, KD)]

            def scores(h):
                pe.wait_ge(kl_set, h // 2 + 1)
                pe.wait_ge(ql_set, h + 1)
                for bank in BANKS:
                    if bank == 0:
                        ins.then_inc(z_part, 1)
                        for s_, n in used45:
                            pe.wait_ge(s_, n)
                    mine = [g for g in REGIONS if g[0] == bank]
                    for n, (_, c0, kb, q0, q1) in enumerate(mine):
                        for i, (kk, qq) in enumerate(((kh, qzh), (kh, qzl), (kl, qzh))):
                            ins = pe.matmul(ps[:, 4 + bank, c0:c0 + q1 - q0],
                                            kk[:, KEY0[kb]:KEY0[kb] + P],
                                            qq[h % 2][:, q0 - LATE0:q1 - LATE0],
                                            start=n == 0 and i == 0, stop=False,
                                            skip_group_check=True)
                        if kb == 4:
                            ins = pe.matmul(ps[:, 4 + bank, c0:c0 + META], ident_bf[:],
                                            mask_last[:], start=False, stop=True,
                                            skip_group_check=True)
                        elif q0 < KEY0[kb] + P:
                            n_ = KEY0[kb] + P - q0
                            ins = pe.matmul(ps[:, 4 + bank, c0:c0 + n_], ident_bf[:],
                                            mask[:, P - n_:P], start=False, stop=True,
                                            skip_group_check=True)
                ins.then_inc(z_ps, 1)

            def soft_cols(part, region, q0, q1):
                a = BANK_OFF[region[0]] + region[1] + q0 - region[3]
                return part[:, a:a + q1 - q0]

            def suffix(h):
                pe.wait_ge(soft_lo, AB * h + AB)
                for g in REGIONS:
                    for part in (awh, awl):
                        ins = pe.matmul(ps[:, 4 + g[0], g[1]:g[1] + g[4] - g[3]], negtri[:],
                                        soft_cols(part, g, g[3], g[4]), start=False, stop=True,
                                        skip_group_check=True)
                    for later in REGIONS:
                        q0, q1 = shared_queries(g, later)
                        if later[2] > g[2] and q0 < q1:
                            o = g[1] + q0 - g[3]
                            for part in (awh, awl):
                                ins = pe.matmul(ps[:, 4 + g[0], o:o + q1 - q0], negones[:],
                                                soft_cols(part, later, q0, q1), start=False,
                                                stop=True, skip_group_check=True)
                ins.then_inc(suf_ps, 1)

            def values(h):
                if h == 0:
                    pe.wait_ge(vl_set, 2)
                pe.wait_ge(prob_lo, AB * h + AB)
                t = h // 2
                for low, bank, origin in ((True, 4, LATE0), (False, 5, Q_SPLIT)):
                    mine = [g for g in REGIONS if (g[4] == Q_SPLIT) == low]
                    for n, g in enumerate(mine):
                        a = BANK_OFF[g[0]] + g[1]
                        for i, (vv, ww) in enumerate(((vh, awh), (vh, awl), (vl, awh))):
                            ins = pe.matmul(ps[:, bank, g[3] - origin:g[4] - origin],
                                            vv[:, g[2], t * P:(t + 1) * P],
                                            ww[:, a:a + g[4] - g[3]], start=n == 0 and i == 0,
                                            stop=n == len(mine) - 1 and i == 2,
                                            skip_group_check=True)
                ins.then_inc(av_ps, 1)

            steps = {"spread": spread, "columns": columns,
                     "norm": norm, "prep": prep, "state": state, "readout": readout,
                     "scores": scores, "suffix": suffix, "values": values, "turn_v": turn_v}

            def run(name, i):
                if name == "scores" and i == 0:
                    pe.wait_ge(masks_set, 4)
                if (name in ("norm", "turn_v", "prep", "state")
                        or (name, i) == ("columns", 0)):
                    for s_, n in used45:
                        pe.wait_ge(s_, n)
                if name in ("spread", "prep", "readout", "scores") or (name, i) == ("columns", 1):
                    for s_, n in used67:
                        pe.wait_ge(s_, n)
                steps[name](i)
                if name == "spread":
                    used67[:] = [(rb_v, 1)]
                if name == "columns" and i == 0:
                    used45[:] = [(ct_set, 1)]
                if name == "columns" and i == 1:
                    used67[:] = [(cols_set, 1)]
                if name == "norm":
                    used45[:] = [(ss_v, i + 1)]
                if name == "turn_v":
                    used45[:] = [(vl_set, i + 1)]
                if name == "prep":
                    used45[:] = [(win_set, i + 1)]
                    used67[:] = [(kern_set, i + 1)]
                if name == "state":
                    used45[:] = [(st_read, i + 1)]
                if name == "readout":
                    used67[:] = [(yg_set, i + 1)]
                if name == "values":
                    used45[:] = [(atl_set, i + 1)]
                    used67[:] = []

            def left(unit):
                if unit < U_GATE:
                    return drained, unit + 1
                if is_gate(unit):
                    return gate_raw, gate_of(unit) + 1
                return glu_sig, 2 * (unit - U_GLU) + 2

            for unit in range(U_PROJ):
                slot = unit % 2
                glu = U_GLU <= unit
                pe.wait_ge(lo_ready, unit + 1)
                if unit == 0:
                    pe.wait_ge(small_v, 1)
                if unit >= 2:
                    pe.wait_ge(*left(unit - 2))
                if glu:
                    pe.wait_ge(*left(unit - 1))
                bank = 2 * slot
                x_pair = (xh, xl)
                if glu:
                    pe.wait_ge(gl_set, KS)
                    for mm in range(2):
                        ins = product(slot, mm, KS, 2 * mm, HL, (gh, gl), 0, stride=2)
                else:
                    ready = x_ready if unit == 0 else None
                    width, col0 = (HL, 0) if unit < U_Q else (HLL, LATE0)
                    ins = product(slot, 0, KD, bank, width, x_pair, col0, ready=ready)
                ins.then_inc(unit_done, 1)
                for name, i in STEPS.get(unit, []):
                    if name in steps:
                        run(name, i)

            def attention_part(m):
                pe.wait_ge(lo_ready, U_PROJ + m + 1)
                if m == 0:
                    pe.wait_ge(atl_set, HEADS)
                if m == 1:
                    pe.wait_ge(*left(U_PROJ - 1))
                if m >= 2:
                    pe.wait_ge(m_gated, m - 1)
                product(m % 2, 0, 2, 4 - 4 * (m % 2), HLL, (atth, attl), 0)

            def space_part(m):
                product(m % 2, 2, KS, 6 - 4 * (m % 2), HLL, (sh, sl), LATE0).then_inc(unit_done, 1)

            attention_part(0)
            attention_part(1)
            pe.wait_ge(sl_set, KS)
            space_part(0)
            space_part(1)
            for m in range(2, KD):
                attention_part(m)
                space_part(m)
            for m in range(KD):
                unit = U_WO + m
                pe.wait_ge(lo_ready, unit + 1)
                if m < 2:
                    pe.wait_ge(m_gated, KD - 1)
                else:
                    pe.wait_ge(h_set, m - 1)
                product(unit % 2, 0, KD, 4 + 2 * (m % 2), HLL, (mh, ml), 0,
                        ready=ml_set if m == 0 else None).then_inc(unit_done, 1)

            def up_unit(f, s, part, ready=None):
                pe.wait_ge(lo_ready, f * 2 + (U_UP + 1 + part))
                if not (isinstance(f, int) and f < 2):
                    pe.wait_ge(up_v, f * 2 + (part - 3))
                product(part, 0, KD, 4 * s + 2 * part, HLL, (xh, xl), 0, ready=ready)\
                    .then_inc(unit_done, 1)

            pe.wait_ge(m_gated, KD)
            up_unit(0, 0, 0, ready=z_ready)
            pe.wait_ge(h_set, KD)
            pe.wait_ge(h_acc, KD)
            for c in range(2):
                ins = pe.matmul(ps[:, 4 + c, 0:HLL], ones[:], acc[:, c * HLL:(c + 1) * HLL],
                                start=True, stop=True)
            ins.then_inc(ss2_ps, 1)
            up_unit(0, 0, 1)
            pe.wait_ge(ss2_v, 1)
            up_unit(1, 1, 0)
            up_unit(1, 1, 1)
            with pe.Fori(1, KF // 2) as ff:
                for s in range(2):
                    for part in range(2):
                        up_unit(ff * 2 + s, s, part)

            def turn(m, s):
                pe.wait_ge(y_add, m + 1)
                if not (isinstance(m, int) and m < 2):
                    pe.wait_ge(yt_set, m - 1)
                for t in range(4):
                    ins = pe.transpose(ps[:, 4 + s, t * P:(t + 1) * P], yo[s][:, t * P:(t + 1) * P],
                                       ident[:])
                ins.then_inc(yt_ps, 1)

            def down(m, s):
                if isinstance(m, int) and m < 2:
                    pe.wait_ge(up_v, 2 * KF - 2 + 2 * m)
                else:
                    pe.wait_ge(y_add, m - 1)
                for half in range(2):
                    pe.wait_ge(lo_ready, m * 2 + (U_DOWN + 1 + half))
                    for i in range(UT):
                        k = half * UT + i
                        if isinstance(m, int) and m == 0:
                            pe.wait_ge(al_set, k + 1)
                        ins = three([ps[:, s, :]], wtile(half, i),
                                    lambda a, c: (ah, al)[a][:, k, :], k == 0, k == KF - 1)
                    ins.then_inc(unit_done, 1)
                    if half == 0 and not (isinstance(m, int) and m == 0):
                        turn(m - 1, 1 - s)

            down(0, 0)
            down(1, 1)
            with pe.Fori(1, KD // 2) as mm:
                for s in range(2):
                    down(mm * 2 + s, s)
            turn(KD - 1, 1)


_INS = ["x", "meta_tokens", "norm1_g", "w_in", "q_norm_g", "k_norm_g", "ssm_a_re", "ssm_a_im",
        "ssm_log_step", "ssm_b_re", "ssm_b_im", "ssm_c_re", "ssm_c_im", "ssm_d", "w_glu", "b_glu",
        "w_attn_proj", "w_ssm_proj", "w_o", "norm2_g", "w_up", "conv_w", "conv_b", "w_down"]


def kernel(**inputs):
    import numpy as _np
    import concourse.bacc as _bacc
    from concourse import mybir as _mybir
    from concourse.bass_utils import run_bass_kernel_spmd as _run

    nc = _bacc.Bacc("TRN2", target_bir_lowering=False, num_devices=1)
    arrays, args = {}, []
    for name in _INS:
        a = _np.ascontiguousarray(inputs[name])
        arrays[f"in_{name}_dram"] = a
        args.append(nc.dram_tensor(f"in_{name}_dram", a.shape, _mybir.dt.from_np(a.dtype),
                                   kind="ExternalInput").ap())
    args.append(nc.dram_tensor("out_0_dram", (1, SEQ, D), F32, kind="ExternalOutput").ap())
    hybrid_trunk(nc, *args)
    return _run(nc, [arrays], core_ids=[0]).results[0]["out_0_dram"]
```
